# Optimizing a Trainium2 kernel written in Bass

```python
import math
import jax, jax.numpy as jnp
from jax import lax
import numpy as np

D_MODEL = 1024
BATCH = 1
SEQ = 256
DEPTH = 4

N_MIXERS = 3
N_MEM = 256
GRID_W = 64
HEAD_DIM = 64
ROPE_THETA = 10000.0
LN_EPS = 1e-5
RMS_EPS = 1e-6
MASK_VALUE = -1e30

FNET_GROUPS = 4
GQA_Q_HEADS = D_MODEL // HEAD_DIM
GQA_KV_HEADS = GQA_Q_HEADS // 4
Q_BLOCK = 128
DIL_PAIRS = ((128, 1), (512, 4), (2048, 16))
DIL_GROUPS = len(DIL_PAIRS)
DIL_HEADS = D_MODEL // HEAD_DIM
DIL_WIDTH = DIL_GROUPS * DIL_HEADS * HEAD_DIM
MEM_HEADS = 4
MEM_WIDTH = MEM_HEADS * HEAD_DIM
BRANCH_WIDTH = D_MODEL
INNER = BRANCH_WIDTH + MEM_WIDTH
TAIL = INNER + MEM_WIDTH
COLS_A = TAIL
COLS_B = GQA_Q_HEADS * HEAD_DIM + 2 * GQA_KV_HEADS * HEAD_DIM + TAIL
COLS_C = 3 * DIL_WIDTH + TAIL
N_LAYERS_A = (DEPTH + 2) // 3
N_LAYERS_B = (DEPTH + 1) // 3
N_LAYERS_C = DEPTH // 3
DEEPNORM_ALPHA = (2.0 * DEPTH) ** 0.25
DEEPNORM_BETA = (8.0 * DEPTH) ** -0.25


def layer_norm(x, g, b):
    xf = x.astype(jnp.float32)
    mu = jnp.mean(xf, axis=-1, keepdims=True)
    var = jnp.mean(jnp.square(xf - mu), axis=-1, keepdims=True)
    y = (xf - mu) * lax.rsqrt(var + LN_EPS) * g.astype(jnp.float32) + b.astype(jnp.float32)
    return y.astype(x.dtype)

def rms_norm(x, g):
    xf = x.astype(jnp.float32)
    return xf * lax.rsqrt(jnp.mean(jnp.square(xf), axis=-1, keepdims=True) + RMS_EPS) * g.astype(jnp.float32)

def rope_angles(pos, dim):
    inv_freq = ROPE_THETA ** (-(jnp.arange(0, dim, 2, dtype=jnp.float32) / dim))
    return pos.astype(jnp.float32)[:, None] * inv_freq[None, :]

def apply_rope(x, ang):
    x1, x2 = jnp.split(x, 2, axis=-1)
    c = jnp.cos(ang)[:, None, :]
    s = jnp.sin(ang)[:, None, :]
    return jnp.concatenate([x1 * c - x2 * s, x2 * c + x1 * s], axis=-1)

def apply_axial_rope(x, ang_row, ang_col):
    half = x.shape[-1] // 2
    return jnp.concatenate([apply_rope(x[..., :half], ang_row), apply_rope(x[..., half:], ang_col)], axis=-1)

def fourier_mix(h):
    B, S, D = h.shape
    hg = h.astype(jnp.float32).reshape(B, S, FNET_GROUPS, D // FNET_GROUPS)
    y = jnp.fft.fftn(hg, axes=(1, 3), norm="ortho").real
    return y.astype(jnp.float32).reshape(B, S, D)

def gqa_block_attention(q, k, v):
    B, S, Hq, Dh = q.shape
    Hkv = k.shape[2]
    G = Hq // Hkv
    nb = S // Q_BLOCK
    qb = q.reshape(B, nb, Q_BLOCK, Hkv, G, Dh).transpose(1, 0, 3, 4, 2, 5)
    kt = k.transpose(0, 2, 1, 3)
    vt = v.transpose(0, 2, 1, 3)
    scale = Dh ** -0.5

    def one_block(qblk):
        s = jnp.einsum("bhgqd,bhkd->bhgqk", qblk, kt) * scale
        p = jax.nn.softmax(s, axis=-1)
        return jnp.einsum("bhgqk,bhkd->bhgqd", p, vt)

    o = lax.map(one_block, qb)
    return o.transpose(1, 0, 4, 2, 3, 5).reshape(B, S, Hq * Dh)

def dilated_group_attention(q, k, v, dil, side):
    B, S, H, Dh = q.shape
    L = S // dil
    nb = -(-L // side)
    Lp = nb * side

    def to_classes(t):
        t = t.reshape(B, L, dil, H, Dh).transpose(0, 2, 1, 3, 4)
        return jnp.pad(t, ((0, 0), (0, 0), (0, Lp - L), (0, 0), (0, 0)))

    qc, kc, vc = to_classes(q), to_classes(k), to_classes(v)
    qb = qc.reshape(B, dil, nb, side, H, Dh)

    def band(t):
        tp = jnp.pad(t, ((0, 0), (0, 0), (side, side), (0, 0), (0, 0)))
        return jnp.concatenate(
            [tp[:, :, i * side: i * side + Lp].reshape(B, dil, nb, side, H, Dh) for i in range(3)], axis=3)

    kb, vb = band(kc), band(vc)
    qi = jnp.arange(side)
    kj = jnp.arange(3 * side) - side
    in_window = jnp.abs(kj[None, :] - qi[:, None]) <= side
    kabs = jnp.arange(nb)[:, None] * side + kj[None, :]
    valid = (kabs >= 0) & (kabs < L)
    mask = in_window[None, :, :] & valid[:, None, :]

    s = jnp.einsum("bcnqhd,bcnkhd->bcnhqk", qb, kb) * (Dh ** -0.5)
    s = jnp.where(mask[None, None, :, None, :, :], s, MASK_VALUE)
    lse = jax.nn.logsumexp(s, axis=-1)
    p = jnp.exp(s - lse[..., None])
    o = jnp.einsum("bcnhqk,bcnkhd->bcnqhd", p, vb)
    o = o.reshape(B, dil, Lp, H, Dh)[:, :, :L].transpose(0, 2, 1, 3, 4).reshape(B, S, H, Dh)
    lse = lse.transpose(0, 1, 2, 4, 3).reshape(B, dil, Lp, H)[:, :, :L]
    lse = lse.transpose(0, 2, 1, 3).reshape(B, S, H)
    return o, lse

def memory_attention(qm, mk, mv):
    s = jnp.einsum("bshd,bmhd->bhsm", qm, mk) * (qm.shape[-1] ** -0.5)
    p = jax.nn.softmax(s, axis=-1)
    o = jnp.einsum("bhsm,bmhd->bshd", p, mv)
    return o.reshape(qm.shape[0], qm.shape[1], -1)

def first_inputs(seed: int = 0) -> dict:
    key = jax.random.key(seed)
    ks = jax.random.split(key, 16)
    f32 = jnp.float32
    w_in_scale = D_MODEL ** -0.5
    return {
        "x": jax.random.normal(ks[0], (BATCH, SEQ, D_MODEL), f32),
        "mem": jax.random.normal(ks[1], (BATCH, N_MEM, D_MODEL), f32),
        "ln_in_g": 1.0 + 0.02 * jax.random.normal(ks[2], (D_MODEL,), f32),
        "ln_in_b": 0.02 * jax.random.normal(ks[3], (D_MODEL,), f32),
        "w_mem_kv": jax.random.normal(ks[4], (D_MODEL, 2 * MEM_WIDTH), f32) * w_in_scale,
        "w_in_a": jax.random.normal(ks[5], (N_LAYERS_A, D_MODEL, COLS_A), f32) * w_in_scale,
        "w_in_b": jax.random.normal(ks[6], (N_LAYERS_B, D_MODEL, COLS_B), f32) * w_in_scale,
        "q_norm_g": 1.0 + 0.02 * jax.random.normal(ks[7], (N_LAYERS_B, HEAD_DIM), f32),
        "k_norm_g": 1.0 + 0.02 * jax.random.normal(ks[8], (N_LAYERS_B, HEAD_DIM), f32),
        "w_in_c": jax.random.normal(ks[9], (N_LAYERS_C, D_MODEL, COLS_C), f32) * w_in_scale,
        "w_out": jax.random.normal(ks[10], (DEPTH, INNER, D_MODEL), f32) * (INNER ** -0.5) * DEEPNORM_BETA,
        "ln_g": 1.0 + 0.02 * jax.random.normal(ks[11], (DEPTH, D_MODEL), f32),
        "ln_b": 0.02 * jax.random.normal(ks[12], (DEPTH, D_MODEL), f32),
    }

def first_block(x, mem, ln_in_g, ln_in_b, w_mem_kv, w_in_a, w_in_b, q_norm_g, k_norm_g, w_in_c, w_out, ln_g, ln_b):
    B, S, D = x.shape
    ROWS = S // GRID_W
    t = jnp.arange(S)
    row = jnp.repeat(jnp.arange(ROWS), GRID_W, total_repeat_length=S)
    col = jnp.tile(jnp.arange(GRID_W), ROWS)
    ang_1d = rope_angles(t, HEAD_DIM)
    ang_row = rope_angles(row, HEAD_DIM // 2)
    ang_col = rope_angles(col, HEAD_DIM // 2)

    mkv = jnp.matmul(mem, w_mem_kv).astype(jnp.float32).reshape(B, N_MEM, 2, MEM_HEADS, HEAD_DIM)
    mk, mv = mkv[:, :, 0], mkv[:, :, 1]

    h = layer_norm(x, ln_in_g, ln_in_b)
    qw = GQA_Q_HEADS * HEAD_DIM
    kvw = GQA_KV_HEADS * HEAD_DIM
    for i in range(DEPTH):
        kind = i % N_MIXERS
        j = i // N_MIXERS
        if kind == 0:
            proj = jnp.matmul(h, w_in_a[j]).astype(jnp.float32)
            branch = fourier_mix(h)
        elif kind == 1:
            proj = jnp.matmul(h, w_in_b[j]).astype(jnp.float32)
            q = proj[..., :qw].reshape(B, S, GQA_Q_HEADS, HEAD_DIM)
            k = proj[..., qw:qw + kvw].reshape(B, S, GQA_KV_HEADS, HEAD_DIM)
            v = proj[..., qw + kvw:qw + 2 * kvw].reshape(B, S, GQA_KV_HEADS, HEAD_DIM)
            q = apply_axial_rope(rms_norm(q, q_norm_g[j]), ang_row, ang_col)
            k = apply_axial_rope(rms_norm(k, k_norm_g[j]), ang_row, ang_col)
            branch = gqa_block_attention(q, k, v)
        else:
            proj = jnp.matmul(h, w_in_c[j]).astype(jnp.float32)
            qkv = proj[..., :3 * DIL_WIDTH].reshape(B, S, 3, DIL_GROUPS, DIL_HEADS, HEAD_DIM)
            outs = []
            lses = []
            for g, (window, dil) in enumerate(DIL_PAIRS):
                qg = apply_rope(qkv[:, :, 0, g], ang_1d)
                kg = apply_rope(qkv[:, :, 1, g], ang_1d)
                og, lg = dilated_group_attention(qg, kg, qkv[:, :, 2, g], dil, window // (2 * dil))
                outs.append(og)
                lses.append(lg)
            wts = jax.nn.softmax(jnp.stack(lses, axis=0), axis=0)
            branch = jnp.sum(wts[..., None] * jnp.stack(outs, axis=0), axis=0).reshape(B, S, BRANCH_WIDTH)
        tail = proj[..., proj.shape[-1] - TAIL:]
        gate = tail[..., :INNER]
        qm = tail[..., INNER:].reshape(B, S, MEM_HEADS, HEAD_DIM)
        mem_out = memory_attention(qm, mk, mv)
        y = jnp.concatenate([branch, mem_out], axis=-1) * jax.nn.silu(gate)
        y = jnp.matmul(y.astype(h.dtype), w_out[i])
        h = layer_norm(DEEPNORM_ALPHA * h + y.astype(h.dtype), ln_g[i], ln_b[i])
    return h


DEPTH_2 = 2

CHUNK = 128
D_MIX = D_MODEL
GMLP_HEADS = 4
GMLP_HEAD_DIM = 64
GMLP_W = GMLP_HEADS * GMLP_HEAD_DIM
SSD_HEADS = 6
SSD_HEAD_DIM = 64
SSD_W = SSD_HEADS * SSD_HEAD_DIM
SSD_GROUPS = 2
SSD_STATE = 64
SSD_CONV = 4
SSD_XBC = SSD_W + 2 * SSD_GROUPS * SSD_STATE
MLA_HEADS = 6
MLA_NOPE = 64
MLA_ROPE = 32
MLA_V = 64
MLA_W = MLA_HEADS * MLA_V
MLA_Q_RANK = 384
MLA_KV_RANK = 256
ROPE_BASE = 10000.0
D_FF = 4 * D_MODEL
EPS = 1e-6
IN_WIDTHS = (2 * GMLP_W, SSD_W, SSD_XBC, SSD_HEADS, MLA_Q_RANK, MLA_KV_RANK, MLA_ROPE)
D_IN = sum(IN_WIDTHS)


def rmsnorm(x, g):
    xf = x.astype(jnp.float32)
    var = jnp.mean(xf * xf, axis=-1, keepdims=True)
    return (xf * lax.rsqrt(var + EPS)).astype(x.dtype) * g

def split_cols(proj):
    idx, acc = [], 0
    for w in IN_WIDTHS[:-1]:
        acc += w
        idx.append(acc)
    return jnp.split(proj, idx, axis=-1)

def rope_tables(S):
    half = MLA_ROPE // 2
    pos = jnp.arange(S, dtype=jnp.float32)
    inv_freq = jnp.power(ROPE_BASE, -jnp.arange(half, dtype=jnp.float32) / half)
    ang = pos[:, None] * inv_freq[None, :]
    return jnp.cos(ang), jnp.sin(ang)

def apply_rope_2(x, cos, sin):
    c = cos[None, :, None, :].astype(x.dtype)
    s = sin[None, :, None, :].astype(x.dtype)
    x1, x2 = jnp.split(x, 2, axis=-1)
    return jnp.concatenate([x1 * c - x2 * s, x2 * c + x1 * s], axis=-1)

def gmlp_mixer(uv, v_norm_g, w_s, b_s):
    Bsz, S, _ = uv.shape
    nc = S // CHUNK
    uv = jax.nn.gelu(uv)
    u, v = jnp.split(uv, 2, axis=-1)
    v = rmsnorm(v, v_norm_g).reshape(Bsz, nc, CHUNK, GMLP_HEADS, GMLP_HEAD_DIM)
    causal = jnp.tril(jnp.ones((CHUNK, CHUNK), dtype=w_s.dtype))
    mixed = jnp.einsum('hts,bcshd->bcthd', w_s * causal, v)
    mixed = mixed + b_s.T[None, None, :, :, None]
    return u * mixed.reshape(Bsz, S, GMLP_W)

def causal_depthwise_conv(x, w, b):
    K, C = w.shape
    out = lax.conv_general_dilated(
        x, w[:, None, :], window_strides=(1,), padding=((K - 1, 0),),
        dimension_numbers=('NWC', 'WIO', 'NWC'), feature_group_count=C)
    return out + b

def ssd_mixer(z, xbc, dt_raw, conv_w, conv_b, dt_bias, a_log, d_skip, norm_g):
    Bsz, S, _ = xbc.shape
    nc = S // CHUNK
    hpg = SSD_HEADS // SSD_GROUPS
    xbc = jax.nn.silu(causal_depthwise_conv(xbc, conv_w, conv_b))
    xs, Bm, Cm = jnp.split(xbc, [SSD_W, SSD_W + SSD_GROUPS * SSD_STATE], axis=-1)
    xs_c = xs.reshape(Bsz, nc, CHUNK, SSD_HEADS, SSD_HEAD_DIM)
    B_c = Bm.reshape(Bsz, nc, CHUNK, SSD_GROUPS, SSD_STATE)
    C_c = Cm.reshape(Bsz, nc, CHUNK, SSD_GROUPS, SSD_STATE)
    dt = jax.nn.softplus((dt_raw + dt_bias).astype(jnp.float32))
    A = -jnp.exp(a_log.astype(jnp.float32))
    dt_h = dt.reshape(Bsz, nc, CHUNK, SSD_HEADS).transpose(0, 1, 3, 2)
    a_h = jnp.cumsum(dt_h * A[None, None, :, None], axis=-1)
    causal = jnp.tril(jnp.ones((CHUNK, CHUNK), dtype=bool))
    seg = a_h[..., :, None] - a_h[..., None, :]
    decay = jnp.exp(jnp.where(causal, seg, -jnp.inf))
    cb = jnp.einsum('bctgn,bcsgn->bcgts', C_c, B_c)
    cb_h = jnp.repeat(cb, hpg, axis=2)
    w = cb_h * decay * dt_h[:, :, :, None, :]
    y_diag = jnp.einsum('bchts,bcshp->bcthp', w, xs_c)
    B_h = jnp.repeat(B_c, hpg, axis=3)
    C_h = jnp.repeat(C_c, hpg, axis=3)
    decay_to_end = jnp.exp(a_h[..., -1:] - a_h) * dt_h
    states = jnp.einsum('bchs,bcshn,bcshp->bchpn', decay_to_end, B_h, xs_c)
    chunk_decay = jnp.exp(a_h[..., -1])

    def step(h, inp):
        dec, st = inp
        return dec[:, :, None, None] * h + st, h

    h0 = jnp.zeros((Bsz, SSD_HEADS, SSD_HEAD_DIM, SSD_STATE), states.dtype)
    _, h_prev = lax.scan(step, h0, (chunk_decay.transpose(1, 0, 2), states.transpose(1, 0, 2, 3, 4)))
    h_prev = h_prev.transpose(1, 0, 2, 3, 4)
    y_off = jnp.einsum('bcthn,bchpn,bcht->bcthp', C_h, h_prev, jnp.exp(a_h))
    y = y_diag + y_off + xs_c * d_skip[:, None]
    y = y.reshape(Bsz, S, SSD_W).astype(z.dtype)
    yg = (y * jax.nn.silu(z)).reshape(Bsz, S, SSD_GROUPS, SSD_W // SSD_GROUPS)
    return rmsnorm(yg, norm_g.reshape(SSD_GROUPS, -1)).reshape(Bsz, S, SSD_W)

def causal_block_attention(q, k, v, scale):
    Bsz, S, H, Dqk = q.shape
    nq = S // CHUNK
    qb = q.reshape(Bsz, nq, CHUNK, H, Dqk).transpose(1, 0, 3, 2, 4)
    k_pos = jnp.arange(S)

    def one_block(args):
        q_blk, blk = args
        s = jnp.einsum('bhqd,bkhd->bhqk', q_blk, k).astype(jnp.float32) * scale
        q_pos = blk * CHUNK + jnp.arange(CHUNK)
        s = jnp.where(k_pos[None, :] <= q_pos[:, None], s, -jnp.inf)
        p = jax.nn.softmax(s, axis=-1).astype(v.dtype)
        return jnp.einsum('bhqk,bkhd->bqhd', p, v)

    out = lax.map(one_block, (qb, jnp.arange(nq)))
    return out.transpose(1, 0, 2, 3, 4).reshape(Bsz, S, H, v.shape[-1])

def mla_mixer(c_q, c_kv, k_rope_raw, q_norm_g, w_qb, kv_norm_g, w_kvb, cos, sin):
    Bsz, S, _ = c_q.shape
    q = (rmsnorm(c_q, q_norm_g) @ w_qb).reshape(Bsz, S, MLA_HEADS, MLA_NOPE + MLA_ROPE)
    kv = (rmsnorm(c_kv, kv_norm_g) @ w_kvb).reshape(Bsz, S, MLA_HEADS, MLA_NOPE + MLA_V)
    q_nope, q_rope = jnp.split(q, [MLA_NOPE], axis=-1)
    k_nope, v = jnp.split(kv, [MLA_NOPE], axis=-1)
    q_rope = apply_rope_2(q_rope, cos, sin)
    k_rope = apply_rope_2(k_rope_raw[:, :, None, :], cos, sin)
    q = jnp.concatenate([q_nope, q_rope], axis=-1)
    k = jnp.concatenate([k_nope, jnp.broadcast_to(k_rope, (Bsz, S, MLA_HEADS, MLA_ROPE))], axis=-1)
    scale = 1.0 / math.sqrt(MLA_NOPE + MLA_ROPE)
    out = causal_block_attention(q, k, v, scale)
    return out.reshape(Bsz, S, MLA_W)

def squared_relu_mlp(h, w1, w2):
    return jnp.square(jax.nn.relu(h @ w1)) @ w2

def second_inputs(seed: int = 0) -> dict:
    key = jax.random.key(seed)
    ks = jax.random.split(key, 21)

    def nrm(k, shape, scale):
        return jax.random.normal(k, shape, jnp.float32) * scale

    def gain(k, shape):
        return 1.0 + 0.02 * jax.random.normal(k, shape, jnp.float32)

    dt0 = jnp.exp(jax.random.uniform(ks[8], (DEPTH_2, SSD_HEADS), jnp.float32,
                                     math.log(1e-3), math.log(1e-1)))
    dt_bias = dt0 + jnp.log(-jnp.expm1(-dt0))
    a_log = jnp.log(jax.random.uniform(ks[9], (DEPTH_2, SSD_HEADS), jnp.float32, 1.0, 16.0))
    return {
        "x": nrm(ks[0], (BATCH, SEQ, D_MODEL), 1.0),
        "norm_mix_g": gain(ks[1], (DEPTH_2, D_MODEL)),
        "w_in": nrm(ks[2], (DEPTH_2, D_MODEL, D_IN), D_MODEL ** -0.5),
        "gmlp_v_norm_g": gain(ks[3], (DEPTH_2, GMLP_W)),
        "gmlp_w_s": nrm(ks[4], (DEPTH_2, GMLP_HEADS, CHUNK, CHUNK), CHUNK ** -0.5),
        "gmlp_b_s": gain(ks[5], (DEPTH_2, GMLP_HEADS, CHUNK)),
        "ssd_conv_w": nrm(ks[6], (DEPTH_2, SSD_CONV, SSD_XBC), SSD_CONV ** -0.5),
        "ssd_conv_b": nrm(ks[7], (DEPTH_2, SSD_XBC), 0.02),
        "ssd_dt_bias": dt_bias,
        "ssd_a_log": a_log,
        "ssd_d": 1.0 + 0.1 * jax.random.normal(ks[10], (DEPTH_2, SSD_HEADS), jnp.float32),
        "ssd_norm_g": gain(ks[11], (DEPTH_2, SSD_W)),
        "mla_q_norm_g": gain(ks[12], (DEPTH_2, MLA_Q_RANK)),
        "mla_w_qb": nrm(ks[13], (DEPTH_2, MLA_Q_RANK, MLA_HEADS * (MLA_NOPE + MLA_ROPE)), MLA_Q_RANK ** -0.5),
        "mla_kv_norm_g": gain(ks[14], (DEPTH_2, MLA_KV_RANK)),
        "mla_w_kvb": nrm(ks[15], (DEPTH_2, MLA_KV_RANK, MLA_HEADS * (MLA_NOPE + MLA_V)), MLA_KV_RANK ** -0.5),
        "w_out": nrm(ks[16], (DEPTH_2, D_MIX, D_MODEL), D_MIX ** -0.5),
        "norm_mlp_g": gain(ks[17], (DEPTH_2, D_MODEL)),
        "mlp_w1": nrm(ks[18], (DEPTH_2, D_MODEL, D_FF), D_MODEL ** -0.5),
        "mlp_w2": nrm(ks[19], (DEPTH_2, D_FF, D_MODEL), D_FF ** -0.5),
        "final_norm_g": gain(ks[20], (D_MODEL,)),
    }

def second_block(x, norm_mix_g, w_in, gmlp_v_norm_g, gmlp_w_s, gmlp_b_s, ssd_conv_w, ssd_conv_b,
              ssd_dt_bias, ssd_a_log, ssd_d, ssd_norm_g, mla_q_norm_g, mla_w_qb, mla_kv_norm_g,
              mla_w_kvb, w_out, norm_mlp_g, mlp_w1, mlp_w2, final_norm_g):
    S = x.shape[1]
    cos, sin = rope_tables(S)
    for l in range(DEPTH_2):
        h = rmsnorm(x, norm_mix_g[l])
        uv, z, xbc, dt_raw, c_q, c_kv, k_rope = split_cols(h @ w_in[l])
        y_a = gmlp_mixer(uv, gmlp_v_norm_g[l], gmlp_w_s[l], gmlp_b_s[l])
        y_b = ssd_mixer(z, xbc, dt_raw, ssd_conv_w[l], ssd_conv_b[l], ssd_dt_bias[l],
                        ssd_a_log[l], ssd_d[l], ssd_norm_g[l])
        y_c = mla_mixer(c_q, c_kv, k_rope, mla_q_norm_g[l], mla_w_qb[l], mla_kv_norm_g[l],
                        mla_w_kvb[l], cos, sin)
        mix = jnp.concatenate([y_a, y_b, y_c], axis=-1)
        x = x + mix @ w_out[l]
        x = x + squared_relu_mlp(rmsnorm(x, norm_mlp_g[l]), mlp_w1[l], mlp_w2[l])
    return rmsnorm(x, final_norm_g)


def setup_inputs(seed=0):
    out = dict(first_inputs(seed))
    for name, value in second_inputs(seed + 1).items():
        if name != "x":
            out[name + "_2"] = value
    return out


def reference(
    x, mem, ln_in_g, ln_in_b, w_mem_kv, w_in_a, w_in_b, q_norm_g, k_norm_g, w_in_c, w_out, ln_g,
    ln_b, norm_mix_g_2, w_in_2, gmlp_v_norm_g_2, gmlp_w_s_2, gmlp_b_s_2, ssd_conv_w_2,
    ssd_conv_b_2, ssd_dt_bias_2, ssd_a_log_2, ssd_d_2, ssd_norm_g_2, mla_q_norm_g_2, mla_w_qb_2,
    mla_kv_norm_g_2, mla_w_kvb_2, w_out_2, norm_mlp_g_2, mlp_w1_2, mlp_w2_2, final_norm_g_2,
):
    x = first_block(
        x, mem, ln_in_g, ln_in_b, w_mem_kv, w_in_a, w_in_b, q_norm_g, k_norm_g, w_in_c, w_out,
        ln_g, ln_b,
    )
    return second_block(
        x, norm_mix_g_2, w_in_2, gmlp_v_norm_g_2, gmlp_w_s_2, gmlp_b_s_2, ssd_conv_w_2,
        ssd_conv_b_2, ssd_dt_bias_2, ssd_a_log_2, ssd_d_2, ssd_norm_g_2, mla_q_norm_g_2,
        mla_w_qb_2, mla_kv_norm_g_2, mla_w_kvb_2, w_out_2, norm_mlp_g_2, mlp_w1_2, mlp_w2_2,
        final_norm_g_2,
    )


_drawn_inputs = setup_inputs


def setup_inputs(seed=0):
    import zlib

    import numpy as np

    out = dict(_drawn_inputs(seed))
    spreads = {}
    factors = {'mem': 2.999,
     'w_mem_kv': 2.778,
     'q_norm_g': 8.0,
     'k_norm_g': 8.0,
     'gmlp_v_norm_g_2': 21.351,
     'gmlp_b_s_2': 8.0,
     'ssd_conv_b_2': 2.865,
     'ssd_norm_g_2': 4.023,
     'mla_q_norm_g_2': 8.0,
     'mla_kv_norm_g_2': 8.0,
     'final_norm_g_2': 22.465,
     'norm_mlp_g_2': 2.864}
    for name, (base, spread) in spreads.items():
        noise = np.random.default_rng([zlib.crc32(name.encode()), seed]).standard_normal(out[name].shape)
        drawn = base * np.exp(spread * noise) if base else spread * noise
        out[name] = __import__('jax').numpy.asarray(drawn.astype(out[name].dtype))
    for name, factor in factors.items():
        out[name] = (out[name] * factor).astype(out[name].dtype)
    return out
```

```python
from contextlib import ExitStack

import numpy as np

import concourse.bass as bass
from concourse import mybir

F32 = mybir.dt.float32
F32R = mybir.dt.float32r
I32 = mybir.dt.int32
ACT = mybir.ActivationFunctionType
ALU = mybir.AluOpType
AX = mybir.AxisListType

P = 128
S = 256
NB = S // P
D = 1024
KT = D // P
DH = 64
N_MEM = 256
MASKED = -1e30
BIG = 3.0e38

MEM_HEADS = 4
MEM_W = MEM_HEADS * DH
INNER = D + MEM_W
YT = INNER // P
TAIL = INNER + MEM_W
HEADS = D // DH
KV_HEADS = HEADS // 4
ALPHA = 8.0 ** 0.25
GW = D // 4
DIL_W = 3 * D

UV = 512
SSD_H = 6
SSD_W = SSD_H * DH
XBC = SSD_W + 256
Q_RANK = 384
KV_RANK = 256
M_ROPE = 32
M_QK = 96
M_H = 6
D_FF = 4096
C_UV, C_Z, C_XBC = 0, UV, UV + SSD_W
C_DT = C_XBC + XBC
C_CKV = C_DT + SSD_H + Q_RANK
DTQ = SSD_H + Q_RANK
KVR = KV_RANK + M_ROPE

RAW_SLOTS = 3
SPLIT_SLOTS = 3
UNIT = 2048


def token_order():
    p = np.arange(S)
    return 16 * (p % 16) + 4 * (p // 16 % 4) + p // 64


CONST_AT = {}


def constants():
    t = token_order()
    parts = []

    def put(name, a):
        a = np.asarray(a, np.float64)
        if a.ndim == 2 and a.shape[0] == S:
            a = a.reshape(NB, P, -1).transpose(1, 0, 2).reshape(P, -1)
        CONST_AT[name] = (sum(x.shape[1] for x in parts), a.shape[1])
        parts.append(a)

    put("ident", np.eye(P))
    put("ones", np.ones((P, P)))
    i = np.arange(P)
    upto = (i[:, None] <= i[None, :]).astype(np.float64)
    put("upto", upto)
    put("future_st", (1 - upto) * MASKED)
    causal = (1 - upto.T) * MASKED
    put("causal", np.concatenate([causal, np.zeros((P, P)), causal], 1))
    a = 2 * np.pi * np.outer(t, t) / S
    put("dft_tok", np.concatenate([np.cos(a), -np.sin(a)], 1) / 16)

    def rope(pos, dim, base=10000.0):
        f = base ** (-(np.arange(0, dim, 2) / dim))
        a = (np.asarray(pos, np.float32)[:, None] * f.astype(np.float32)[None, :]).astype(np.float64)
        c, s = np.cos(a), np.sin(a)
        return np.concatenate([c, c], 1), np.concatenate([-s, s], 1)

    rc, rs = rope(t // 64, DH // 2)
    cc, cs = rope(t % 64, DH // 2)
    put("axial_cos", np.concatenate([rc, cc], 1))
    put("axial_sin", np.concatenate([rs, cs], 1))
    c, s = rope(t, DH)
    put("line_cos", c)
    put("line_sin", s)
    c, s = rope(np.arange(S), M_ROPE)
    put("mla_cos", c)
    put("mla_sin", s)
    mask = np.zeros((S, 512))
    for b in range(NB):
        q = t[b * P:(b + 1) * P, None]
        own = t[None, b * P:(b + 1) * P]
        mask[b * P:(b + 1) * P, 0:S] = np.abs(t[None, :] - q) > 64
        mask[b * P:(b + 1) * P, S:S + P] = (own - q) % 4 != 0
        mask[b * P:(b + 1) * P, S + P:] = (own - q) % 16 != 0
    put("dilated_mask", mask * MASKED)
    n_kept = sum(x.shape[1] for x in parts)
    j = np.arange(GW)
    a = 2 * np.pi * np.outer(j, j) / GW
    put("dft_ch", np.concatenate([np.cos(a), np.sin(a)], 1) / 16)
    put("residual", np.eye(P) * ALPHA)
    return np.ascontiguousarray(np.concatenate(parts, 1).astype(np.float32)), n_kept


def build(nc, A, out):
    _, n_kept = constants()
    with ExitStack() as ctx:
        def sb(name, shape, dt=F32):
            return ctx.enter_context(nc.sbuf_tensor(name, shape, dt))

        w_raw = sb("w_raw", [P, RAW_SLOTS, UNIT])
        w_hi = sb("w_hi", [P, SPLIT_SLOTS, UNIT], F32R)
        w_lo = sb("w_lo", [P, SPLIT_SLOTS, UNIT], F32R)
        h_hi = sb("h_hi", [P, KT, S], F32R)
        h_lo = sb("h_lo", [P, KT, S], F32R)
        r_hi = sb("r_hi", [P, YT, S], F32R)
        r_lo = sb("r_lo", [P, YT, S], F32R)
        const = sb("const", [P, n_kept])
        dft_hi = sb("dft_hi", [P, 2, 512], F32R)
        dft_lo = sb("dft_lo", [P, 2, 512], F32R)
        res_hi = sb("res_hi", [P, P], F32R)
        res_lo = sb("res_lo", [P, P], F32R)
        ident_r = sb("ident_r", [P, P], F32R)
        gate = sb("gate", [P, YT, S])
        mkT = sb("mkT", [P, 2, N_MEM])
        mv = sb("mv", [P, NB, MEM_W])
        N_COL_A, N_COL_B = 80, 106
        col_a = sb("col_a", [P, N_COL_A])
        col_b = sb("col_b", [P, N_COL_B])
        row = sb("row", [P, 2 * DH + 2 * 256 + 36])
        masked = sb("masked", [P, 2, 512])
        prob = sb("prob", [P, 3, 512])
        probT = sb("probT", [P, 2, 512])
        split_t = sb("split_t", [P, 2, 512])
        stat = sb("stat", [P, 512])
        ARENA = 9728
        arena = sb("arena", [P, ARENA])

        bank = [ctx.enter_context(nc.psum_tensor(f"bank{i}", [P, 512], F32)) for i in range(8)]

        def K(name):
            at, n = CONST_AT[name]
            return const[:, at:at + n]

        ident = K("ident")

        class Steps:

            def __init__(self, name):
                self.sem = ctx.enter_context(nc.semaphore(name))
                self.order, self.made, self.unit = {}, 0, {}
                every.append(self)

            def at(self, key):
                return self.order.setdefault(key, len(self.order) + 1)

            def after(self, key):
                return self.sem, self.at(key)

            def next(self, key):
                self.made += 1
                assert self.at(key) == self.made, (key, self.at(key), self.made)
                self.unit[key] = len(units) - 1
                return 1

        every = []
        product_done = Steps("product_done")
        act_read = Steps("act_read")
        dve_read = Steps("dve_read")
        out_read = Steps("out_read")
        w_rounded = Steps("w_rounded")
        w_split = Steps("w_split")
        tables_rounded = Steps("tables_rounded")
        tables_split = Steps("tables_split")
        a_exp = Steps("a_exp")
        row_stats = Steps("row_stats")
        rows_normal = Steps("rows_normal")
        rows_normal_v = Steps("rows_normal_v")
        h_rounded = Steps("h_rounded")
        h_ready = Steps("h_ready")
        r_ready = Steps("r_ready")
        row_max = Steps("row_max")
        exp_half = Steps("exp_half")
        exp_done = Steps("exp_done")
        probs_normal = Steps("probs_normal")
        roped = Steps("roped")
        square_sum = Steps("square_sum")
        square_hi = Steps("square_hi")
        latent_normal = Steps("latent_normal")
        xbc_ready = Steps("xbc_ready")
        conv_done = Steps("conv_done")
        gmlp_ready = Steps("gmlp_ready")
        steps_in = Steps("steps_in")
        exp_small = Steps("exp_small")
        steps_ready = Steps("steps_ready")
        exp_seg = Steps("exp_seg")
        decay_ready = Steps("decay_ready")
        state_in = Steps("state_in")
        mixer_out = Steps("mixer_out")
        row_out = Steps("row_out")
        vector_step = Steps("vector_step")
        w_loaded = [ctx.enter_context(nc.semaphore(f"w_loaded{i}")) for i in range(RAW_SLOTS)]
        consts_loaded = ctx.enter_context(nc.semaphore("consts_loaded"))
        x_loaded = ctx.enter_context(nc.semaphore("x_loaded"))
        mem_loaded = ctx.enter_context(nc.semaphore("mem_loaded"))
        rows_loaded = ctx.enter_context(nc.semaphore("rows_loaded"))
        ws_loaded = ctx.enter_context(nc.semaphore("ws_loaded"))
        gf_loaded = ctx.enter_context(nc.semaphore("gf_loaded"))
        stored = ctx.enter_context(nc.semaphore("stored"))

        units = []
        unit_done = {}
        down_done = {}
        left = {}

        def view(at, *shape):
            n = int(np.prod(shape))
            assert at + n <= ARENA, (at, shape)
            v = arena[:, at:at + n]
            if len(shape) == 1:
                return v
            names = "abcd"[:len(shape)]
            return v.rearrange(f"p ({' '.join(names)}) -> p {' '.join(names)}", **{k: s for k, s in zip(names, shape)})

        z = view(2048, NB, D)
        x_in = view(0, NB, D)
        mem_in = view(4096, NB, D)
        const_once = view(6144, 1024 + P)
        rows_a = arena[0:N_COL_A, 7300:7300 + P]
        rows_b = arena[0:N_COL_B, 7500:7500 + P]
        qmT = view(8000, 2, S)
        spectra = view(0, NB, 4, 512)
        qkv = view(0, NB, 1536)
        b_sq = view(3072, 1280)
        k_dup = view(4352, NB, KV_HEADS, 2, DH)
        b_rot = b_sq[:, 0:1024]
        gcos = view(5376, 2, NB, DH)
        gsin = view(5632, 2, NB, DH)
        bkT = view(5888, KV_HEADS, S)
        b_qmT = view(6912, 2, S)
        bqT = view(7424, 8, S)
        cqT = view(0, 3, 4, S)
        ckT = view(3072, 3, 4, S)
        cv = view(6144, NB, 3, 512)
        c_rot = prob[:, 0:2, :]
        c_tmp = split_t[:, 1, 0:256]
        c_qmT = view(9216, 2, S)
        x = view(0, NB, D)
        qtok = view(2048, NB, 576)
        zg = view(3200, NB, SSD_W)
        xbcT = view(4096, 5, S + 3)
        mqT = view(4096, M_H, S)
        xs = view(5632, NB, SSD_W)
        kvtok = view(6400, NB, 768)
        ktok = view(7936, NB, 576)
        cqt = view(7936, NB, DTQ)
        ckt = view(7936 + NB * DTQ, NB, KVR)
        y_b = probT[:, :, :].rearrange("p a b -> p (a b)")[:, 0:NB * SSD_W].rearrange("p (b n) -> p b n", b=NB)
        uv = gate[:, 0:4, :].rearrange("p a b -> p (a b)").rearrange("p (b n) -> p b n", b=NB)
        mkvT = gate[:, 4:10, :]
        conv = prob[:, :, :].rearrange("p a b -> p (a b)")[:, 0:1280].rearrange("p (t s) -> p t s", t=5)
        decay = prob[:, :, :].rearrange("p a b -> p (a b)").rearrange("p (i t) -> p i t", t=P)
        ws_raw = probT[:, 0, :].rearrange("p (h s) -> p h s", h=4)
        wsT = probT[:, 1, :].rearrange("p (h t) -> p h t", h=4)
        b_tok = masked[:, 0, 0:P]
        x_dec = masked[:, 1, 0:SSD_W]
        st_sb = masked[:, 0, P:P + 192]
        gf = gate[:, 0:4, :].rearrange("p a b -> p (a b)")

        def S_(at, n):
            return stat[:, at:at + n]

        q_gain, k_gain = row[:, 0:DH], row[:, DH:2 * DH]
        gv = row[:, 2 * DH:2 * DH + 512].rearrange("p (l n) -> p l n", l=2)
        dt_bias = row[:, 640:652].rearrange("p (l h) -> p l h", l=2)
        a_neg = row[:, 652:664].rearrange("p (l h) -> p l h", l=2)
        d_skip = row[:, 664:676].rearrange("p (l h) -> p l h", l=2)

        def ln_cols(i):
            if i == 0:
                return col_a[:, 0:8], col_a[:, 8:16]
            return col_a[:, 16 + 8 * (i - 1):24 + 8 * (i - 1)], col_a[:, 48 + 8 * (i - 1):56 + 8 * (i - 1)]

        col_at, n_b = {}, 0
        for nm, n in (("mix", 8), ("mlp", 8), ("conv_w", 20), ("conv_b", 5), ("cq", 3), ("ckv", 2), ("ssd", 3), ("bs", 4)):
            col_at[nm] = (n_b, n)
            n_b += 2 * n
        assert n_b == N_COL_B

        def col(nm, l):
            at, n = col_at[nm]
            return col_b[:, at + l * n:at + (l + 1) * n]

        ROW_DMAS = 4 + 8 + 6
        block = ctx.enter_context(nc.Block())

        def rows_of(w, k0, kts, c0, n):
            return w[k0:k0 + kts * P, c0:c0 + n].rearrange("(k p) n -> p k n", p=P), kts, n

        LAYERS = [("a", 0), ("b", 0), ("c", 0), ("a", 1)]
        LAYER_NAMES = [f"{k}{j}" for k, j in LAYERS] + ["d"]
        BY_SCALAR = [(0, 0), (0, 1), (1, 1)]

        def attention_order(n, steps="stv"):
            lag = {"s": 0, "t": 2, "v": 3}
            for i in range(n + 3):
                for what in steps:
                    if 0 <= i - lag[what] < n:
                        yield what, i - lag[what]

        @block.tensor
        def _(pe):
            def unit(source):
                u = len(units)
                units.append(source)
                pe.wait_ge(w_split.sem, w_split.at(u))
                slot, (_, kts, n) = u % SPLIT_SLOTS, source
                return u, [w[:, slot, 0:kts * n].rearrange("p (k n) -> p k n", k=kts) for w in (w_hi, w_lo)]

            def mm3(o, lhs, rhs, start, stop):
                nc.tensor.matmul(o, lhs[0], rhs[0], start=start, stop=False)
                nc.tensor.matmul(o, lhs[0], rhs[1], start=False, stop=False)
                return nc.tensor.matmul(o, lhs[1], rhs[0], start=False, stop=stop)

            def hT(k, b=None):
                cols = slice(0, S) if b is None else slice(b * P, (b + 1) * P)
                return h_hi[:, k, cols], h_lo[:, k, cols]

            def rT(k, b=None):
                cols = slice(0, S) if b is None else slice(b * P, (b + 1) * P)
                return r_hi[:, k, cols], r_lo[:, k, cols]

            def feature_major(key, b, source, act, reader=act_read, hidden=None):
                if b in left:
                    pe.wait_ge(*left[b])
                left[b] = reader.after(key)
                o = bank[b]
                u, w = unit(source)
                _, kts, n = source
                for m in range(n // P):
                    for k in range(kts):
                        if hidden is not None and m == 0 and k % 2 == 0:
                            pe.wait_ge(h_ready.sem, h_ready.at((hidden, k // 2)))
                        i = mm3(o[:, m * S:(m + 1) * S], [a[:, k, m * P:(m + 1) * P] for a in w], act(k),
                                k == 0, k == kts - 1)
                i.then_inc(product_done.sem, product_done.next(key))
                unit_done[u] = key

            def token_major(keys, banks, sources, act, reader=act_read, hidden=None, opened=True, closed=True):
                for b in range(NB):
                    if opened and banks[b] in left:
                        pe.wait_ge(*left[banks[b]])
                    left[banks[b]] = reader.after(keys[b])
                o = [bank[banks[b]] for b in range(NB)]
                k0 = 0
                for s, source in enumerate(sources):
                    u, w = unit(source)
                    _, kts, n = source
                    for b in range(NB):
                        last_unit = s == len(sources) - 1
                        for k in range(kts):
                            if hidden is not None and b == 0 and k % 2 == 0:
                                pe.wait_ge(h_ready.sem, h_ready.at((hidden, (k0 + k) // 2)))
                            i = mm3(o[b][:, 0:n], act(k0 + k, b), [a[:, k, :] for a in w],
                                    opened and s == 0 and k == 0, closed and last_unit and k == kts - 1)
                        if last_unit and closed:
                            i.then_inc(product_done.sem, product_done.next(keys[b]))
                        elif b == NB - 1:
                            i.then_inc(product_done.sem, product_done.next(("unit", u)))
                    unit_done[u] = keys[NB - 1] if last_unit and closed else ("unit", u)
                    k0 += kts

            def transposes(key, b, ins, reader, width=P):
                if b in left:
                    pe.wait_ge(*left[b])
                left[b] = reader.after(key)
                o = bank[b]
                for n, a in enumerate(ins):
                    i = nc.tensor.transpose(o[0:a.shape[1], n * width:n * width + P], a, ident)
                i.then_inc(product_done.sem, product_done.next(key))

            def hidden_from_rows(L, b0):
                for b in range(NB):
                    for j in range(4):
                        if b == 0:
                            pe.wait_ge(rows_normal.sem, rows_normal.at((L, 0, j // 2)))
                            if b0 + j in left:
                                pe.wait_ge(*left[b0 + j])
                            left[b0 + j] = dve_read.after((L, "zt", j))
                        elif j < 2:
                            pe.wait_ge(rows_normal_v.sem, rows_normal_v.at(L))
                        else:
                            pe.wait_ge(rows_normal.sem, rows_normal.at((L, 1, 1)))
                        for m in range(2):
                            k = 2 * j + m
                            i = nc.tensor.transpose(bank[b0 + j][:, m * S + b * P:m * S + (b + 1) * P], z[:, b, k * P:(k + 1) * P], ident)
                        if b == NB - 1:
                            i.then_inc(product_done.sem, product_done.next((L, "zt", j)))

            def attend(L, heads, sb0, tb0, ob, q_of, k_of, v_of, o_of):
                for what, i in attention_order(len(heads)):
                    h = heads[i]
                    if what == "s":
                        n_b = sb0 + i % 2
                        if n_b in left:
                            pe.wait_ge(*left[n_b])
                        left[n_b] = act_read.after((L, "s", h))
                        o = bank[n_b]
                        for b in range(NB):
                            m = nc.tensor.matmul(o[:, b * S:(b + 1) * S], q_of(h)[:, b * P:(b + 1) * P], k_of(h),
                                                 start=True, stop=True)
                        m.then_inc(product_done.sem, product_done.next((L, "s", h)))
                    elif what == "t":
                        pe.wait_ge(probs_normal.sem, probs_normal.at((L, h)))
                        pr = prob[:, i % 3, :]
                        transposes((L, "t", h), tb0 + i % 2,
                                   [pr[:, b * S + k * P:b * S + (k + 1) * P] for k in range(2) for b in range(NB)],
                                   act_read)
                    else:
                        pe.wait_ge(act_read.sem, act_read.at((L, "t", h)))
                        key, b, o, first, last = o_of(i, h)
                        if first:
                            if b in left:
                                pe.wait_ge(*left[b])
                            left[b] = out_read.after(key)
                        for k in range(2):
                            m = nc.tensor.matmul(o, v_of(h, k), probT[:, i % 2, k * S:(k + 1) * S],
                                                 start=k == 0, stop=k == 1)
                        m.then_inc(product_done.sem, product_done.next(key if last else (L, "o", h)))

            def memory_heads(L, qT_):
                def o_of(i, h):
                    b = 7
                    return (L, "mo"), b, bank[b][64 * (h % 2):64 * (h % 2) + 64, (h // 2) * S:(h // 2 + 1) * S], i == 0, i == 3
                pe.wait_ge(act_read.sem, act_read.at((L, "qm")))
                attend((L, "m"), range(MEM_HEADS), 0, 2, 7,
                       lambda h: qT_[64 * (h % 2):64 * (h % 2) + 64, h // 2, :],
                       lambda h: mkT[64 * (h % 2):64 * (h % 2) + 64, h // 2, :],
                       lambda h, k: mv[:, k, h * DH:(h + 1) * DH], o_of)

            def gates(L, w, tail, hidden=None):
                feature_major((L, "qm"), 0, rows_of(w, 0, KT, tail + INNER, MEM_W), hT, hidden=hidden)
                for u in range(5):
                    feature_major((L, "gate", u), 1 + u, rows_of(w, 0, KT, tail + u * 256, 256), hT)

            def out_product(L, i):
                for n in range(2):
                    for b in range(NB):
                        if 2 * n + b in left:
                            pe.wait_ge(*left[2 * n + b])
                        if n == 0 and b == 1:
                            left[2 * n + b] = rows_normal_v.after(L)
                        else:
                            left[2 * n + b] = rows_normal.after((L, b, n))
                        for j in range(4):
                            mm3(bank[2 * n + b][:, j * P:(j + 1) * P], hT(4 * n + j, b), (res_hi[:], res_lo[:]), j == 0, False)
                    for k0, kts in ((8, 2), (0, 4), (4, 4)):
                        u, w = unit(rows_of(A["w_out"][i], k0 * P, kts, n * 512, 512))
                        for b in range(NB):
                            for k in range(kts):
                                if n == 0 and b == 0 and k % 2 == 0:
                                    pe.wait_ge(r_ready.sem, r_ready.at((L, (k0 + k) // 2)))
                                m = mm3(bank[2 * n + b][:, :], rT(k0 + k, b), [a[:, k, :] for a in w], False, k0 + k == 7)
                            if k0 == 4:
                                m.then_inc(product_done.sem, product_done.next((L, "wo", n, b)))
                            elif b == NB - 1:
                                m.then_inc(product_done.sem, product_done.next(("unit", u)))
                        unit_done[u] = (L, "wo", n, NB - 1) if k0 == 4 else ("unit", u)

            pe.wait_ge(consts_loaded, 32)
            pe.wait_ge(rows_loaded, 16 * ROW_DMAS)
            if 0 in left:
                pe.wait_ge(*left[0])
            left[0] = act_read.after("cols")
            o = bank[0]
            nc.tensor.transpose(o[:, 0:N_COL_A], rows_a, ident[0:N_COL_A, 0:N_COL_A])
            nc.tensor.transpose(o[:, 128:128 + N_COL_B], rows_b, ident[0:N_COL_B, 0:N_COL_B]).then_inc(product_done.sem, product_done.next("cols"))
            pe.wait_ge(mem_loaded, 16)
            for j in range(4):
                transposes(("mem", "t", j), 4 + j,
                           [mem_in[:, b, k * P:(k + 1) * P] for k in (2 * j, 2 * j + 1) for b in range(NB)], dve_read)
            hidden_from_rows("in", 0)
            for j in range(4):
                pe.wait_ge(r_ready.sem, r_ready.at(("mem", j)))
            feature_major(("mem", "k"), 4, rows_of(A["w_mem_kv"], 0, KT, 0, MEM_W), rT)
            u, w = unit(rows_of(A["w_mem_kv"], 0, KT, MEM_W, MEM_W))
            if 5 in left:
                pe.wait_ge(*left[5])
            left[5] = act_read.after(("mem", "v"))
            o = bank[5]
            for b in range(NB):
                for k in range(KT):
                    i = mm3(o[:, b * MEM_W:(b + 1) * MEM_W], rT(k, b), [a[:, k, :] for a in w], k == 0, k == KT - 1)
            i.then_inc(product_done.sem, product_done.next(("mem", "v")))
            unit_done[u] = ("mem", "v")

            for li, (kind, j) in enumerate(LAYERS):
                L = f"{kind}{j}"
                if kind == "a":
                    w = A["w_in_a"][j]
                    gates(L, w, 0, hidden=L)
                    memory_heads(L, qmT)
                    if j == 0:
                        pe.wait_ge(tables_split.sem, tables_split.at("lo"))
                    for g in range(4):
                        for b in range(NB):
                            n_b = 2 * (g % 3) + b
                            if n_b in left:
                                pe.wait_ge(*left[n_b])
                            left[n_b] = (act_read if b == 0 else dve_read).after((L, "f1", g, b))
                            o = bank[n_b]
                            for k in range(2):
                                i = mm3(o[:, :], hT(2 * g + k, b), (dft_hi[:, k, :], dft_lo[:, k, :]), k == 0, k == 1)
                            i.then_inc(product_done.sem, product_done.next((L, "f1", g, b)))
                    dt = K("dft_tok").rearrange("p (b c) -> p b c", b=NB)
                    for t in range(4):
                        pe.wait_ge(act_read.sem, act_read.at((L, "f1", t, 0)))
                        pe.wait_ge(dve_read.sem, dve_read.at((L, "f1", t, 1)))
                        n_b = 2 * (t % 2)
                        if n_b in left:
                            pe.wait_ge(*left[n_b])
                        left[n_b] = out_read.after((L, "f2", t))
                        o = bank[n_b]
                        for c in range(2):
                            for part in range(2):
                                for b in range(NB):
                                    i = nc.tensor.matmul(
                                        o[:, c * S:(c + 1) * S], spectra[:, b, t, part * GW + c * P:part * GW + (c + 1) * P],
                                        dt[:, b, part * S:(part + 1) * S], start=part + b == 0, stop=part + b == 2)
                        i.then_inc(product_done.sem, product_done.next((L, "f2", t)))
                elif kind == "b":
                    w = A["w_in_b"][0]
                    for c in range(3):
                        token_major([(L, "p", c, b) for b in range(NB)], [2 * c, 2 * c + 1],
                                    [rows_of(w, kh * 512, 4, c * 512, 512) for kh in range(2)], hT, hidden=L if c == 0 else None)
                    gates(L, w, 1536)
                    for t in range(4):
                        for b in range(NB):
                            pe.wait_ge(roped.sem, roped.at((L, "q", b)))
                        transposes((L, "qt", t), 6 + t % 2,
                                   [qkv[:, b, m * P:(m + 1) * P] for m in (2 * t, 2 * t + 1) for b in range(NB)], act_read)
                    for t in range(2):
                        for b in range(NB):
                            pe.wait_ge(roped.sem, roped.at((L, "k", b)))
                        transposes((L, "kt", t), 6 + t % 2,
                                   [k_dup[:, b, m, :, :].rearrange("p a d -> p (a d)") for m in (2 * t, 2 * t + 1) for b in range(NB)],
                                   act_read)
                    memory_heads(L, b_qmT)
                    for t in range(4):
                        pe.wait_ge(act_read.sem, act_read.at((L, "qt", t)))
                    for t in range(2):
                        pe.wait_ge(act_read.sem, act_read.at((L, "kt", t)))

                    def o_of(i, h):
                        b = 4 + (i // 4) % 3
                        return (L, "ao", i // 4), b, bank[b][64 * (h % 2):64 * (h % 2) + 64, (i % 4 // 2) * S:(i % 4 // 2 + 1) * S], i % 4 == 0, i % 4 == 3
                    attend((L, "h"), range(HEADS), 0, 2, 4,
                           lambda h: bqT[64 * (h % 2):64 * (h % 2) + 64, h // 2, :],
                           lambda h: bkT[64 * (h % 2):64 * (h % 2) + 64, h // 4, :],
                           lambda h, k: qkv[:, k, 1280 + (h // 4) * DH:1280 + (h // 4 + 1) * DH], o_of)
                else:
                    w = A["w_in_c"][0]
                    gates(L, w, 3 * DIL_W, hidden=L)
                    memory_heads(L, c_qmT)
                    for half in range(2):
                        chunks = [(s, g) for g in range(3) for s in range(2)] + [(2, g) for g in range(3)]

                        def turn(n):
                            s, g = chunks[n]
                            for t in range(2):
                                for b in range(NB):
                                    pe.wait_ge(roped.sem, roped.at((L, half, s, g, b)))
                                transposes((L, half, "xt", s, g, t), 4 + t,
                                           [c_rot[:, b, m * P:(m + 1) * P] for m in (2 * t, 2 * t + 1) for b in range(NB)],
                                           act_read)
                        for n, (s, g) in enumerate(chunks):
                            token_major([(L, half, "p", s, g, b) for b in range(NB)], [2 * (n % 2), 2 * (n % 2) + 1],
                                        [rows_of(w, kh * 512, 4, s * DIL_W + g * D + half * 512, 512) for kh in range(2)],
                                        hT, reader=dve_read if s < 2 else act_read)
                            if 1 <= n <= 6:
                                turn(n - 1)
                        for g in range(3):
                            for b in range(NB):
                                pe.wait_ge(act_read.sem, act_read.at((L, half, "p", 2, g, b)))
                            for s in range(2):
                                for t in range(2):
                                    pe.wait_ge(act_read.sem, act_read.at((L, half, "xt", s, g, t)))
                        for what, i in attention_order(16):
                            h, b = i // 2, i % 2
                            at, pr = 64 * (h % 2), h // 2
                            qs = slice(b * P, (b + 1) * P)
                            if what == "s":
                                n_b = i % 2
                                if n_b in left:
                                    pe.wait_ge(*left[n_b])
                                left[n_b] = dve_read.after((L, half, "s", i))
                                o = bank[n_b]
                                for g, (c0, c1, ks) in enumerate(((0, S, slice(0, S)), (S, S + P, qs), (S + P, 512, qs))):
                                    m = nc.tensor.matmul(o[:, c0:c1], cqT[at:at + 64, g, pr, qs], ckT[at:at + 64, g, pr, ks],
                                                         start=True, stop=True)
                                m.then_inc(product_done.sem, product_done.next((L, half, "s", i)))
                            elif what == "t":
                                pe.wait_ge(probs_normal.sem, probs_normal.at((L, half, i)))
                                transposes((L, half, "t", i), 2 + i % 2, [prob[:, i % 3, k * P:(k + 1) * P] for k in range(4)], act_read)
                            else:
                                pe.wait_ge(act_read.sem, act_read.at((L, half, "t", i)))
                                ob = 6 + (i // 8) % 2
                                key = (L, half, "ao", i // 8)
                                if i % 8 == 0:
                                    if ob in left:
                                        pe.wait_ge(*left[ob])
                                    left[ob] = out_read.after(key)
                                o = bank[ob][at:at + 64, (pr % 2) * S + b * P:(pr % 2) * S + (b + 1) * P]
                                for k, (g, kb) in enumerate(((0, 0), (0, 1), (1, b), (2, b))):
                                    m = nc.tensor.matmul(o, cv[:, kb, g, h * DH:(h + 1) * DH], probT[:, i % 2, k * P:(k + 1) * P],
                                                         start=k == 0, stop=k == 3)
                                m.then_inc(product_done.sem, product_done.next(key if i % 8 == 7 else (L, half, "o", i)))
                out_product(L, li)
                hidden_from_rows(L, 4)

            for t in range(4):
                pe.wait_ge(h_ready.sem, h_ready.at(("d", t)))
            for b in range(NB):
                for n in range(2):
                    n_b = 2 * b + n
                    if n_b in left:
                        pe.wait_ge(*left[n_b])
                    left[n_b] = act_read.after(("x", b, n))
                    o = bank[n_b]
                    for t in range(4):
                        k = 4 * n + t
                        nc.tensor.matmul(o[:, t * P:(t + 1) * P], hT(k, b)[0], ident_r[:], start=True, stop=False)
                        i = nc.tensor.matmul(o[:, t * P:(t + 1) * P], hT(k, b)[1], ident_r[:], start=False, stop=True)
                    i.then_inc(product_done.sem, product_done.next(("x", b, n)))

            for l in range(2):
                L = f"d{l}"
                w = A["w_in_2"][l]
                hidden_from_rows((L, "mix"), 4)

                def proj(nm, banks, c0, n, hidden=None):
                    token_major([(L, nm, b) for b in range(NB)], banks, [rows_of(w, kh * 512, 4, c0, n) for kh in range(2)], hT, hidden=hidden)
                proj("cq", [0, 1], C_DT, DTQ, hidden=(L, "mix"))
                proj("ck", [2, 3], C_CKV, KVR)
                for u, n in enumerate((256, 256, 128)):
                    feature_major((L, "xbc", u), 4 + u, rows_of(w, 0, KT, C_XBC + u * 256, n), hT)
                proj("z", [0, 1], C_Z, SSD_W)
                proj("uv", [2, 3], C_UV, UV)
                tiles = [(cqt, SSD_H + k * P, "cq") for k in range(3)] + [(ckt, k * P, "ck") for k in range(2)]
                for t in range(3):
                    for nm in ("cq", "ck"):
                        for b in range(NB):
                            pe.wait_ge(latent_normal.sem, latent_normal.at((L, nm, b)))
                    transposes((L, "lt", t), 4 + t % 2,
                               [a[:, b, at:at + P] for a, at, _ in tiles[2 * t:2 * t + 2] for b in range(NB)], dve_read)
                pe.wait_ge(ws_loaded, 16 * (l + 1))
                transposes((L, "wst"), 7, [ws_raw[:, h, :] for h in range(4)], dve_read)
                for t in range(3):
                    pe.wait_ge(r_ready.sem, r_ready.at((L, "lt", t)))
                u, wq = unit(rows_of(A["mla_w_qb_2"][l], 0, 3, 0, 576))
                for n in range(2):
                    for b in range(NB):
                        n_b = 2 * n + b
                        if n_b in left:
                            pe.wait_ge(*left[n_b])
                        left[n_b] = act_read.after((L, "qb", n, b))
                        o = bank[n_b]
                        for k in range(3):
                            i = mm3(o[:, 0:288], rT(5 + k, b), [a[:, k, n * 288:(n + 1) * 288] for a in wq], k == 0, k == 2)
                        i.then_inc(product_done.sem, product_done.next((L, "qb", n, b)))
                unit_done[u] = (L, "qb", 1, 1)
                u, wkv = unit(rows_of(A["mla_w_kvb_2"][l], 0, 2, 0, 768))
                for n in range(2):
                    for b in range(NB):
                        n_b = [4, 5, 6, 0][2 * n + b]
                        if n_b in left:
                            pe.wait_ge(*left[n_b])
                        left[n_b] = act_read.after((L, "kv", n, b))
                        o = bank[n_b]
                        for k in range(2):
                            i = mm3(o[:, 0:384], rT(8 + k, b), [a[:, k, n * 384:(n + 1) * 384] for a in wkv], k == 0, k == 1)
                        i.then_inc(product_done.sem, product_done.next((L, "kv", n, b)))
                unit_done[u] = (L, "kv", 1, 1)
                pe.wait_ge(gmlp_ready.sem, gmlp_ready.at((L, "v")))
                pe.wait_ge(dve_read.sem, dve_read.at((L, "wst")))
                if 7 in left:
                    pe.wait_ge(*left[7])
                left[7] = dve_read.after((L, "gm"))
                o = bank[7]
                v_half = uv[:, :, 256:512].rearrange("p c (h d) -> p h c d", h=4)
                ov = o[:, :].rearrange("p (h c d) -> p h c d", h=4, c=NB)
                for h in range(4):
                    i = nc.tensor.matmul(ov[:, h, :, :], wsT[:, h, :], v_half[:, h, :, :], start=True, stop=True)
                i.then_inc(product_done.sem, product_done.next((L, "gm")))
                pe.wait_ge(xbc_ready.sem, xbc_ready.at(L))
                for c in range(NB):
                    transposes((L, "xs", c), 1 + c, [xbcT[:, t, 3 + c * P:3 + (c + 1) * P] for t in range(4 if c == 0 else 3)], act_read)
                for g in range(2):
                    n_b = 3 + g
                    if n_b in left:
                        pe.wait_ge(*left[n_b])
                    o = bank[n_b]
                    for c in range(NB):
                        i = nc.tensor.matmul(o[:, c * P:(c + 1) * P],
                                             xbcT[64 * g:64 * g + 64, 3, 3 + c * P:3 + (c + 1) * P],
                                             xbcT[64 * g:64 * g + 64, 4, 3 + c * P:3 + (c + 1) * P], start=True, stop=True)
                    i.then_inc(product_done.sem, product_done.next((L, "cb", g)))
                pe.wait_ge(steps_ready.sem, steps_ready.at((L, "dtA")))
                dtA = S_(64, 12)
                if 7 in left:
                    pe.wait_ge(*left[7])
                left[7] = dve_read.after((L, "cum"))
                o = bank[7]
                nc.tensor.matmul(o[:, 0:12], K("upto"), dtA, start=True, stop=True)
                nc.tensor.matmul(o[:, 12:24], K("ones"), dtA, start=True, stop=True).then_inc(product_done.sem, product_done.next((L, "cum")))
                for c in range(NB):
                    for g in range(2):
                        n_b = [5, 6, 0, 1][2 * c + g]
                        if n_b in left:
                            pe.wait_ge(*left[n_b])
                        left[n_b] = dve_read.after((L, "rc", c, g))
                        o = bank[n_b]
                        for h in range(3):
                            at = 64 + c * SSD_H + 3 * g + h
                            i = nc.tensor.matmul(o[:, h * P:(h + 1) * P], stat[:, at:at + 1].to_broadcast([P, P]), K("upto"),
                                                 start=True, stop=True)
                        i.then_inc(product_done.sem, product_done.next((L, "rc", c, g)))
                pe.wait_ge(state_in.sem, state_in.at(L))
                if 2 in left:
                    pe.wait_ge(*left[2])
                left[2] = act_read.after((L, "st"))
                o = bank[2]
                for g in range(2):
                    i = nc.tensor.matmul(o[64 * g:64 * g + 64, 0:192], b_tok[:, 64 * g:64 * g + 64], x_dec[:, 192 * g:192 * g + 192],
                                         start=True, stop=True)
                i.then_inc(product_done.sem, product_done.next((L, "st")))
                pe.wait_ge(act_read.sem, act_read.at((L, "st")))
                for g in range(2):
                    n_b = [7, 1][g]
                    if n_b in left:
                        pe.wait_ge(*left[n_b])
                    left[n_b] = dve_read.after((L, "yo", g))
                    o = bank[n_b]
                    i = nc.tensor.matmul(o[:, 0:192], xbcT[64 * g:64 * g + 64, 4, 3 + P:3 + S], st_sb[64 * g:64 * g + 64, :],
                                         start=True, stop=True)
                    i.then_inc(product_done.sem, product_done.next((L, "yo", g)))
                for c in range(NB):
                    for g in range(2):
                        pe.wait_ge(decay_ready.sem, decay_ready.at((L, c, g)))
                        left[3 + g] = decay_ready.after((L, c, g))
                    n_b = 5 + c
                    if n_b in left:
                        pe.wait_ge(*left[n_b])
                    left[n_b] = dve_read.after((L, "yd", c))
                    o = bank[n_b]
                    for h in range(SSD_H):
                        i = nc.tensor.matmul(o[:, h * DH:(h + 1) * DH], decay[:, c * SSD_H + h, :], xs[:, c, h * DH:(h + 1) * DH],
                                             start=True, stop=True)
                    i.then_inc(product_done.sem, product_done.next((L, "yd", c)))
                for t in range(3):
                    pe.wait_ge(roped.sem, roped.at((L, "q")))
                    transposes((L, "qt", t), 0 + t % 2, [qtok[:, b, h * M_QK:(h + 1) * M_QK] for h in (2 * t, 2 * t + 1) for b in range(NB)], act_read)
                for t in range(3):
                    pe.wait_ge(roped.sem, roped.at((L, "k")))
                    transposes((L, "kt", t), 0 + (t + 1) % 2, [ktok[:, b, h * M_QK:(h + 1) * M_QK] for h in (2 * t, 2 * t + 1) for b in range(NB)], act_read)
                pe.wait_ge(dve_read.sem, dve_read.at((L, "gm")))
                transposes((L, "at"), 3, [uv[:, b, k * P:(k + 1) * P] for k in range(2) for b in range(NB)], dve_read)
                pe.wait_ge(mixer_out.sem, mixer_out.at((L, "b")))
                transposes((L, "bt", 0), 2, [y_b[:, b, k * P:(k + 1) * P] for k in range(2) for b in range(NB)], dve_read)
                transposes((L, "bt", 1), 4, [y_b[:, b, 2 * P:3 * P] for b in range(NB)], dve_read)
                for t in range(3):
                    pe.wait_ge(act_read.sem, act_read.at((L, "qt", t)))
                    pe.wait_ge(act_read.sem, act_read.at((L, "kt", t)))
                for what, h in attention_order(M_H):
                    if what == "s":
                        n_b = 0 + h % 2
                        if n_b in left:
                            pe.wait_ge(*left[n_b])
                        left[n_b] = dve_read.after((L, "s", h))
                        o = bank[n_b]
                        for b in range(NB):
                            n = (b + 1) * P
                            m = nc.tensor.matmul(o[:, b * P:b * P + n], mqT[0:M_QK, h, b * P:(b + 1) * P], mkvT[0:M_QK, h, 0:n],
                                                 start=True, stop=True)
                        m.then_inc(product_done.sem, product_done.next((L, "s", h)))
                    elif what == "t":
                        pe.wait_ge(probs_normal.sem, probs_normal.at((L, h)))
                        transposes((L, "t", h), 2 + h % 2, [prob[:, h % 3, k * P:(k + 1) * P] for k in range(3)], act_read)
                    else:
                        pe.wait_ge(act_read.sem, act_read.at((L, "t", h)))
                        ob, key = 5 + h // 4, (L, "co", h // 4)
                        if h % 4 == 0:
                            if ob in left:
                                pe.wait_ge(*left[ob])
                            left[ob] = out_read.after(key)
                        o = bank[ob][64 * (h % 2):64 * (h % 2) + 64, (h % 4 // 2) * S:(h % 4 // 2 + 1) * S]
                        vh = kvtok[:, :, h * P + DH:(h + 1) * P]
                        nc.tensor.matmul(o, vh[:, 0, :], probT[:, h % 2, 0:S], start=True, stop=False)
                        m = nc.tensor.matmul(o[:, P:S], vh[:, 1, :], probT[:, h % 2, S:S + P], start=False, stop=True)
                        m.then_inc(product_done.sem, product_done.next(key if h in (3, 5) else (L, "o", h)))
                for key in ((L, "at"), (L, "bt", 0), (L, "bt", 1), (L, "co", 0), (L, "co", 1)):
                    pe.wait_ge(r_ready.sem, r_ready.at(key))
                for n in range(2):
                    token_major([(L, "wo", n, b) for b in range(NB)], [2 * n, 2 * n + 1],
                                [rows_of(A["w_out_2"][l], kh * 512, 4, n * 512, 512) for kh in range(2)], rT, reader=dve_read)
                hidden_from_rows((L, "mlp"), 4)

                def up(e):
                    for u in range(2):
                        feature_major((L, "up", e, u), (2 * e + u) % 4,
                                      rows_of(A["mlp_w1_2"][l], 0, KT, (2 * e + u) * 256, 256), hT,
                                      hidden=(L, "mlp") if e + u == 0 else None)

                def down(e):
                    for u in range(2):
                        pe.wait_ge(r_ready.sem, r_ready.at((L, "up", e, u)))
                    for n in range(2):
                        token_major([(L, "dn", n, b) for b in range(NB)], [4 + 2 * n, 5 + 2 * n],
                                    [rows_of(A["mlp_w2_2"][l], e * 512, 4, n * 512, 512)],
                                    lambda k, b: rT(4 * (e % 2) + k, b), reader=dve_read, opened=e == 0, closed=e == 7)
                    down_done[L, e] = unit_done[len(units) - 1]
                for e in range(9):
                    if e < 8:
                        up(e)
                    if e > 0:
                        down(e - 1)

        N_UNITS = len(units)

        @block.sync
        def _(sp):
            n_c = n_kept
            sp.dma_start(const[:], A["const"][:, 0:n_c]).then_inc(consts_loaded, 16)
            sp.dma_start(const_once, A["const"][:, n_c:]).then_inc(consts_loaded, 16)
            xv = A["x"][0].rearrange("(c b a) d -> a b c d", a=4, b=4)
            for a in range(4):
                for b in range(4):
                    p0 = (a % 2) * 64 + b * 16
                    sp.dma_start(x_in[p0:p0 + 16, a // 2, :], xv[a, b]).then_inc(x_loaded, 16)
            sp.dma_start(mem_in, A["mem"][0].rearrange("(b p) d -> p b d", p=P)).then_inc(mem_loaded, 16)
            for u, (source, kts, n) in enumerate(units):
                if u >= RAW_SLOTS:
                    sp.wait_ge(w_split.sem, w_split.at(u - RAW_SLOTS))
                sp.dma_start(w_raw[:, u % RAW_SLOTS, 0:kts * n].rearrange("p (k n) -> p k n", k=kts), source)\
                    .then_inc(w_loaded[u % RAW_SLOTS], 16)
                for l, key in enumerate((("a1", "mo"), ("d0", "co", 1))):
                    if u == product_done.unit[key] + RAW_SLOTS + 1:
                        sp.wait_ge(product_done.sem, product_done.at(key))
                        sp.dma_start(ws_raw, A["gmlp_w_s_2"][l].rearrange("h t s -> t h s")).then_inc(ws_loaded, 16)
            sp.wait_ge(product_done.sem, product_done.at(("d1", "co", 1)))
            sp.dma_start(gf, A["final_norm_g_2"].partition_broadcast(P)).then_inc(gf_loaded, 16)
            for b in range(NB):
                sp.wait_ge(row_out.sem, row_out.at(b))
                sp.dma_start(out[0, b * P:(b + 1) * P, :], z[:, b, :]).then_inc(stored, 16)
            sp.wait_ge(stored, 16 * NB)

        @block.gpsimd
        def _(pool):
            rows = [(A["ln_in_g"], None), (A["ln_in_b"], None), (A["ln_g"], None), (A["ln_b"], None)]
            at = 0
            for a, _ in rows:
                flat = a if len(a.shape) == 1 else a.rearrange("l n -> (l n)")
                n = flat.shape[0] // P
                pool.dma_start(rows_a[at:at + n, :], flat.rearrange("(k p) -> k p", p=P)).then_inc(rows_loaded, 16)
                at += n
            at = 0
            for nm in ("norm_mix_g_2", "norm_mlp_g_2", "ssd_conv_w_2", "ssd_conv_b_2", "mla_q_norm_g_2", "mla_kv_norm_g_2",
                       "ssd_norm_g_2", "gmlp_b_s_2"):
                a = A[nm]
                flat = a.rearrange("l n -> (l n)") if len(a.shape) == 2 else a.rearrange("l k n -> (l k n)")
                n = flat.shape[0] // P
                pool.dma_start(rows_b[at:at + n, :], flat.rearrange("(k p) -> k p", p=P)).then_inc(rows_loaded, 16)
                at += n
            at = 0
            for nm in ("q_norm_g", "k_norm_g", "gmlp_v_norm_g_2", "ssd_dt_bias_2", "ssd_a_log_2", "ssd_d_2"):
                flat = A[nm].rearrange("l n -> (l n)")
                n = flat.shape[0]
                pool.dma_start(row[:, at:at + n], flat.partition_broadcast(P)).then_inc(rows_loaded, 16)
                at += n
            for u, (_, kts, n) in enumerate(units):
                pool.wait_ge(w_rounded.sem, w_rounded.at(u))
                s, m = u % SPLIT_SLOTS, kts * n
                nc.gpsimd.tensor_tensor(w_lo[:, s, 0:m], w_raw[:, u % RAW_SLOTS, 0:m], w_hi[:, s, 0:m].bitcast(F32),
                                               ALU.subtract).then_inc(w_split.sem, w_split.next(u))

        @block.scalar
        def _(act):
            rounded = [0]

            def round_weights(key):
                while rounded[0] < min(N_UNITS, product_done.unit[key] + 1 + SPLIT_SLOTS):
                    u = rounded[0]
                    _, kts, n = units[u]
                    act.wait_ge(w_loaded[u % RAW_SLOTS], 16 * (u // RAW_SLOTS + 1))
                    if u >= SPLIT_SLOTS:
                        act.wait_ge(product_done.sem, product_done.at(unit_done[u - SPLIT_SLOTS]))
                    nc.scalar.activation(w_hi[:, u % SPLIT_SLOTS, 0:kts * n], w_raw[:, u % RAW_SLOTS, 0:kts * n], ACT.Copy).then_inc(w_rounded.sem, w_rounded.next(u))
                    rounded[0] += 1

            def evac(key, dst, src, func=ACT.Copy, scale=1.0, bias=0.0):
                round_weights(key)
                act.wait_ge(product_done.sem, product_done.at(key))
                args = {} if func == ACT.Copy else {"bias": bias}
                nc.scalar.activation(dst, src, func, scale=scale, **args).then_inc(act_read.sem, act_read.next(key))

            def flat2(a):
                return a.rearrange("p a b -> p (a b)")

            def attend(L, n):
                for what, i in attention_order(n):
                    if what == "s":
                        round_weights((L, "s", i))
                        act.wait_ge(product_done.sem, product_done.at((L, "s", i)))
                        if i >= 3:
                            act.wait_ge(product_done.sem, product_done.at((L, "t", i - 3)))
                        act.wait_ge(row_max.sem, row_max.at((L, i)))
                        o = bank[i % 2]
                        for b in range(NB):
                            ins = nc.scalar.activation(prob[:, i % 3, b * S:(b + 1) * S], o[:, b * S:(b + 1) * S], ACT.Exp,
                                                       bias=S_(16 + 4 * (i % 3) + b, 1), accum_out=S_(32 + 4 * (i % 3) + b, 1))
                            if b == 0:
                                ins.then_inc(exp_half.sem, exp_half.next((L, "s", i)))
                            else:
                                ins.then_inc(act_read.sem, act_read.next((L, "s", i)))
                    elif what == "t":
                        if i >= 2:
                            act.wait_ge(product_done.sem, product_done.at(out_key(L, i - 2)))
                        evac((L, "t", i), probT[:, i % 2, :], bank[2 + i % 2][:, :])

            def out_key(L, i):
                base, what = L
                if what == "m":
                    return (base, "mo") if i == 3 else (L, "o", i)
                return (base, "ao", i // 4) if i % 4 == 3 else (L, "o", i)

            def gates(L, dst):
                evac((L, "qm"), flat2(dst), bank[0][:, :], scale=0.125)
                for u in range(5):
                    evac((L, "gate", u), flat2(gate[:, 2 * u:2 * u + 2, :]), bank[1 + u][:, :], ACT.Silu)

            def hidden_hi(L, nxt):
                for j in range(4):
                    act.wait_ge(dve_read.sem, dve_read.at((L, "zt", j)))
                    nc.scalar.activation(flat2(h_hi[:, 2 * j:2 * j + 2, :]), split_t[:, j % 2, :], ACT.Copy)\
                        .then_inc(h_rounded.sem, h_rounded.next((nxt, j)))

            act.wait_ge(consts_loaded, 32)
            nc.scalar.activation(flat2(dft_hi[:, :, :]), const_once[:, 0:1024], ACT.Copy)
            nc.scalar.activation(ident_r[:], ident, ACT.Copy)
            nc.scalar.activation(res_hi[:], const_once[:, 1024:1024 + P], ACT.Copy).then_inc(tables_rounded.sem, tables_rounded.next(0))
            round_weights("cols")
            act.wait_ge(product_done.sem, product_done.at("cols"))
            nc.scalar.activation(col_a[:], bank[0][:, 0:N_COL_A], ACT.Copy)
            nc.scalar.activation(col_b[:], bank[0][:, 128:128 + N_COL_B], ACT.Copy).then_inc(act_read.sem, act_read.next("cols"))
            act.wait_ge(rows_loaded, 16 * ROW_DMAS)
            nc.scalar.activation(row[:, 652:664], row[:, 652:664], ACT.Exp).then_inc(a_exp.sem, a_exp.next(0))
            act.wait_ge(x_loaded, 256)
            for b, n in BY_SCALAR:
                act.wait_ge(row_stats.sem, row_stats.at(("in", b)))
                nc.scalar.activation(z[:, b, n * 512:(n + 1) * 512], x_in[:, b, n * 512:(n + 1) * 512], ACT.Identity,
                                     scale=S_(8 + b, 1), bias=S_(10 + b, 1)).then_inc(rows_normal.sem, rows_normal.next(("in", b, n)))
            hidden_hi("in", "a0")
            evac(("mem", "k"), flat2(mkT[:, :, :]), bank[4][:, :])
            evac(("mem", "v"), flat2(mv[:, :, :]), bank[5][:, :])

            for li, (kind, j) in enumerate(LAYERS):
                L = f"{kind}{j}"
                if kind == "a":
                    gates(L, qmT)
                    attend((L, "m"), MEM_HEADS)
                    for g in range(4):
                        evac((L, "f1", g, 0), spectra[:, 0, g, :], bank[2 * (g % 3)][:, :])
                elif kind == "b":
                    for c in range(3):
                        for b in range(NB):
                            round_weights((L, "p", c, b))
                            act.wait_ge(product_done.sem, product_done.at((L, "p", c, b)))
                            nc.scalar.activation(qkv[:, b, c * 512:(c + 1) * 512], bank[2 * c + b][:, :], ACT.Copy).then_inc(act_read.sem, act_read.next((L, "p", c, b)))
                    gates(L, b_qmT)
                    for t in range(4):
                        evac((L, "qt", t), flat2(bqT[:, 2 * t:2 * t + 2, :]), bank[6 + t % 2][:, :], scale=0.125)
                    for t in range(2):
                        evac((L, "kt", t), flat2(bkT[:, 2 * t:2 * t + 2, :]), bank[6 + t % 2][:, :])
                    attend((L, "m"), MEM_HEADS)
                    attend((L, "h"), HEADS)
                else:
                    gates(L, c_qmT)
                    attend((L, "m"), MEM_HEADS)
                    for half in range(2):
                        chunks = [(s, g) for g in range(3) for s in range(2)] + [(2, g) for g in range(3)]
                        for n, (s, g) in enumerate(chunks):
                            if s == 2:
                                for b in range(NB):
                                    evac((L, half, "p", s, g, b), cv[:, b, g, :], bank[2 * (n % 2) + b][:, :])
                            if 1 <= n <= 6:
                                s, g = chunks[n - 1]
                                for t in range(2):
                                    evac((L, half, "xt", s, g, t), flat2((cqT if s == 0 else ckT)[:, g, 2 * t:2 * t + 2, :]),
                                         bank[4 + t][:, :], scale=0.125 if s == 0 else 1.0)
                        for what, i in attention_order(16):
                            if what == "s":
                                round_weights((L, half, "s", i))
                                act.wait_ge(product_done.sem, product_done.at((L, half, "s", i)))
                                if i >= 3:
                                    act.wait_ge(product_done.sem, product_done.at((L, half, "t", i - 3)))
                                act.wait_ge(dve_read.sem, dve_read.at((L, half, "s", i)))
                                nc.scalar.activation(prob[:, i % 3, :], masked[:, i % 2, :], ACT.Exp, scale=-1.0,
                                                            bias=S_(16 + 4 * (i % 3), 1), accum_out=S_(32 + 4 * (i % 3), 1)).then_inc(exp_done.sem, exp_done.next((L, half, i)))
                            elif what == "t":
                                if i >= 2:
                                    act.wait_ge(product_done.sem, product_done.at((L, half, "o", i - 2) if (i - 2) % 8 != 7 else (L, half, "ao", (i - 2) // 8)))
                                evac((L, half, "t", i), probT[:, i % 2, :], bank[2 + i % 2][:, :])
                round_weights((L, "wo", 1, 0))
                for b, n in BY_SCALAR:
                    act.wait_ge(row_stats.sem, row_stats.at((L, b)))
                    nc.scalar.activation(z[:, b, n * 512:(n + 1) * 512], bank[2 * n + b][:, :], ACT.Identity,
                                         scale=S_(8 + b, 1), bias=S_(10 + b, 1)).then_inc(rows_normal.sem, rows_normal.next((L, b, n)))
                hidden_hi(L, LAYER_NAMES[li + 1])
                round_weights((L, "wo", 1, 1))

            def row_squares(squares, a, total, key):
                if square_sum.made:
                    act.wait_ge(square_sum.sem, square_sum.made)
                nc.scalar.activation(squares, a, ACT.Square, accum_out=total).then_inc(square_sum.sem, square_sum.next(key))

            def half_squares(L, key, b, n):
                cols = slice(n * 512, (n + 1) * 512)
                row_squares(z[:, b, cols], x[:, b, cols], S_(2 * b + n, 1), (L, key, b, n))

            def normal_rows(L):
                for b, n in BY_SCALAR:
                    act.wait_ge(row_stats.sem, row_stats.at((L, b)))
                    nc.scalar.activation(z[:, b, n * 512:(n + 1) * 512], x[:, b, n * 512:(n + 1) * 512], ACT.Identity,
                                         scale=S_(8 + b, 1)).then_inc(rows_normal.sem, rows_normal.next((L, b, n)))
                hidden_hi(L, L)

            for l in range(2):
                L = f"d{l}"
                if l == 0:
                    for b in range(NB):
                        for n in range(2):
                            evac(("x", b, n), x[:, b, n * 512:(n + 1) * 512], bank[2 * b + n][:, :])
                            act.wait_ge(act_read.sem, act_read.at(("x", b, n)))
                            half_squares(L, "mix", b, n)
                else:
                    round_weights(("d0", "dn", 1, 1))
                    for n in range(2):
                        for b in range(NB):
                            act.wait_ge(dve_read.sem, dve_read.at(("d0", "dn", n, b)))
                            half_squares(L, "mix", b, n)
                normal_rows((L, "mix"))
                for b in range(NB):
                    evac((L, "cq", b), cqt[:, b, :], bank[b][:, 0:DTQ])
                for b in range(NB):
                    evac((L, "ck", b), ckt[:, b, :], bank[2 + b][:, 0:KVR])
                for nm, a, c0, n, s0 in (("cq", cqt, SSD_H, Q_RANK, 0), ("ck", ckt, 0, KV_RANK, 2)):
                    for b in range(NB):
                        act.wait_ge(act_read.sem, act_read.at((L, nm, b)))
                        row_squares(split_t[:, 1, 0:n], a[:, b, c0:c0 + n], S_(44 + s0 + b, 1), (L, nm, b))
                for u, n in enumerate((2, 2, 1)):
                    evac((L, "xbc", u), xbcT[:, 2 * u:2 * u + n, 3:3 + S], bank[4 + u][:, 0:n * S].rearrange("p (t s) -> p t s", t=n))
                for b in range(NB):
                    evac((L, "z", b), zg[:, b, :], bank[b][:, 0:SSD_W], ACT.Silu)
                round_weights((L, "uv", 0))
                act.wait_ge(conv_done.sem, conv_done.at(L))
                nc.scalar.activation(xbcT[:, :, 3:3 + S], conv, ACT.Silu).then_inc(xbc_ready.sem, xbc_ready.next(L))
                for b in range(NB):
                    evac((L, "uv", b), uv[:, b, :], bank[2 + b][:, :], ACT.Gelu_apprx_tanh)
                for b in range(NB):
                    act.wait_ge(act_read.sem, act_read.at((L, "uv", b)))
                    row_squares(split_t[:, 1, 0:256], uv[:, b, 256:512], S_(48 + b, 1), (L, "uv", b))
                act.wait_ge(steps_in.sem, steps_in.at((L, "e")))
                nc.scalar.activation(S_(88, 12), S_(76, 12), ACT.Exp).then_inc(exp_small.sem, exp_small.next((L, "e")))
                for n in range(2):
                    for b in range(NB):
                        evac((L, "qb", n, b), qtok[:, b, n * 288:(n + 1) * 288], bank[2 * n + b][:, 0:288])
                for n in range(2):
                    for b in range(NB):
                        evac((L, "kv", n, b), kvtok[:, b, n * 384:(n + 1) * 384], bank[[4, 5, 6, 0][2 * n + b]][:, 0:384])
                round_weights((L, "xs", 0))
                act.wait_ge(product_done.sem, product_done.at((L, "xs", 0)))
                nc.scalar.activation(b_tok, bank[1][:, SSD_W:512], ACT.Copy)
                nc.scalar.activation(xs[:, 0, :], bank[1][:, 0:SSD_W], ACT.Copy).then_inc(act_read.sem, act_read.next((L, "xs", 0)))
                evac((L, "xs", 1), xs[:, 1, :], bank[2][:, 0:SSD_W])
                act.wait_ge(steps_in.sem, steps_in.at((L, "end")))
                nc.scalar.activation(S_(136, 12), S_(124, 12), ACT.Exp).then_inc(exp_small.sem, exp_small.next((L, "end")))
                for c in range(NB):
                    for g in range(2):
                        round_weights((L, "rc", c, g))
                        act.wait_ge(dve_read.sem, dve_read.at((L, "rc", c, g)))
                        d3 = decay[:, c * SSD_H + 3 * g:c * SSD_H + 3 * g + 3, :]
                        nc.scalar.activation(d3, d3, ACT.Exp).then_inc(exp_seg.sem, exp_seg.next((L, c, g)))
                evac((L, "st"), st_sb, bank[2][:, 0:192])
                for t in range(3):
                    evac((L, "qt", t), flat2(mqT[0:M_QK, 2 * t:2 * t + 2, :]), bank[t % 2][0:M_QK, :], scale=float(M_QK) ** -0.5)
                for t in range(3):
                    evac((L, "kt", t), flat2(mkvT[0:M_QK, 2 * t:2 * t + 2, :]), bank[(t + 1) % 2][0:M_QK, :])
                for what, h in attention_order(M_H):
                    if what == "s":
                        round_weights((L, "s", h))
                        act.wait_ge(product_done.sem, product_done.at((L, "s", h)))
                        if h >= 3:
                            act.wait_ge(product_done.sem, product_done.at((L, "t", h - 3)))
                        for b, (c0, c1) in enumerate(((0, P), (P, P + S))):
                            if b == 0:
                                act.wait_ge(row_max.sem, row_max.at((L, h)))
                            else:
                                act.wait_ge(dve_read.sem, dve_read.at((L, "s", h)))
                            nc.scalar.activation(prob[:, h % 3, c0:c1], masked[:, h % 2, c0:c1], ACT.Exp, scale=-1.0,
                                                        bias=S_(16 + 4 * (h % 3) + b, 1), accum_out=S_(32 + 4 * (h % 3) + b, 1)).then_inc(exp_done.sem, exp_done.next((L, h, b)))
                    elif what == "t":
                        if h >= 2:
                            act.wait_ge(product_done.sem, product_done.at((L, "co", 0) if h - 2 == 3 else (L, "o", h - 2)))
                        evac((L, "t", h), probT[:, h % 2, 0:384], bank[2 + h % 2][:, 0:384])
                round_weights((L, "wo", 1, 1))
                for n in range(2):
                    for b in range(NB):
                        act.wait_ge(dve_read.sem, dve_read.at((L, "wo", n, b)))
                        half_squares(L, "mlp", b, n)
                normal_rows((L, "mlp"))
                for e in range(8):
                    for u in range(2):
                        t = (2 * e + u) % 4
                        round_weights((L, "up", e, u))
                        act.wait_ge(product_done.sem, product_done.at((L, "up", e, u)))
                        if 2 * e + u >= 2:
                            act.wait_ge(r_ready.sem, r_ready.at((L, "up", (2 * e + u - 2) // 2, u)))
                        relu = masked[:, u, :]
                        nc.scalar.activation(relu, bank[t][:, :], ACT.Relu).then_inc(act_read.sem, act_read.next((L, "up", e, u)))
                        act.wait_ge(act_read.sem, act_read.at((L, "up", e, u)))
                        if e >= 2:
                            act.wait_ge(product_done.sem, product_done.at(down_done[L, e - 2]))
                        t0 = 4 * (e % 2) + 2 * u
                        nc.scalar.activation(flat2(r_hi[:, t0:t0 + 2, :]), relu, ACT.Square).then_inc(square_hi.sem, square_hi.next((L, "up", e, u)))
            round_weights(("d1", "dn", 1, 1))
            for n in range(2):
                for b in range(NB):
                    act.wait_ge(dve_read.sem, dve_read.at(("d1", "dn", n, b)))
                    half_squares("end", "end", b, n)

        @block.vector
        def _(dve):
            v = nc.vector

            def link(ins):
                ins.then_inc(vector_step.sem, vector_step.next(vector_step.made))
                dve.wait_ge(vector_step.sem, vector_step.made)

            def tt(o, a, b, op):
                link(v.tensor_tensor(o, a, b, op))

            def ts(o, a, s1, s2, op0, op1=ALU.bypass):
                link(v.tensor_scalar(o, a, s1, None, op0) if s2 is None else v.tensor_scalar(o, a, s1, s2, op0, op1))

            def stt(o, a, s, b, op0, op1):
                link(v.scalar_tensor_tensor(o, a, s, b, op0, op1))

            MUL, ADD, SUB = ALU.mult, ALU.add, ALU.subtract

            def rsqrt(y, a, t):
                ts(y.bitcast(I32), a.bitcast(I32), 1, None, ALU.logical_shift_right)
                ts(y.bitcast(I32), y.bitcast(I32), -1.0, float(0x5F3759DF), MUL, ADD)
                for n in range(3):
                    tt(t, y, y, MUL)
                    stt(t, a, -0.5, t, MUL, MUL)
                    stt(y, t, 1.5, y, ADD, MUL)

            def flat2(a):
                return a.rearrange("p a b -> p (a b)")

            def split(hi, lo, value):
                link(v.tensor_copy(hi, value))
                return v.tensor_tensor(lo, value, hi.bitcast(F32), SUB)

            def split_hidden(L, nxt, b0, gain, shift, natural=False):
                for j in range(5):
                    if j < 4:
                        dve.wait_ge(product_done.sem, product_done.at((L, "zt", j)))
                        if j >= 2:
                            dve.wait_ge(h_ready.sem, h_ready.at((nxt, j - 2)))
                        t = split_t[:, j % 2, :]
                        for m in range(2):
                            k = 2 * j + m
                            src, dst = bank[b0 + j][:, m * S:(m + 1) * S], t[:, m * S:(m + 1) * S]
                            if natural:
                                src = src.rearrange("p (a b c) -> p a b c", a=4, b=4)
                                dst = dst.rearrange("p (c b a) -> p a b c", a=4, b=4)
                            if shift is None:
                                ins = v.tensor_scalar(dst, src, gain[:, k:k + 1], None, MUL)
                            else:
                                ins = v.tensor_scalar(dst, src, gain[:, k:k + 1], shift[:, k:k + 1], MUL, ADD)
                        ins.then_inc(dve_read.sem, dve_read.next((L, "zt", j)))
                    if j > 0:
                        pair = slice(2 * j - 2, 2 * j)
                        dve.wait_ge(dve_read.sem, dve_read.at((L, "zt", j - 1)))
                        dve.wait_ge(h_rounded.sem, h_rounded.at((nxt, j - 1)))
                        v.tensor_tensor(flat2(h_lo[:, pair, :]), split_t[:, (j - 1) % 2, :], flat2(h_hi[:, pair, :]).bitcast(F32), SUB)\
                            .then_inc(h_ready.sem, h_ready.next((nxt, j - 1)))
                dve.wait_ge(h_ready.sem, h_ready.made)

            def rsqrt_col(y, a, t):
                ts(y.bitcast(I32), a.bitcast(I32), -0.5, float(0x5F3759DF - 2 ** 31), MUL, ADD)
                for three in (3.0, 12.0, 768.0):
                    stt(t, y, a, y, MUL, MUL)
                    if three < 768.0:
                        stt(y, t, three, y, SUB, MUL)
                return v.scalar_tensor_tensor(y, t, three, y, SUB, MUL)

            def row_norm(L, b):
                mean, var = S_(152 + 2 * b, 1), S_(153 + 2 * b, 1)
                link(v.bn_aggr(S_(152 + 2 * b, 2), S_(128 + 12 * b, 12)))
                ts(S_(4 + b, 1), var, 2.0 ** 26, 1e-5 * 2.0 ** 26, MUL, ADD)
                link(rsqrt_col(S_(8 + b, 1), S_(4 + b, 1), S_(6 + b, 1)))
                v.scalar_tensor_tensor(S_(10 + b, 1), mean, -1.0, S_(8 + b, 1), MUL, MUL).then_inc(row_stats.sem, row_stats.next((L, b)))

            def normal_half(L, src):
                v.tensor_scalar(z[:, 1, 0:512], src, S_(154, 1), S_(9, 1), SUB, MUL).then_inc(rows_normal_v.sem, rows_normal_v.next(L))

            def softmax_max(L, i, src, key):
                dve.wait_ge(product_done.sem, product_done.at(key))
                v.tensor_reduce(S_(16 + 4 * (i % 3), 2), src.rearrange("p (b k) -> p b k", b=NB), AX.X, ALU.max, negate=True).then_inc(row_max.sem, row_max.next((L, i)))
                dve.wait_ge(row_max.sem, row_max.made)

            def gated(L, j, key, src):
                dve.wait_ge(product_done.sem, product_done.at(key))
                if src is not None:
                    t = split_t[:, 0, :]
                    v.tensor_tensor(t, src, flat2(gate[:, 2 * j:2 * j + 2, :]), MUL).then_inc(out_read.sem, out_read.next(key))
                    dve.wait_ge(out_read.sem, out_read.made)
                    split(flat2(r_hi[:, 2 * j:2 * j + 2, :]), flat2(r_lo[:, 2 * j:2 * j + 2, :]), t).then_inc(r_ready.sem, r_ready.next((L, j)))
                    dve.wait_ge(r_ready.sem, r_ready.made)

            def normalise(i, parts):
                n = len(parts)
                link(v.reciprocal(S_(52 + 2 * (i % 3), n), S_(32 + 4 * (i % 3), n)))
                return S_(52 + 2 * (i % 3), n)

            def attend(L, n, outs):
                for what, i in attention_order(n, "tsv"):
                    if what == "s":
                        softmax_max(L, i, bank[i % 2][:, :], (L, "s", i))
                    elif what == "t":
                        dve.wait_ge(act_read.sem, act_read.at((L, "s", i)))
                        r = normalise(i, range(NB))
                        for b in range(NB):
                            p_ = prob[:, i % 3, b * S:(b + 1) * S]
                            ins = v.tensor_scalar(p_, p_, r[:, b:b + 1], None, MUL)
                            if b == 1:
                                ins.then_inc(probs_normal.sem, probs_normal.next((L, i)))
                                dve.wait_ge(probs_normal.sem, probs_normal.made)
                            else:
                                link(ins)
                    else:
                        outs(i)

            dve.wait_ge(consts_loaded, 32)
            dve.wait_ge(tables_rounded.sem, tables_rounded.at(0))
            tt(flat2(dft_lo[:, :, :]), const_once[:, 0:1024], flat2(dft_hi[:, :, :]).bitcast(F32), SUB)
            v.tensor_tensor(res_lo[:], const_once[:, 1024:1024 + P], res_hi[:].bitcast(F32), SUB).then_inc(tables_split.sem, tables_split.next("lo"))
            dve.wait_ge(tables_split.sem, tables_split.made)
            dve.wait_ge(x_loaded, 256)
            for b in range(NB):
                for n in range(2):
                    link(v.bn_stats(S_(128 + 12 * b + 6 * n, 6), x_in[:, b, n * 512:(n + 1) * 512]))
                row_norm("in", b)
            normal_half("in", x_in[:, 1, 0:512])
            for j in range(4):
                dve.wait_ge(product_done.sem, product_done.at(("mem", "t", j)))
                t = split_t[:, 0, :]
                v.tensor_copy(t, bank[4 + j][:, :]).then_inc(dve_read.sem, dve_read.next(("mem", "t", j)))
                dve.wait_ge(dve_read.sem, dve_read.made)
                split(flat2(r_hi[:, 2 * j:2 * j + 2, :]), flat2(r_lo[:, 2 * j:2 * j + 2, :]), t).then_inc(r_ready.sem, r_ready.next(("mem", j)))
                dve.wait_ge(r_ready.sem, r_ready.made)
            dve.wait_ge(act_read.sem, act_read.at("cols"))
            split_hidden("in", "a0", 0, *ln_cols(0))

            for li, (kind, j) in enumerate(LAYERS):
                L = f"{kind}{j}"

                def mem_out(i):
                    if i == 3:
                        gated(L, 4, (L, "mo"), bank[7][:, :])
                if kind == "a":
                    for u in range(5):
                        dve.wait_ge(act_read.sem, act_read.at((L, "gate", u)))
                    attend((L, "m"), MEM_HEADS, mem_out)
                    for g in range(4):
                        dve.wait_ge(product_done.sem, product_done.at((L, "f1", g, 1)))
                        v.tensor_copy(spectra[:, 1, g, :], bank[2 * (g % 3) + 1][:, :]).then_inc(dve_read.sem, dve_read.next((L, "f1", g, 1)))
                        dve.wait_ge(dve_read.sem, dve_read.made)
                    for t in range(4):
                        gated(L, t, (L, "f2", t), bank[2 * (t % 2)][:, :])
                elif kind == "b":
                    for n, g in enumerate((q_gain, k_gain)):
                        cos_t = K("axial_cos").rearrange("p (b d) -> p b d", b=NB)
                        sin_t = K("axial_sin").rearrange("p (b d) -> p b d", b=NB)
                        gb = g.unsqueeze(1).to_broadcast([P, NB, DH])
                        tt(gcos[:, n, :, :], cos_t, gb, MUL)
                        g4 = g.rearrange("p (h r e) -> p h r e", h=2, r=2)
                        for b in range(NB):
                            s4 = sin_t[:, b, :].rearrange("p (h r e) -> p h r e", h=2, r=2)
                            o4 = gsin[:, n, b, :].rearrange("p (h r e) -> p h r e", h=2, r=2)
                            for r in range(2):
                                tt(o4[:, :, r, :], s4[:, :, r, :], g4[:, :, 1 - r, :], MUL)
                    ssq = S_(160, 40)
                    for b in range(NB):
                        for c in range(3):
                            dve.wait_ge(act_read.sem, act_read.at((L, "p", c, b)))
                        tt(b_sq, qkv[:, b, 0:1280], qkv[:, b, 0:1280], MUL)
                        link(v.tensor_reduce(ssq[:, 20 * b:20 * b + 20], b_sq.rearrange("p (h d) -> p h d", d=DH), AX.X, ALU.add))
                    ts(ssq, ssq, 1.0 / DH, 1e-6, MUL, ADD)
                    rs = S_(200, 40)
                    rsqrt(rs, ssq, S_(240, 40))
                    for n, (c0, nh) in enumerate(((0, HEADS), (D, KV_HEADS))):
                        for b in range(NB):
                            src = qkv[:, b, c0:c0 + nh * DH]
                            rot = b_rot[:, 0:nh * DH]
                            s5 = src.rearrange("p (h f r e) -> p h f r e", f=2, r=2, e=16)
                            r5 = rot.rearrange("p (h f r e) -> p h f r e", f=2, r=2, e=16)
                            t5 = gsin[:, n, b, :].rearrange("p (f r e) -> p f r e", f=2, r=2)
                            for r in range(2):
                                for f in range(2):
                                    tt(r5[:, :, f, r, :], s5[:, :, f, 1 - r, :], t5[:, f, r, :].unsqueeze(1).to_broadcast([P, nh, 16]), MUL)
                            s3 = src.rearrange("p (h d) -> p h d", d=DH)
                            tt(s3, s3, gcos[:, n, b, :].unsqueeze(1).to_broadcast([P, nh, DH]), MUL)
                            tt(src, src, rot, ADD)
                            rb = rs[:, 20 * b + (0 if n == 0 else HEADS):20 * b + (HEADS if n == 0 else 20)]
                            if n == 0:
                                v.tensor_tensor(s3, s3, rb.unsqueeze(2).to_broadcast([P, nh, DH]), MUL).then_inc(roped.sem, roped.next((L, "q", b)))
                                dve.wait_ge(roped.sem, roped.made)
                            else:
                                for r in range(2):
                                    ins = v.tensor_tensor(k_dup[:, b, :, r, :], s3, rb.unsqueeze(2).to_broadcast([P, nh, DH]), MUL)
                                    if r == 1:
                                        ins.then_inc(roped.sem, roped.next((L, "k", b)))
                                        dve.wait_ge(roped.sem, roped.made)
                                    else:
                                        link(ins)
                    for u in range(5):
                        dve.wait_ge(act_read.sem, act_read.at((L, "gate", u)))
                    attend((L, "m"), MEM_HEADS, mem_out)

                    def head_out(i):
                        if i % 4 == 3:
                            gated(L, i // 4, (L, "ao", i // 4), bank[4 + (i // 4) % 3][:, :])
                    attend((L, "h"), HEADS, head_out)
                else:
                    for u in range(5):
                        dve.wait_ge(act_read.sem, act_read.at((L, "gate", u)))
                    attend((L, "m"), MEM_HEADS, mem_out)
                    cos_t = K("line_cos").rearrange("p (b d) -> p b d", b=NB)
                    sin_t = K("line_sin").rearrange("p (b d) -> p b d", b=NB)
                    mask = K("dilated_mask").rearrange("p (b k) -> p b k", b=NB)
                    for half in range(2):
                        chunks = [(s, g) for g in range(3) for s in range(2)]
                        for n, (s, g) in enumerate(chunks):
                            for b in range(NB):
                                dve.wait_ge(product_done.sem, product_done.at((L, half, "p", s, g, b)))
                                if (half, n) > (0, 0):
                                    ph, pn = (half, n - 1) if n else (0, 5)
                                    dve.wait_ge(product_done.sem, product_done.at((L, ph, "xt", *chunks[pn], 1)))
                                src = bank[2 * (n % 2) + b][:, :]
                                s4 = src.rearrange("p (h r e) -> p h r e", r=2, e=32)
                                s3 = src.rearrange("p (h d) -> p h d", d=DH)
                                dst = c_rot[:, b, :]
                                d4 = dst.rearrange("p (h r e) -> p h r e", r=2, e=32)
                                c3 = c_tmp.rearrange("p (h e) -> p h e", e=32)
                                tt(dst.rearrange("p (h d) -> p h d", d=DH), s3, cos_t[:, b, :].unsqueeze(1).to_broadcast([P, 8, DH]), MUL)
                                for r in range(2):
                                    sr = sin_t[:, b, r * 32:(r + 1) * 32].unsqueeze(1).to_broadcast([P, 8, 32])
                                    ins = v.tensor_tensor(c3, s4[:, :, 1 - r, :], sr, MUL)
                                    if r:
                                        ins.then_inc(dve_read.sem, dve_read.next((L, half, "p", s, g, b)))
                                        dve.wait_ge(dve_read.sem, dve_read.made)
                                    else:
                                        link(ins)
                                    ins = v.tensor_tensor(d4[:, :, r, :], d4[:, :, r, :], c3, ADD)
                                    if r:
                                        ins.then_inc(roped.sem, roped.next((L, half, s, g, b)))
                                        dve.wait_ge(roped.sem, roped.made)
                                    else:
                                        link(ins)
                        for what, i in attention_order(16, "tsv"):
                            if what == "s":
                                dve.wait_ge(product_done.sem, product_done.at((L, half, "s", i)))
                                if i >= 2:
                                    dve.wait_ge(exp_done.sem, exp_done.at((L, half, i - 2)))
                                v.tensor_tensor_reduce(out=masked[:, i % 2, :], in0=bank[i % 2][:, :], in1=mask[:, i % 2, :], scale=-1.0,
                                                          scalar=BIG, op0=ADD, op1=ALU.min, accum_out=S_(16 + 4 * (i % 3), 1)).then_inc(dve_read.sem, dve_read.next((L, half, "s", i)))
                                dve.wait_ge(dve_read.sem, dve_read.made)
                            elif what == "t":
                                dve.wait_ge(exp_done.sem, exp_done.at((L, half, i)))
                                r = normalise(i, range(1))
                                p_ = prob[:, i % 3, :]
                                v.tensor_scalar(p_, p_, r, None, MUL).then_inc(probs_normal.sem, probs_normal.next((L, half, i)))
                                dve.wait_ge(probs_normal.sem, probs_normal.made)
                            elif i % 8 == 7:
                                gated(L, 2 * half + i // 8, (L, half, "ao", i // 8), bank[6 + i // 8][:, :])
                for n in range(2):
                    for b in range(NB):
                        dve.wait_ge(product_done.sem, product_done.at((L, "wo", n, b)))
                        link(v.bn_stats(S_(128 + 12 * b + 6 * n, 6), bank[2 * n + b][:, :]))
                        if n == 1:
                            row_norm(L, b)
                normal_half(L, bank[1][:, :])
                split_hidden(L, LAYER_NAMES[li + 1], 4, *ln_cols(li + 1), natural=li == 3)

            def add_rows(key, n, b, o):
                dve.wait_ge(product_done.sem, product_done.at(key))
                xx = x[:, b, n * 512:(n + 1) * 512]
                v.tensor_tensor(xx, xx, o[:, :], ADD).then_inc(dve_read.sem, dve_read.next(key))

            def rms(L, key, b):
                a = S_(4 + b, 1)
                dve.wait_ge(square_sum.sem, square_sum.at((L, key, b, 0)))
                ts(a, S_(2 * b, 1), 1e-6 * D, None, ADD)
                dve.wait_ge(square_sum.sem, square_sum.at((L, key, b, 1)))
                ts(a, a, S_(2 * b + 1, 1), 2.0 ** 26 / D, ADD, MUL)
                rsqrt_col(S_(8 + b, 1), a, S_(6 + b, 1)).then_inc(row_stats.sem, row_stats.next(((L, key), b)))

            def rms_rows(L, key, gain):
                dve.wait_ge(row_stats.sem, row_stats.at(((L, key), 1)))
                v.tensor_scalar(z[:, 1, 0:512], x[:, 1, 0:512], S_(9, 1), None, MUL).then_inc(rows_normal_v.sem, rows_normal_v.next((L, key)))
                split_hidden((L, key), (L, key), 4, gain, None)

            dve.wait_ge(a_exp.sem, a_exp.at(0))
            ts(row[:, 652:664], row[:, 652:664], -1.0, None, MUL)
            for l in range(2):
                L = f"d{l}"
                if l == 0:
                    for b in range(NB):
                        rms(L, "mix", b)
                rms_rows(L, "mix", col("mix", l))
                link(v.memset(xbcT[:, :, 0:3], 0.0))
                for nm in ("cq", "ck"):
                    for b in range(NB):
                        dve.wait_ge(square_sum.sem, square_sum.at((L, nm, b)))
                ts(S_(104, 2), S_(44, 2), 1.0 / Q_RANK, 1e-6, MUL, ADD)
                ts(S_(106, 2), S_(46, 2), 1.0 / KV_RANK, 1e-6, MUL, ADD)
                rsqrt(S_(108, 4), S_(104, 4), S_(112, 4))
                for i, (nm, a, c0, n) in enumerate((("cq", cqt, SSD_H, Q_RANK), ("ck", ckt, 0, KV_RANK))):
                    for b in range(NB):
                        v.tensor_scalar(a[:, b, c0:c0 + n], a[:, b, c0:c0 + n], S_(108 + 2 * i + b, 1), None, MUL).then_inc(latent_normal.sem, latent_normal.next((L, nm, b)))
                        dve.wait_ge(latent_normal.sem, latent_normal.made)
                val, low = S_(256, 12), S_(76, 12)
                tt(val.rearrange("p (b h) -> p b h", b=NB), cqt[:, :, 0:SSD_H], dt_bias[:, l, :].unsqueeze(1).to_broadcast([P, NB, SSD_H]), ADD)
                v.scalar_tensor_tensor(low, val, -1.0, val, MUL, ALU.min).then_inc(steps_in.sem, steps_in.next((L, "e")))
                dve.wait_ge(steps_in.sem, steps_in.made)
                kr, kt_, ku = S_(320, 64), S_(384, 64), ckt[:, :, KV_RANK:KVR]
                cos_m = K("mla_cos").rearrange("p (b d) -> p b d", b=NB)
                sin_m = K("mla_sin").rearrange("p (b d) -> p b d", b=NB)
                kr3, kt3 = kr.rearrange("p (b d) -> p b d", b=NB), kt_.rearrange("p (b d) -> p b d", b=NB)
                tt(kr3, ku, cos_m, MUL)
                for r in range(2):
                    tt(kt3[:, :, 16 * r:16 * r + 16], ku[:, :, 16 - 16 * r:32 - 16 * r], sin_m[:, :, 16 * r:16 * r + 16], MUL)
                tt(kr, kr, kt_, ADD)
                gains = [col("cq", l)[:, k:k + 1] for k in range(3)] + [col("ckv", l)[:, k:k + 1] for k in range(2)]
                for t in range(3):
                    dve.wait_ge(product_done.sem, product_done.at((L, "lt", t)))
                    m_n = 2 if t < 2 else 1
                    for m in range(m_n):
                        ins = v.tensor_scalar(split_t[:, 0, m * S:(m + 1) * S], bank[4 + t % 2][:, m * S:(m + 1) * S], gains[2 * t + m], None, MUL)
                        if m == m_n - 1:
                            ins.then_inc(dve_read.sem, dve_read.next((L, "lt", t)))
                            dve.wait_ge(dve_read.sem, dve_read.made)
                        else:
                            link(ins)
                    split(flat2(r_hi[:, 5 + 2 * t:5 + 2 * t + m_n, :]), flat2(r_lo[:, 5 + 2 * t:5 + 2 * t + m_n, :]), split_t[:, 0, 0:m_n * S]).then_inc(r_ready.sem, r_ready.next((L, "lt", t)))
                    dve.wait_ge(r_ready.sem, r_ready.made)
                cw, cb = col("conv_w", l), col("conv_b", l)
                for t in range(5):
                    dve.wait_ge(act_read.sem, act_read.at((L, "xbc", t // 2)))
                    ts(conv[:, t, :], xbcT[:, t, 3:3 + S], cw[:, 15 + t:16 + t], cb[:, t:t + 1], MUL, ADD)
                    for k in range(3):
                        ins = v.scalar_tensor_tensor(conv[:, t, :], xbcT[:, t, k:k + S], cw[:, 5 * k + t:5 * k + t + 1], conv[:, t, :], MUL, ADD)
                        if (t, k) == (4, 2):
                            ins.then_inc(conv_done.sem, conv_done.next(L))
                            dve.wait_ge(conv_done.sem, conv_done.made)
                        else:
                            link(ins)
                dve.wait_ge(product_done.sem, product_done.at((L, "wst")))
                v.tensor_tensor(wsT, bank[7][:, :].rearrange("p (h t) -> p h t", h=4), K("upto").unsqueeze(1).to_broadcast([P, 4, P]), MUL).then_inc(dve_read.sem, dve_read.next((L, "wst")))
                dve.wait_ge(dve_read.sem, dve_read.made)
                for b in range(NB):
                    dve.wait_ge(square_sum.sem, square_sum.at((L, "uv", b)))
                ts(S_(268, 2), S_(48, 2), 1.0 / 256, 1e-6, MUL, ADD)
                rsqrt(S_(270, 2), S_(268, 2), S_(272, 2))
                for b in range(NB):
                    vv = uv[:, b, 256:512]
                    ins = v.scalar_tensor_tensor(vv, vv, S_(270 + b, 1), gv[:, l, :], MUL, MUL)
                    if b == 1:
                        ins.then_inc(gmlp_ready.sem, gmlp_ready.next((L, "v")))
                        dve.wait_ge(gmlp_ready.sem, gmlp_ready.made)
                    else:
                        link(ins)
                dve.wait_ge(exp_small.sem, exp_small.at((L, "e")))
                e, w1, w2, q = S_(88, 12), S_(276, 12), S_(288, 12), S_(300, 12)
                ts(w1, e, 2.0, None, ADD)
                link(v.reciprocal(w1, w1))
                tt(w1, w1, e, MUL)
                tt(w2, w1, w1, MUL)
                ts(q, w2, 1.0 / 17, None, MUL)
                for n in (15, 13, 11, 9, 7, 5, 3):
                    stt(q, q, 1.0 / n, w2, ADD, MUL)
                stt(q, q, 1.0, w1, ADD, MUL)
                dt = S_(52 + 400, 12)
                ts(val, val, 0.0, None, ALU.max)
                stt(dt, q, 2.0, val, MUL, ADD)
                v.tensor_tensor(S_(64, 12).rearrange("p (b h) -> p b h", b=NB), dt.rearrange("p (b h) -> p b h", b=NB), a_neg[:, l, :].unsqueeze(1).to_broadcast([P, NB, SSD_H]), MUL).then_inc(steps_ready.sem, steps_ready.next((L, "dtA")))
                dve.wait_ge(steps_ready.sem, steps_ready.made)
                for n in range(2):
                    for b in range(NB):
                        dve.wait_ge(act_read.sem, act_read.at((L, "qb", n, b)))
                rot = split_t[:, 0, 0:384].rearrange("p (b h d) -> p b h d", b=NB, h=M_H)
                for b in range(NB):
                    qr = qtok[:, b, :].rearrange("p (h d) -> p h d", h=M_H)[:, :, DH:M_QK]
                    for r in range(2):
                        tt(rot[:, b, :, 16 * r:16 * r + 16], qr[:, :, 16 - 16 * r:32 - 16 * r],
                           sin_m[:, b, 16 * r:16 * r + 16].unsqueeze(1).to_broadcast([P, M_H, 16]), MUL)
                    tt(qr, qr, cos_m[:, b, :].unsqueeze(1).to_broadcast([P, M_H, M_ROPE]), MUL)
                    ins = v.tensor_tensor(qr, qr, rot[:, b, :, :], ADD)
                    if b == 1:
                        ins.then_inc(roped.sem, roped.next((L, "q")))
                        dve.wait_ge(roped.sem, roped.made)
                    else:
                        link(ins)
                for n in range(2):
                    for b in range(NB):
                        dve.wait_ge(act_read.sem, act_read.at((L, "kv", n, b)))
                for b in range(NB):
                    kk = ktok[:, b, :].rearrange("p (h d) -> p h d", h=M_H)
                    link(v.tensor_copy(kk[:, :, 0:DH], kvtok[:, b, :].rearrange("p (h d) -> p h d", h=M_H)[:, :, 0:DH]))
                    ins = v.tensor_copy(kk[:, :, DH:M_QK], kr3[:, b, :].unsqueeze(1).to_broadcast([P, M_H, M_ROPE]))
                    if b == 1:
                        ins.then_inc(roped.sem, roped.next((L, "k")))
                        dve.wait_ge(roped.sem, roped.made)
                    else:
                        link(ins)
                dve.wait_ge(product_done.sem, product_done.at((L, "gm")))
                og = bank[7][:, :].rearrange("p (h c d) -> p h c d", h=4, c=NB)
                for h in range(4):
                    uu = uv[:, :, h * DH:(h + 1) * DH]
                    ins = v.scalar_tensor_tensor(uu, og[:, h, :, :], col("bs", l)[:, h:h + 1], uu, ADD, MUL)
                    if h == 3:
                        ins.then_inc(dve_read.sem, dve_read.next((L, "gm")))
                        dve.wait_ge(dve_read.sem, dve_read.made)
                    else:
                        link(ins)
                dve.wait_ge(product_done.sem, product_done.at((L, "cum")))
                cum = S_(464, 24)
                v.tensor_copy(cum, bank[7][:, 0:24]).then_inc(dve_read.sem, dve_read.next((L, "cum")))
                dve.wait_ge(dve_read.sem, dve_read.made)
                tt(S_(124, 6), cum[:, 12:18], cum[:, 0:6], SUB)
                v.tensor_copy(S_(130, 6), cum[:, 6:12]).then_inc(steps_in.sem, steps_in.next((L, "end")))
                dve.wait_ge(steps_in.sem, steps_in.made)
                for c in range(NB):
                    for g in range(2):
                        dve.wait_ge(product_done.sem, product_done.at((L, "rc", c, g)))
                        for h in range(3):
                            i = c * SSD_H + 3 * g + h
                            bk = bank[[5, 6, 0, 1][2 * c + g]][:, h * P:(h + 1) * P]
                            ins = v.scalar_tensor_tensor(decay[:, i, :], bk, cum[:, i:i + 1], K("future_st"), SUB, ADD)
                            if h == 2:
                                ins.then_inc(dve_read.sem, dve_read.next((L, "rc", c, g)))
                                dve.wait_ge(dve_read.sem, dve_read.made)
                            else:
                                link(ins)
                dve.wait_ge(exp_small.sem, exp_small.at((L, "end")))
                tt(S_(490, 6), S_(136, 6), dt[:, 0:6], MUL)
                dve.wait_ge(act_read.sem, act_read.at((L, "xs", 0)))
                v.tensor_tensor(x_dec.rearrange("p (h d) -> p h d", h=SSD_H), xs[:, 0, :].rearrange("p (h d) -> p h d", h=SSD_H), S_(490, 6).unsqueeze(2).to_broadcast([P, SSD_H, DH]), MUL).then_inc(state_in.sem, state_in.next(L))
                dve.wait_ge(state_in.sem, state_in.made)
                for g in range(2):
                    dve.wait_ge(product_done.sem, product_done.at((L, "cb", g)))
                for c in range(NB):
                    for g in range(2):
                        dve.wait_ge(exp_seg.sem, exp_seg.at((L, c, g)))
                        for h in range(3):
                            i = c * SSD_H + 3 * g + h
                            ins = v.scalar_tensor_tensor(decay[:, i, :], decay[:, i, :], dt[:, i:i + 1], bank[3 + g][:, c * P:(c + 1) * P], MUL, MUL)
                            if h == 2:
                                ins.then_inc(decay_ready.sem, decay_ready.next((L, c, g)))
                                dve.wait_ge(decay_ready.sem, decay_ready.made)
                            else:
                                link(ins)
                for c in range(NB):
                    dve.wait_ge(act_read.sem, act_read.at((L, "xs", c)))
                    y3 = y_b[:, c, :].rearrange("p (h d) -> p h d", h=SSD_H)
                    tt(y3, xs[:, c, :].rearrange("p (h d) -> p h d", h=SSD_H), d_skip[:, l, :].unsqueeze(2).to_broadcast([P, SSD_H, DH]), MUL)
                t3 = split_t[:, 0, 0:SSD_W]
                for g in range(2):
                    dve.wait_ge(product_done.sem, product_done.at((L, "yo", g)))
                    v.tensor_tensor(t3[:, 192 * g:192 * g + 192].rearrange("p (h d) -> p h d", h=3), bank[[7, 1][g]][:, 0:192].rearrange("p (h d) -> p h d", h=3), S_(142 + 3 * g, 3).unsqueeze(2).to_broadcast([P, 3, DH]), MUL).then_inc(dve_read.sem, dve_read.next((L, "yo", g)))
                    dve.wait_ge(dve_read.sem, dve_read.made)
                tt(y_b[:, 1, :], y_b[:, 1, :], t3, ADD)
                for c in range(NB):
                    dve.wait_ge(product_done.sem, product_done.at((L, "yd", c)))
                    v.tensor_tensor(y_b[:, c, :], y_b[:, c, :], bank[5 + c][:, 0:SSD_W], ADD).then_inc(dve_read.sem, dve_read.next((L, "yd", c)))
                    dve.wait_ge(dve_read.sem, dve_read.made)
                for b in range(NB):
                    dve.wait_ge(act_read.sem, act_read.at((L, "z", b)))
                yf, zf = flat2(y_b), flat2(zg)
                tt(yf, yf, zf, MUL)
                sq = flat2(zg)
                tt(sq, yf, yf, MUL)
                y4 = yf.rearrange("p (g n) -> p g n", g=4)
                link(v.tensor_reduce(S_(496, 4), sq.rearrange("p (g n) -> p g n", g=4), AX.X, ALU.add))
                ts(S_(496, 4), S_(496, 4), 1.0 / 192, 1e-6, MUL, ADD)
                rsqrt(S_(500, 4), S_(496, 4), S_(504, 4))
                v.tensor_tensor(y4, y4, S_(500, 4).unsqueeze(2).to_broadcast([P, 4, 192]), MUL).then_inc(mixer_out.sem, mixer_out.next((L, "b")))
                dve.wait_ge(mixer_out.sem, mixer_out.made)
                dve.wait_ge(product_done.sem, product_done.at((L, "at")))
                t = split_t[:, 0, :]
                v.tensor_copy(t, bank[3][:, :]).then_inc(dve_read.sem, dve_read.next((L, "at")))
                dve.wait_ge(dve_read.sem, dve_read.made)
                split(flat2(r_hi[:, 0:2, :]), flat2(r_lo[:, 0:2, :]), t).then_inc(r_ready.sem, r_ready.next((L, "at")))
                dve.wait_ge(r_ready.sem, r_ready.made)
                for j, bk in ((0, 2), (1, 4)):
                    dve.wait_ge(product_done.sem, product_done.at((L, "bt", j)))
                    m_n = 2 - j
                    for m in range(m_n):
                        ins = v.tensor_scalar(t[:, m * S:(m + 1) * S], bank[bk][:, m * S:(m + 1) * S], col("ssd", l)[:, 2 * j + m:2 * j + m + 1], None, MUL)
                        if m == m_n - 1:
                            ins.then_inc(dve_read.sem, dve_read.next((L, "bt", j)))
                            dve.wait_ge(dve_read.sem, dve_read.made)
                        else:
                            link(ins)
                    split(flat2(r_hi[:, 2 + 2 * j:2 + 2 * j + m_n, :]), flat2(r_lo[:, 2 + 2 * j:2 + 2 * j + m_n, :]), t[:, 0:m_n * S]).then_inc(r_ready.sem, r_ready.next((L, "bt", j)))
                    dve.wait_ge(r_ready.sem, r_ready.made)
                for what, h in attention_order(M_H, "tsv"):
                    if what == "s":
                        dve.wait_ge(product_done.sem, product_done.at((L, "s", h)))
                        o = bank[h % 2]
                        for b, (c0, c1) in enumerate(((0, P), (P, P + S))):
                            if h >= 2:
                                dve.wait_ge(exp_done.sem, exp_done.at((L, h - 2, b)))
                            if h >= 3:
                                dve.wait_ge(exp_done.sem, exp_done.at((L, h - 3, b)))
                            ins = v.tensor_tensor_reduce(out=masked[:, h % 2, c0:c1], in0=o[:, c0:c1], in1=K("causal")[:, c0:c1] if b == 0 else K("causal")[:, P:P + S],
                                                      scale=-1.0, scalar=BIG, op0=ADD, op1=ALU.min, accum_out=S_(16 + 4 * (h % 3) + b, 1))
                            if b == 1:
                                ins.then_inc(dve_read.sem, dve_read.next((L, "s", h)))
                                dve.wait_ge(dve_read.sem, dve_read.made)
                            else:
                                ins.then_inc(row_max.sem, row_max.next((L, h)))
                                dve.wait_ge(row_max.sem, row_max.made)
                    elif what == "t":
                        for b in range(NB):
                            dve.wait_ge(exp_done.sem, exp_done.at((L, h, b)))
                        r = normalise(h, range(NB))
                        for b, (c0, c1) in enumerate(((0, P), (P, P + S))):
                            p_ = prob[:, h % 3, c0:c1]
                            ins = v.tensor_scalar(p_, p_, r[:, b:b + 1], None, MUL)
                            if b == 1:
                                ins.then_inc(probs_normal.sem, probs_normal.next((L, h)))
                                dve.wait_ge(probs_normal.sem, probs_normal.made)
                            else:
                                link(ins)
                    elif h in (3, 5):
                        j = h // 4
                        dve.wait_ge(product_done.sem, product_done.at((L, "co", j)))
                        m_n = 2 - j
                        v.tensor_copy(t[:, 0:m_n * S], bank[5 + j][:, 0:m_n * S]).then_inc(out_read.sem, out_read.next((L, "co", j)))
                        dve.wait_ge(out_read.sem, out_read.made)
                        split(flat2(r_hi[:, 5 + 2 * j:5 + 2 * j + m_n, :]), flat2(r_lo[:, 5 + 2 * j:5 + 2 * j + m_n, :]), t[:, 0:m_n * S]).then_inc(r_ready.sem, r_ready.next((L, "co", j)))
                        dve.wait_ge(r_ready.sem, r_ready.made)
                for n in range(2):
                    for b in range(NB):
                        add_rows((L, "wo", n, b), n, b, bank[2 * n + b])
                        if n == 1:
                            rms(L, "mlp", b)
                rms_rows(L, "mlp", col("mlp", l))
                for e in range(8):
                    for u in range(2):
                        dve.wait_ge(square_hi.sem, square_hi.at((L, "up", e, u)))
                        relu, f = masked[:, u, :], split_t[:, u, :]
                        tt(f, relu, relu, MUL)
                        t0 = 4 * (e % 2) + 2 * u
                        v.tensor_tensor(flat2(r_lo[:, t0:t0 + 2, :]), f, flat2(r_hi[:, t0:t0 + 2, :]).bitcast(F32), SUB).then_inc(r_ready.sem, r_ready.next((L, "up", e, u)))
                        dve.wait_ge(r_ready.sem, r_ready.made)
                for n in range(2):
                    for b in range(NB):
                        add_rows((L, "dn", n, b), n, b, bank[4 + 2 * n + b])
                        if n == 1 and l == 0:
                            rms("d1", "mix", b)
                        elif n == 1:
                            rms("end", "end", b)
                            if b == 0:
                                dve.wait_ge(gf_loaded, 16)
                            dve.wait_ge(row_stats.sem, row_stats.made)
                            v.scalar_tensor_tensor(z[:, b, :], x[:, b, :], S_(8 + b, 1), gf, MUL, MUL).then_inc(row_out.sem, row_out.next(b))

        for steps in every:
            assert steps.made == len(steps.order)


_INS = ["x", "mem", "ln_in_g", "ln_in_b", "w_mem_kv", "w_in_a", "w_in_b", "q_norm_g", "k_norm_g", "w_in_c", "w_out", "ln_g",
        "ln_b", "norm_mix_g_2", "w_in_2", "gmlp_v_norm_g_2", "gmlp_w_s_2", "gmlp_b_s_2", "ssd_conv_w_2", "ssd_conv_b_2",
        "ssd_dt_bias_2", "ssd_a_log_2", "ssd_d_2", "ssd_norm_g_2", "mla_q_norm_g_2", "mla_w_qb_2", "mla_kv_norm_g_2",
        "mla_w_kvb_2", "w_out_2", "norm_mlp_g_2", "mlp_w1_2", "mlp_w2_2", "final_norm_g_2"]


def kernel(**inputs):
    import concourse.bacc as bacc
    from concourse.bass_utils import run_bass_kernel_spmd

    nc = bacc.Bacc("TRN2", target_bir_lowering=False, num_devices=1)
    arrays, aps = {}, {}
    for name in _INS + ["const"]:
        a = constants()[0] if name == "const" else np.ascontiguousarray(inputs[name])
        arrays[f"in_{name}"] = a
        aps[name] = nc.dram_tensor(f"in_{name}", a.shape, mybir.dt.from_np(a.dtype), kind="ExternalInput").ap()
    out = nc.dram_tensor("out", (1, S, D), F32, kind="ExternalOutput").ap()
    build(nc, aps, out)
    return run_bass_kernel_spmd(nc, [arrays], core_ids=[0]).results[0]["out"]
```

```python
from contextlib import ExitStack

import numpy as np

import concourse.bass as bass
from concourse import mybir

F32 = mybir.dt.float32
F32R = mybir.dt.float32r
I32 = mybir.dt.int32
ACT = mybir.ActivationFunctionType
ALU = mybir.AluOpType
AX = mybir.AxisListType

P = 128
S = 256
NB = S // P
D = 1024
KT = D // P
DH = 64
N_MEM = 256
MASKED = -1e30
BIG = 3.0e38

MEM_HEADS = 4
MEM_W = MEM_HEADS * DH
INNER = D + MEM_W
YT = INNER // P
TAIL = INNER + MEM_W
HEADS = D // DH
KV_HEADS = HEADS // 4
ALPHA = 8.0 ** 0.25
GW = D // 4
DIL_W = 3 * D

UV = 512
SSD_H = 6
SSD_W = SSD_H * DH
XBC = SSD_W + 256
Q_RANK = 384
KV_RANK = 256
M_ROPE = 32
M_QK = 96
M_H = 6
D_FF = 4096
C_UV, C_Z, C_XBC = 0, UV, UV + SSD_W
C_DT = C_XBC + XBC
C_CKV = C_DT + SSD_H + Q_RANK
DTQ = SSD_H + Q_RANK
KVR = KV_RANK + M_ROPE

RAW_SLOTS = 3
SPLIT_SLOTS = 3
UNIT = 2048


def token_order():
    p = np.arange(S)
    return 16 * (p % 16) + 4 * (p // 16 % 4) + p // 64


CONST_AT = {}


def constants():
    t = token_order()
    parts = []

    def put(name, a):
        a = np.asarray(a, np.float64)
        if a.ndim == 2 and a.shape[0] == S:
            a = a.reshape(NB, P, -1).transpose(1, 0, 2).reshape(P, -1)
        CONST_AT[name] = (sum(x.shape[1] for x in parts), a.shape[1])
        parts.append(a)

    put("ident", np.eye(P))
    put("ones", np.ones((P, P)))
    i = np.arange(P)
    upto = (i[:, None] <= i[None, :]).astype(np.float64)
    put("upto", upto)
    put("future_st", (1 - upto) * MASKED)
    causal = (1 - upto.T) * MASKED
    put("causal", np.concatenate([causal, np.zeros((P, P)), causal], 1))
    a = 2 * np.pi * np.outer(t, t) / S
    put("dft_tok", np.concatenate([np.cos(a), -np.sin(a)], 1) / 16)

    def rope(pos, dim, base=10000.0):
        f = base ** (-(np.arange(0, dim, 2) / dim))
        a = (np.asarray(pos, np.float32)[:, None] * f.astype(np.float32)[None, :]).astype(np.float64)
        c, s = np.cos(a), np.sin(a)
        return np.concatenate([c, c], 1), np.concatenate([-s, s], 1)

    rc, rs = rope(t // 64, DH // 2)
    cc, cs = rope(t % 64, DH // 2)
    put("axial_cos", np.concatenate([rc, cc], 1))
    put("axial_sin", np.concatenate([rs, cs], 1))
    c, s = rope(t, DH)
    put("line_cos", c)
    put("line_sin", s)
    c, s = rope(np.arange(S), M_ROPE)
    put("mla_cos", c)
    put("mla_sin", s)
    mask = np.zeros((S, 512))
    for b in range(NB):
        q = t[b * P:(b + 1) * P, None]
        own = t[None, b * P:(b + 1) * P]
        mask[b * P:(b + 1) * P, 0:S] = np.abs(t[None, :] - q) > 64
        mask[b * P:(b + 1) * P, S:S + P] = (own - q) % 4 != 0
        mask[b * P:(b + 1) * P, S + P:] = (own - q) % 16 != 0
    put("dilated_mask", mask * MASKED)
    n_kept = sum(x.shape[1] for x in parts)
    j = np.arange(GW)
    a = 2 * np.pi * np.outer(j, j) / GW
    put("dft_ch", np.concatenate([np.cos(a), np.sin(a)], 1) / 16)
    put("residual", np.eye(P) * ALPHA)
    return np.ascontiguousarray(np.concatenate(parts, 1).astype(np.float32)), n_kept


def build(nc, A, out):
    _, n_kept = constants()
    with ExitStack() as ctx:
        def sb(name, shape, dt=F32):
            return ctx.enter_context(nc.sbuf_tensor(name, shape, dt))

        w_raw = sb("w_raw", [P, RAW_SLOTS, UNIT])
        w_hi = sb("w_hi", [P, SPLIT_SLOTS, UNIT], F32R)
        w_lo = sb("w_lo", [P, SPLIT_SLOTS, UNIT], F32R)
        h_hi = sb("h_hi", [P, KT, S], F32R)
        h_lo = sb("h_lo", [P, KT, S], F32R)
        r_hi = sb("r_hi", [P, YT, S], F32R)
        r_lo = sb("r_lo", [P, YT, S], F32R)
        const = sb("const", [P, n_kept])
        dft_hi = sb("dft_hi", [P, 2, 512], F32R)
        dft_lo = sb("dft_lo", [P, 2, 512], F32R)
        res_hi = sb("res_hi", [P, P], F32R)
        res_lo = sb("res_lo", [P, P], F32R)
        ident_r = sb("ident_r", [P, P], F32R)
        gate = sb("gate", [P, YT, S])
        mem_kv = sb("mem_kv", [P, 2, 512])
        mkT = mem_kv[:, 0, :].rearrange("p (a m) -> p a m", a=2)
        mv = mem_kv[:, 1, :].rearrange("p (b n) -> p b n", b=NB)
        N_COL_A, N_COL_B = 80, 106
        col_a = sb("col_a", [P, N_COL_A])
        col_b = sb("col_b", [P, N_COL_B])
        row = sb("row", [P, 2 * DH + 2 * 256 + 36])
        masked = sb("masked", [P, 2, 512])
        prob = sb("prob", [P, 3, 512])
        probT = sb("probT", [P, 2, 512])
        split_t = sb("split_t", [P, 2, 512])
        stat = sb("stat", [P, 512])
        ARENA = 9728
        arena = sb("arena", [P, ARENA])

        bank = [ctx.enter_context(nc.psum_tensor(f"bank{i}", [P, 512], F32)) for i in range(8)]

        def K(name):
            at, n = CONST_AT[name]
            return const[:, at:at + n]

        ident = K("ident")

        class Steps:

            def __init__(self, name):
                self.sem = ctx.enter_context(nc.semaphore(name))
                self.order, self.made, self.unit = {}, 0, {}
                every.append(self)

            def at(self, key):
                return self.order.setdefault(key, len(self.order) + 1)

            def after(self, key):
                return self.sem, self.at(key)

            def next(self, key):
                self.made += 1
                assert self.at(key) == self.made, (key, self.at(key), self.made)
                self.unit[key] = len(units) - 1
                return 1

        every = []
        product_done = Steps("product_done")
        act_read = Steps("act_read")
        dve_read = Steps("dve_read")
        state_read = Steps("state_read")
        gating_read = Steps("gating_read")
        out_read = Steps("out_read")
        w_rounded = Steps("w_rounded")
        w_split = Steps("w_split")
        tables_rounded = Steps("tables_rounded")
        tables_split = Steps("tables_split")
        a_exp = Steps("a_exp")
        row_stats = Steps("row_stats")
        rows_normal = Steps("rows_normal")
        rows_normal_v = Steps("rows_normal_v")
        h_rounded = Steps("h_rounded")
        h_ready = Steps("h_ready")
        r_ready = Steps("r_ready")
        gate_ready = Steps("gate_ready")
        gated_hi = Steps("gated_hi")
        row_max = Steps("row_max")
        exp_half = Steps("exp_half")
        exp_done = Steps("exp_done")
        probs_normal = Steps("probs_normal")
        roped = Steps("roped")
        square_sum = Steps("square_sum")
        square_hi = Steps("square_hi")
        latent_normal = Steps("latent_normal")
        xbc_ready = Steps("xbc_ready")
        conv_done = Steps("conv_done")
        gmlp_ready = Steps("gmlp_ready")
        steps_in = Steps("steps_in")
        exp_small = Steps("exp_small")
        steps_ready = Steps("steps_ready")
        exp_seg = Steps("exp_seg")
        decay_ready = Steps("decay_ready")
        split_hi = Steps("split_hi")
        z_gated = Steps("z_gated")
        state_in = Steps("state_in")
        mixer_out = Steps("mixer_out")
        row_out = Steps("row_out")
        vector_step = Steps("vector_step")
        w_loaded = [ctx.enter_context(nc.semaphore(f"w_loaded{i}")) for i in range(RAW_SLOTS)]
        ident_loaded = ctx.enter_context(nc.semaphore("ident_loaded"))
        consts_loaded = ctx.enter_context(nc.semaphore("consts_loaded"))
        x_loaded = ctx.enter_context(nc.semaphore("x_loaded"))
        mem_loaded = ctx.enter_context(nc.semaphore("mem_loaded"))
        rows_a_loaded = ctx.enter_context(nc.semaphore("rows_a_loaded"))
        rows_b_loaded = ctx.enter_context(nc.semaphore("rows_b_loaded"))
        ws_loaded = ctx.enter_context(nc.semaphore("ws_loaded"))
        gf_loaded = ctx.enter_context(nc.semaphore("gf_loaded"))
        stored = ctx.enter_context(nc.semaphore("stored"))

        units = []
        unit_done = {}
        down_done = {}
        left = {}

        def view(at, *shape):
            n = int(np.prod(shape))
            assert at + n <= ARENA, (at, shape)
            v = arena[:, at:at + n]
            if len(shape) == 1:
                return v
            names = "abcd"[:len(shape)]
            return v.rearrange(f"p ({' '.join(names)}) -> p {' '.join(names)}", **{k: s for k, s in zip(names, shape)})

        z = view(2048, NB, D)
        x_in = view(0, NB, D)
        mem_in = view(4096, NB, D)
        const_once = view(6144, 1024 + P)
        rows_a = arena[0:N_COL_A, 7300:7300 + P]
        rows_b = sb("rows_b", [N_COL_B, P])
        qmT = view(8000, 2, S)
        spectra = view(0, NB, 4, 512)
        qkv = view(0, NB, 1536)
        b_sq = view(3072, 1280)
        k_dup = view(4352, NB, KV_HEADS, 2, DH)
        b_rot = b_sq[:, 0:1024]
        gcos = view(5376, 2, NB, DH)
        gsin = view(5632, 2, NB, DH)
        bkT = view(5888, KV_HEADS, S)
        b_qmT = view(6912, 2, S)
        bqT = view(7424, 8, S)
        cqT = view(0, 3, 4, S)
        ckT = view(3072, 3, 4, S)
        cv = view(6144, NB, 3, 512)
        c_rot = prob[:, 0:2, :]
        c_tmp = split_t[:, 1, 0:256]
        c_qmT = view(9216, 2, S)
        x = view(0, NB, D)
        qtok = view(2048, NB, 576)
        zg = view(3200, NB, SSD_W)
        xbcT = view(4096, 5, S + 3)
        mqT = view(4096, M_H, S)
        xs = view(5632, NB, SSD_W)
        kvtok = view(6400, NB, 768)
        ktok = view(7936, NB, 576)
        cqt = view(7936, NB, DTQ)
        ckt = view(7936 + NB * DTQ, NB, KVR)
        mem_space = mem_kv[:, :, :].rearrange("p a b -> p (a b)")
        y_b = mem_space[:, 0:NB * SSD_W].rearrange("p (b n) -> p b n", b=NB)
        st_sb = mem_space[:, NB * SSD_W:NB * SSD_W + 192]
        tables_at = CONST_AT["dft_tok"][0]
        decay = const[:, tables_at:tables_at + NB * SSD_H * P].rearrange("p (i t) -> p i t", t=P)
        ws_raw = K("dilated_mask")[:, 0:512].rearrange("p (h s) -> p h s", h=4)
        wsT = K("dilated_mask")[:, 512:1024].rearrange("p (h t) -> p h t", h=4)
        b_tok = view(3968, P)
        x_dec = view(9292, SSD_W)
        assert CONST_AT["mla_cos"][0] == tables_at + NB * SSD_H * P
        uv = gate[:, 0:4, :].rearrange("p a b -> p (a b)").rearrange("p (b n) -> p b n", b=NB)
        mkvT = gate[:, 4:10, :]
        conv = prob[:, :, :].rearrange("p a b -> p (a b)")[:, 0:1280].rearrange("p (t s) -> p t s", t=5)
        gf = gate[:, 0:4, :].rearrange("p a b -> p (a b)")

        def S_(at, n):
            return stat[:, at:at + n]

        q_gain, k_gain = row[:, 0:DH], row[:, DH:2 * DH]
        gv = row[:, 2 * DH:2 * DH + 512].rearrange("p (l n) -> p l n", l=2)
        dt_bias = row[:, 640:652].rearrange("p (l h) -> p l h", l=2)
        a_neg = row[:, 652:664].rearrange("p (l h) -> p l h", l=2)
        d_skip = row[:, 664:676].rearrange("p (l h) -> p l h", l=2)

        def ln_cols(i):
            if i == 0:
                return col_a[:, 0:8], col_a[:, 8:16]
            return col_a[:, 16 + 8 * (i - 1):24 + 8 * (i - 1)], col_a[:, 48 + 8 * (i - 1):56 + 8 * (i - 1)]

        col_at, n_b = {}, 0
        for nm, n in (("mix", 8), ("mlp", 8), ("conv_w", 20), ("conv_b", 5), ("cq", 3), ("ckv", 2), ("ssd", 3), ("bs", 4)):
            col_at[nm] = (n_b, n)
            n_b += 2 * n
        assert n_b == N_COL_B

        def col(nm, l):
            at, n = col_at[nm]
            return col_b[:, at + l * n:at + (l + 1) * n]

        ROW_A_DMAS, ROW_B_DMAS = 4, 8 + 6

        LATENT_BANK, QB_BANK, RC_BANK, XS_BANK, Z_BANK = (7, 0, 1), (5, 6, 7, 0), (2, 3, 4, 5), (0, 6), (0, 6)
        KV_BANK, QT_BANK, KT_BANK, STATE_BANK, CB_BANK = (2, 3, 4, 5), (7, 2, 3), (4, 5, 7), (0, 6), 7
        GATING_BANK, HEAD_BANK = 1, (7, 1)
        block = ctx.enter_context(nc.Block())

        def rows_of(w, k0, kts, c0, n):
            return w[k0:k0 + kts * P, c0:c0 + n].rearrange("(k p) n -> p k n", p=P), kts, n

        LAYERS = [("a", 0), ("b", 0), ("c", 0), ("a", 1)]
        LAYER_NAMES = [f"{k}{j}" for k, j in LAYERS] + ["d"]
        BY_SCALAR = [(0, 0), (0, 1), (1, 1)]

        CHUNK_BANKS = [[2 * (n % 2), 2 * (n % 2) + 1] for n in range(8)] + [[6, 7]]
        HEADS_BEFORE, HEADS_AFTER = 2, 5

        def attention_order(n, steps="stv"):
            lag = {"s": 0, "t": 2, "v": 3}
            for i in range(n + 3):
                for what in steps:
                    if 0 <= i - lag[what] < n:
                        yield what, i - lag[what]

        memory_order, cuts = list(attention_order(MEM_HEADS)), (0, 2, 4, 7, 9, 11, 12)
        MEMORY_STEPS = [memory_order[c0:c1] for c0, c1 in zip(cuts[:-1], cuts[1:])]
        GATE_BANK = (4, 5, 6, 4, 5)

        @block.tensor
        def _(pe):
            def unit(source):
                u = len(units)
                units.append(source)
                pe.wait_ge(w_split.sem, w_split.at(u))
                slot, (_, kts, n) = u % SPLIT_SLOTS, source
                return u, [w[:, slot, 0:kts * n].rearrange("p (k n) -> p k n", k=kts) for w in (w_hi, w_lo)]

            def mm3(o, lhs, rhs, start, stop):
                nc.tensor.matmul(o, lhs[0], rhs[0], start=start, stop=False)
                nc.tensor.matmul(o, lhs[0], rhs[1], start=False, stop=False)
                return nc.tensor.matmul(o, lhs[1], rhs[0], start=False, stop=stop)

            def hT(k, b=None):
                cols = slice(0, S) if b is None else slice(b * P, (b + 1) * P)
                return h_hi[:, k, cols], h_lo[:, k, cols]

            def rT(k, b=None):
                cols = slice(0, S) if b is None else slice(b * P, (b + 1) * P)
                return r_hi[:, k, cols], r_lo[:, k, cols]

            def feature_major(key, b, source, act, reader=act_read, hidden=None):
                if b in left:
                    pe.wait_ge(*left[b])
                left[b] = reader.after(key)
                o = bank[b]
                u, w = unit(source)
                _, kts, n = source
                for m in range(n // P):
                    for k in range(kts):
                        if hidden is not None and m == 0 and k % 2 == 0:
                            pe.wait_ge(h_ready.sem, h_ready.at((hidden, k // 2)))
                        i = mm3(o[:, m * S:(m + 1) * S], [a[:, k, m * P:(m + 1) * P] for a in w], act(k),
                                k == 0, k == kts - 1)
                i.then_inc(product_done.sem, product_done.next(key))
                unit_done[u] = key

            def token_major(keys, banks, sources, act, reader=act_read, hidden=None, opened=True, closed=True):
                for b in range(NB):
                    if opened and banks[b] in left:
                        pe.wait_ge(*left[banks[b]])
                    left[banks[b]] = reader.after(keys[b])
                o = [bank[banks[b]] for b in range(NB)]
                k0 = 0
                for s, source in enumerate(sources):
                    u, w = unit(source)
                    _, kts, n = source
                    for b in range(NB):
                        last_unit = s == len(sources) - 1
                        for k in range(kts):
                            if hidden is not None and b == 0 and k % 2 == 0:
                                pe.wait_ge(h_ready.sem, h_ready.at((hidden, (k0 + k) // 2)))
                            i = mm3(o[b][:, 0:n], act(k0 + k, b), [a[:, k, :] for a in w],
                                    opened and s == 0 and k == 0, closed and last_unit and k == kts - 1)
                        if last_unit and closed:
                            i.then_inc(product_done.sem, product_done.next(keys[b]))
                        elif b == NB - 1:
                            i.then_inc(product_done.sem, product_done.next(("unit", u)))
                    unit_done[u] = keys[NB - 1] if last_unit and closed else ("unit", u)
                    k0 += kts

            def transposes(key, b, ins, reader, width=P):
                if b in left:
                    pe.wait_ge(*left[b])
                left[b] = reader.after(key)
                o = bank[b]
                for n, a in enumerate(ins):
                    i = nc.tensor.transpose(o[0:a.shape[1], n * width:n * width + P], a, ident)
                i.then_inc(product_done.sem, product_done.next(key))

            def hidden_from_rows(L, b0):
                for b in range(NB):
                    for j in range(4):
                        if b == 0:
                            pe.wait_ge(rows_normal.sem, rows_normal.at((L, 0, j // 2)))
                            if b0 + j in left:
                                pe.wait_ge(*left[b0 + j])
                            left[b0 + j] = dve_read.after((L, "zt", j))
                        elif j < 2:
                            pe.wait_ge(rows_normal_v.sem, rows_normal_v.at(L))
                        else:
                            pe.wait_ge(rows_normal.sem, rows_normal.at((L, 1, 1)))
                        for m in range(2):
                            k = 2 * j + m
                            i = nc.tensor.transpose(bank[b0 + j][:, m * S + b * P:m * S + (b + 1) * P], z[:, b, k * P:(k + 1) * P], ident)
                        if b == NB - 1:
                            i.then_inc(product_done.sem, product_done.next((L, "zt", j)))

            def attend(L, heads, steps, sb0, tb0, q_of, k_of, v_of, o_of):
                for what, i in steps:
                    h = heads[i]
                    if what == "s":
                        n_b = sb0 + i % 2
                        if n_b in left:
                            pe.wait_ge(*left[n_b])
                        left[n_b] = act_read.after((L, "s", h))
                        o = bank[n_b]
                        for b in range(NB):
                            m = nc.tensor.matmul(o[:, b * S:(b + 1) * S], q_of(h)[:, b * P:(b + 1) * P], k_of(h),
                                                 start=True, stop=True)
                        m.then_inc(product_done.sem, product_done.next((L, "s", h)))
                    elif what == "t":
                        pe.wait_ge(probs_normal.sem, probs_normal.at((L, h)))
                        pr = prob[:, i % 3, :]
                        transposes((L, "t", h), tb0 + i % 2,
                                   [pr[:, b * S + k * P:b * S + (k + 1) * P] for k in range(2) for b in range(NB)],
                                   act_read)
                    else:
                        pe.wait_ge(act_read.sem, act_read.at((L, "t", h)))
                        key, b, o, first, last = o_of(i, h)
                        if first:
                            if b in left:
                                pe.wait_ge(*left[b])
                            left[b] = out_read.after(key)
                        for k in range(2):
                            m = nc.tensor.matmul(o, v_of(h, k), probT[:, i % 2, k * S:(k + 1) * S],
                                                 start=k == 0, stop=k == 1)
                        m.then_inc(product_done.sem, product_done.next(key if last else (L, "o", h)))

            def memory_heads(L, qT_, steps):
                def o_of(i, h):
                    b = 7
                    return (L, "mo"), b, bank[b][64 * (h % 2):64 * (h % 2) + 64, (h // 2) * S:(h // 2 + 1) * S], i == 0, i == 3
                pe.wait_ge(act_read.sem, act_read.at((L, "qm")))
                attend((L, "m"), range(MEM_HEADS), steps, 0, 2,
                       lambda h: qT_[64 * (h % 2):64 * (h % 2) + 64, h // 2, :],
                       lambda h: mkT[64 * (h % 2):64 * (h % 2) + 64, h // 2, :],
                       lambda h, k: mv[:, k, h * DH:(h + 1) * DH], o_of)

            def gates(L, w, tail, hidden=None, qT_=None):
                feature_major((L, "qm"), 0, rows_of(w, 0, KT, tail + INNER, MEM_W), hT, hidden=hidden)
                for u in range(5):
                    feature_major((L, "gate", u), GATE_BANK[u], rows_of(w, 0, KT, tail + u * 256, 256), hT)
                    if qT_ is not None:
                        memory_heads(L, qT_, MEMORY_STEPS[u])

            def out_product(L, i):
                for n in range(2):
                    for b in range(NB):
                        if 2 * n + b in left:
                            pe.wait_ge(*left[2 * n + b])
                        if n == 0 and b == 1:
                            left[2 * n + b] = rows_normal_v.after(L)
                        else:
                            left[2 * n + b] = rows_normal.after((L, b, n))
                        for j in range(4):
                            mm3(bank[2 * n + b][:, j * P:(j + 1) * P], hT(4 * n + j, b), (res_hi[:], res_lo[:]), j == 0, False)
                    for k0, kts in ((8, 2), (0, 4), (4, 4)):
                        u, w = unit(rows_of(A["w_out"][i], k0 * P, kts, n * 512, 512))
                        for b in range(NB):
                            for k in range(kts):
                                if n == 0 and b == 0 and k % 2 == 0:
                                    pe.wait_ge(r_ready.sem, r_ready.at((L, (k0 + k) // 2)))
                                m = mm3(bank[2 * n + b][:, :], rT(k0 + k, b), [a[:, k, :] for a in w], False, k0 + k == 7)
                            if k0 == 4:
                                m.then_inc(product_done.sem, product_done.next((L, "wo", n, b)))
                            elif b == NB - 1:
                                m.then_inc(product_done.sem, product_done.next(("unit", u)))
                        unit_done[u] = (L, "wo", n, NB - 1) if k0 == 4 else ("unit", u)

            pe.wait_ge(ident_loaded, 16)
            pe.wait_ge(mem_loaded, 16)
            for j in range(4):
                transposes(("mem", "t", j), 4 + j,
                           [mem_in[:, b, k * P:(k + 1) * P] for k in (2 * j, 2 * j + 1) for b in range(NB)], r_ready)
            pe.wait_ge(rows_a_loaded, 16 * ROW_A_DMAS)
            left[0] = act_read.after(("cols", "a"))
            nc.tensor.transpose(bank[0][:, 0:N_COL_A], rows_a, ident[0:N_COL_A, 0:N_COL_A])\
                .then_inc(product_done.sem, product_done.next(("cols", "a")))
            for j in range(4):
                pe.wait_ge(r_ready.sem, r_ready.at(("mem", "t", j)))
            feature_major(("mem", "k"), 4, rows_of(A["w_mem_kv"], 0, KT, 0, MEM_W), rT)
            hidden_from_rows("in", 0)
            u, w = unit(rows_of(A["w_mem_kv"], 0, KT, MEM_W, MEM_W))
            if 5 in left:
                pe.wait_ge(*left[5])
            left[5] = act_read.after(("mem", "v"))
            o = bank[5]
            for b in range(NB):
                for k in range(KT):
                    i = mm3(o[:, b * MEM_W:(b + 1) * MEM_W], rT(k, b), [a[:, k, :] for a in w], k == 0, k == KT - 1)
            i.then_inc(product_done.sem, product_done.next(("mem", "v")))
            unit_done[u] = ("mem", "v")

            for li, (kind, j) in enumerate(LAYERS):
                L = f"{kind}{j}"
                if kind == "a":
                    w = A["w_in_a"][j]
                    gates(L, w, 0, hidden=L, qT_=qmT)
                    if j == 0:
                        pe.wait_ge(consts_loaded, 32)
                        pe.wait_ge(tables_split.sem, tables_split.at("lo"))
                    for g in range(4):
                        for b in range(NB):
                            n_b = 2 * (g % 3) + b
                            if n_b in left:
                                pe.wait_ge(*left[n_b])
                            left[n_b] = (act_read if b == 0 else dve_read).after((L, "f1", g, b))
                            o = bank[n_b]
                            for k in range(2):
                                i = mm3(o[:, :], hT(2 * g + k, b), (dft_hi[:, k, :], dft_lo[:, k, :]), k == 0, k == 1)
                            i.then_inc(product_done.sem, product_done.next((L, "f1", g, b)))
                        if g == 0:
                            memory_heads(L, qmT, MEMORY_STEPS[5])
                    dt = K("dft_tok").rearrange("p (b c) -> p b c", b=NB)
                    for t in range(4):
                        pe.wait_ge(act_read.sem, act_read.at((L, "f1", t, 0)))
                        pe.wait_ge(dve_read.sem, dve_read.at((L, "f1", t, 1)))
                        n_b = 2 * (t % 2)
                        if n_b in left:
                            pe.wait_ge(*left[n_b])
                        left[n_b] = out_read.after((L, "f2", t))
                        o = bank[n_b]
                        for c in range(2):
                            for part in range(2):
                                for b in range(NB):
                                    i = nc.tensor.matmul(
                                        o[:, c * S:(c + 1) * S], spectra[:, b, t, part * GW + c * P:part * GW + (c + 1) * P],
                                        dt[:, b, part * S:(part + 1) * S], start=part + b == 0, stop=part + b == 2)
                        i.then_inc(product_done.sem, product_done.next((L, "f2", t)))
                elif kind == "b":
                    w = A["w_in_b"][0]
                    for c in range(3):
                        token_major([(L, "p", c, b) for b in range(NB)], [2 * c, 2 * c + 1],
                                    [rows_of(w, kh * 512, 4, c * 512, 512) for kh in range(2)], hT, hidden=L if c == 0 else None)
                    gates(L, w, 1536)
                    for t in range(4):
                        for b in range(NB):
                            pe.wait_ge(roped.sem, roped.at((L, "q", b)))
                        transposes((L, "qt", t), 6 + t % 2,
                                   [qkv[:, b, m * P:(m + 1) * P] for m in (2 * t, 2 * t + 1) for b in range(NB)], act_read)
                    for t in range(2):
                        for b in range(NB):
                            pe.wait_ge(roped.sem, roped.at((L, "k", b)))
                        transposes((L, "kt", t), 6 + t % 2,
                                   [k_dup[:, b, m, :, :].rearrange("p a d -> p (a d)") for m in (2 * t, 2 * t + 1) for b in range(NB)],
                                   act_read)
                    memory_heads(L, b_qmT, attention_order(MEM_HEADS))
                    for t in range(4):
                        pe.wait_ge(act_read.sem, act_read.at((L, "qt", t)))
                    for t in range(2):
                        pe.wait_ge(act_read.sem, act_read.at((L, "kt", t)))

                    def o_of(i, h):
                        b = 4 + (i // 4) % 3
                        return (L, "ao", i // 4), b, bank[b][64 * (h % 2):64 * (h % 2) + 64, (i % 4 // 2) * S:(i % 4 // 2 + 1) * S], i % 4 == 0, i % 4 == 3
                    attend((L, "h"), range(HEADS), attention_order(HEADS), 0, 2,
                           lambda h: bqT[64 * (h % 2):64 * (h % 2) + 64, h // 2, :],
                           lambda h: bkT[64 * (h % 2):64 * (h % 2) + 64, h // 4, :],
                           lambda h, k: qkv[:, k, 1280 + (h // 4) * DH:1280 + (h // 4 + 1) * DH], o_of)
                else:
                    w = A["w_in_c"][0]
                    gates(L, w, 3 * DIL_W, hidden=L, qT_=c_qmT)
                    chunks = [(s, g) for g in range(3) for s in range(2)] + [(2, g) for g in range(3)]

                    def chunk(half, n):
                        s, g = chunks[n]
                        token_major([(L, half, "p", s, g, b) for b in range(NB)], CHUNK_BANKS[n],
                                    [rows_of(w, kh * 512, 4, s * DIL_W + g * D + half * 512, 512) for kh in range(2)],
                                    hT, reader=dve_read if s < 2 else act_read)

                    def turn(half, n):
                        s, g = chunks[n]
                        for t in range(2):
                            for b in range(NB):
                                pe.wait_ge(roped.sem, roped.at((L, half, s, g, b)))
                            transposes((L, half, "xt", s, g, t), 4 + t,
                                       [c_rot[:, b, m * P:(m + 1) * P] for m in (2 * t, 2 * t + 1) for b in range(NB)],
                                       act_read)

                    def dilated_heads(half, steps):
                        for what, i in steps:
                            h, b = i // 2, i % 2
                            at, pr = 64 * (h % 2), h // 2
                            qs = slice(b * P, (b + 1) * P)
                            if what == "s":
                                n_b = i % 2
                                if n_b in left:
                                    pe.wait_ge(*left[n_b])
                                left[n_b] = dve_read.after((L, half, "s", i))
                                o = bank[n_b]
                                for g, (c0, c1, ks) in enumerate(((0, S, slice(0, S)), (S, S + P, qs), (S + P, 512, qs))):
                                    m = nc.tensor.matmul(o[:, c0:c1], cqT[at:at + 64, g, pr, qs], ckT[at:at + 64, g, pr, ks],
                                                         start=True, stop=True)
                                m.then_inc(product_done.sem, product_done.next((L, half, "s", i)))
                            elif what == "t":
                                pe.wait_ge(probs_normal.sem, probs_normal.at((L, half, i)))
                                transposes((L, half, "t", i), 2 + i % 2, [prob[:, i % 3, k * P:(k + 1) * P] for k in range(4)], act_read)
                            else:
                                if i == 0:
                                    for g in range(3):
                                        for kb in range(NB):
                                            pe.wait_ge(act_read.sem, act_read.at((L, half, "p", 2, g, kb)))
                                pe.wait_ge(act_read.sem, act_read.at((L, half, "t", i)))
                                ob = 6 + (i // 8) % 2
                                key = (L, half, "ao", i // 8)
                                if i % 8 == 0:
                                    if ob in left:
                                        pe.wait_ge(*left[ob])
                                    left[ob] = out_read.after(key)
                                o = bank[ob][at:at + 64, (pr % 2) * S + b * P:(pr % 2) * S + (b + 1) * P]
                                for k, (g, kb) in enumerate(((0, 0), (0, 1), (1, b), (2, b))):
                                    m = nc.tensor.matmul(o, cv[:, kb, g, h * DH:(h + 1) * DH], probT[:, i % 2, k * P:(k + 1) * P],
                                                         start=k == 0, stop=k == 3)
                                m.then_inc(product_done.sem, product_done.next(key if i % 8 == 7 else (L, half, "o", i)))

                    order = list(attention_order(16))
                    chunk(0, 0)
                    memory_heads(L, c_qmT, MEMORY_STEPS[5])
                    for half in range(2):
                        for n in range(1, 8):
                            chunk(half, n)
                            if n <= 6:
                                turn(half, n - 1)
                        for g in range(3):
                            for s in range(2):
                                for t in range(2):
                                    pe.wait_ge(act_read.sem, act_read.at((L, half, "xt", s, g, t)))
                        dilated_heads(half, order[:HEADS_BEFORE])
                        chunk(half, 8)
                        dilated_heads(half, order[HEADS_BEFORE:-HEADS_AFTER])
                        if half == 0:
                            chunk(1, 0)
                        dilated_heads(half, order[-HEADS_AFTER:])
                out_product(L, li)
                hidden_from_rows(L, 4)

            pe.wait_ge(rows_b_loaded, 16 * ROW_B_DMAS)
            if 4 in left:
                pe.wait_ge(*left[4])
            left[4] = act_read.after(("cols", "b"))
            nc.tensor.transpose(bank[4][:, 0:N_COL_B], rows_b[:, :], ident[0:N_COL_B, 0:N_COL_B])\
                .then_inc(product_done.sem, product_done.next(("cols", "b")))
            for t in range(4):
                pe.wait_ge(h_ready.sem, h_ready.at(("d", t)))
            for b in range(NB):
                for n in range(2):
                    n_b = 2 * b + n
                    if n_b in left:
                        pe.wait_ge(*left[n_b])
                    left[n_b] = act_read.after(("x", b, n))
                    o = bank[n_b]
                    for t in range(4):
                        k = 4 * n + t
                        nc.tensor.matmul(o[:, t * P:(t + 1) * P], hT(k, b)[0], ident_r[:], start=True, stop=False)
                        i = nc.tensor.matmul(o[:, t * P:(t + 1) * P], hT(k, b)[1], ident_r[:], start=False, stop=True)
                    i.then_inc(product_done.sem, product_done.next(("x", b, n)))

            for l in range(2):
                L = f"d{l}"
                w = A["w_in_2"][l]
                hidden_from_rows((L, "mix"), 4)

                def proj(nm, banks, c0, n, hidden=None):
                    token_major([(L, nm, b) for b in range(NB)], banks, [rows_of(w, kh * 512, 4, c0, n) for kh in range(2)], hT, hidden=hidden)
                proj("cq", [0, 1], C_DT, DTQ, hidden=(L, "mix"))
                proj("ck", [2, 3], C_CKV, KVR)
                for u, n in enumerate((256, 256, 128)):
                    feature_major((L, "xbc", u), 4 + u, rows_of(w, 0, KT, C_XBC + u * 256, n), hT)
                tiles = [(cqt, SSD_H + k * P, "cq") for k in range(3)] + [(ckt, k * P, "ck") for k in range(2)]
                for t in range(3):
                    for nm in ("cq", "ck"):
                        for b in range(NB):
                            pe.wait_ge(latent_normal.sem, latent_normal.at((L, nm, b)))
                    transposes((L, "lt", t), LATENT_BANK[t],
                               [a[:, b, at:at + P] for a, at, _ in tiles[2 * t:2 * t + 2] for b in range(NB)], r_ready)
                proj("uv", [2, 3], C_UV, UV)
                pe.wait_ge(ws_loaded, 16 * (l + 1))
                transposes((L, "wst"), 4, [ws_raw[:, h, :] for h in range(4)], dve_read)
                u, wq = unit(rows_of(A["mla_w_qb_2"][l], 0, 3, 0, 576))
                for n in range(2):
                    for b in range(NB):
                        n_b = QB_BANK[2 * n + b]
                        if n_b in left:
                            pe.wait_ge(*left[n_b])
                        left[n_b] = act_read.after((L, "qb", n, b))
                        o = bank[n_b]
                        for k in range(3):
                            if n + b == 0 and k % 2 == 0:
                                pe.wait_ge(r_ready.sem, r_ready.at((L, "lt", k // 2)))
                            i = mm3(o[:, 0:288], rT(5 + k, b), [a[:, k, n * 288:(n + 1) * 288] for a in wq], k == 0, k == 2)
                        i.then_inc(product_done.sem, product_done.next((L, "qb", n, b)))
                unit_done[u] = (L, "qb", 1, 1)
                pe.wait_ge(steps_ready.sem, steps_ready.at((L, "dtA")))
                dtA = S_(64, 12)
                if 1 in left:
                    pe.wait_ge(*left[1])
                left[1] = dve_read.after((L, "cum"))
                o = bank[1]
                nc.tensor.matmul(o[:, 0:12], K("upto"), dtA, start=True, stop=True)
                nc.tensor.matmul(o[:, 12:24], K("ones"), dtA, start=True, stop=True).then_inc(product_done.sem, product_done.next((L, "cum")))
                for c in range(NB):
                    for g in range(2):
                        n_b = RC_BANK[2 * c + g]
                        if n_b in left:
                            pe.wait_ge(*left[n_b])
                        left[n_b] = dve_read.after((L, "rc", c, g))
                        o = bank[n_b]
                        for h in range(3):
                            at = 64 + c * SSD_H + 3 * g + h
                            i = nc.tensor.matmul(o[:, h * P:(h + 1) * P], stat[:, at:at + 1].to_broadcast([P, P]), K("upto"),
                                                 start=True, stop=True)
                        i.then_inc(product_done.sem, product_done.next((L, "rc", c, g)))
                pe.wait_ge(gmlp_ready.sem, gmlp_ready.at((L, "v")))
                pe.wait_ge(dve_read.sem, dve_read.at((L, "wst")))
                if 1 in left:
                    pe.wait_ge(*left[1])
                left[1] = gating_read.after((L, "gm"))
                v_half = uv[:, :, 256:512].rearrange("p c (h d) -> p h c d", h=4)
                ov = bank[1][:, :].rearrange("p (h c d) -> p h c d", h=4, c=NB)
                for h in range(4):
                    i = nc.tensor.matmul(ov[:, h, :, :], wsT[:, h, :], v_half[:, h, :, :], start=True, stop=True)
                i.then_inc(product_done.sem, product_done.next((L, "gm")))
                pe.wait_ge(xbc_ready.sem, xbc_ready.at(L))
                for c in range(NB):
                    transposes((L, "xs", c), XS_BANK[c], [xbcT[:, t, 3 + c * P:3 + (c + 1) * P] for t in range(4 if c == 0 else 3)], act_read)
                if CB_BANK in left:
                    pe.wait_ge(*left[CB_BANK])
                for g in range(2):
                    if g == 1:
                        pe.wait_ge(product_done.sem, product_done.at((L, "cb", 0)))
                    for c in range(NB):
                        i = nc.tensor.matmul(bank[CB_BANK][:, g * S + c * P:g * S + (c + 1) * P],
                                             xbcT[64 * g:64 * g + 64, 3, 3 + c * P:3 + (c + 1) * P],
                                             xbcT[64 * g:64 * g + 64, 4, 3 + c * P:3 + (c + 1) * P], start=True, stop=True)
                    i.then_inc(product_done.sem, product_done.next((L, "cb", g)))
                proj("z", Z_BANK, C_Z, SSD_W)
                pe.wait_ge(state_in.sem, state_in.at(L))
                if 1 in left:
                    pe.wait_ge(*left[1])
                left[1] = act_read.after((L, "st"))
                o = bank[1]
                for g in range(2):
                    i = nc.tensor.matmul(o[64 * g:64 * g + 64, 0:192], b_tok[:, 64 * g:64 * g + 64], x_dec[:, 192 * g:192 * g + 192],
                                         start=True, stop=True)
                i.then_inc(product_done.sem, product_done.next((L, "st")))
                u, wkv = unit(rows_of(A["mla_w_kvb_2"][l], 0, 2, 0, 768))
                pe.wait_ge(r_ready.sem, r_ready.at((L, "lt", 2)))
                for n in range(2):
                    for b in range(NB):
                        n_b = KV_BANK[2 * n + b]
                        if n_b in left:
                            pe.wait_ge(*left[n_b])
                        left[n_b] = act_read.after((L, "kv", n, b))
                        o = bank[n_b]
                        for k in range(2):
                            i = mm3(o[:, 0:384], rT(8 + k, b), [a[:, k, n * 384:(n + 1) * 384] for a in wkv], k == 0, k == 1)
                        i.then_inc(product_done.sem, product_done.next((L, "kv", n, b)))
                unit_done[u] = (L, "kv", 1, 1)
                for c in range(NB):
                    for g in range(2):
                        pe.wait_ge(decay_ready.sem, decay_ready.at((L, c, g)))
                    n_b = STATE_BANK[c]
                    if n_b in left:
                        pe.wait_ge(*left[n_b])
                    left[n_b] = state_read.after((L, "yd", c))
                    for h in range(SSD_H):
                        i = nc.tensor.matmul(bank[n_b][:, h * DH:(h + 1) * DH], decay[:, c * SSD_H + h, :], xs[:, c, h * DH:(h + 1) * DH],
                                             start=True, stop=True)
                    i.then_inc(product_done.sem, product_done.next((L, "yd", c)))
                pe.wait_ge(act_read.sem, act_read.at((L, "st")))
                for g in range(2):
                    left[1] = state_read.after((L, "yo", g))
                    if g == 1:
                        pe.wait_ge(product_done.sem, product_done.at((L, "yo", 0)))
                    i = nc.tensor.matmul(bank[1][:, 192 * g:192 * g + 192], xbcT[64 * g:64 * g + 64, 4, 3 + P:3 + S],
                                         st_sb[64 * g:64 * g + 64, :], start=True, stop=True)
                    i.then_inc(product_done.sem, product_done.next((L, "yo", g)))

                pe.wait_ge(roped.sem, roped.at((L, "q")))
                left[CB_BANK] = decay_ready.after((L, NB - 1, 1))
                for t in range(3):
                    transposes((L, "qt", t), QT_BANK[t], [qtok[:, b, h * M_QK:(h + 1) * M_QK] for h in (2 * t, 2 * t + 1) for b in range(NB)], act_read)
                pe.wait_ge(roped.sem, roped.at((L, "k")))
                for t in range(3):
                    transposes((L, "kt", t), KT_BANK[t], [ktok[:, b, h * M_QK:(h + 1) * M_QK] for h in (2 * t, 2 * t + 1) for b in range(NB)], act_read)
                pe.wait_ge(gating_read.sem, gating_read.at((L, "gm")))
                transposes((L, "at"), GATING_BANK, [uv[:, b, k * P:(k + 1) * P] for k in range(2) for b in range(NB)], r_ready)

                for t in range(3):
                    pe.wait_ge(act_read.sem, act_read.at((L, "qt", t)))
                    pe.wait_ge(act_read.sem, act_read.at((L, "kt", t)))
                for what, h in attention_order(M_H):
                    if what == "s":
                        n_b = 4 + h % 2
                        if n_b in left:
                            pe.wait_ge(*left[n_b])
                        left[n_b] = dve_read.after((L, "s", h))
                        o = bank[n_b]
                        for b in range(NB):
                            n = (b + 1) * P
                            m = nc.tensor.matmul(o[:, b * P:b * P + n], mqT[0:M_QK, h, b * P:(b + 1) * P], mkvT[0:M_QK, h, 0:n],
                                                 start=True, stop=True)
                        m.then_inc(product_done.sem, product_done.next((L, "s", h)))
                    elif what == "t":
                        pe.wait_ge(probs_normal.sem, probs_normal.at((L, h)))
                        transposes((L, "t", h), 2 + h % 2, [prob[:, h % 3, k * P:(k + 1) * P] for k in range(3)], act_read)
                    else:
                        pe.wait_ge(act_read.sem, act_read.at((L, "t", h)))
                        ob, key = HEAD_BANK[h // 4], (L, "co", h // 4)
                        if h % 4 == 0:
                            if ob in left:
                                pe.wait_ge(*left[ob])
                            left[ob] = out_read.after(key)
                        o = bank[ob][64 * (h % 2):64 * (h % 2) + 64, (h % 4 // 2) * S:(h % 4 // 2 + 1) * S]
                        vh = kvtok[:, :, h * P + DH:(h + 1) * P]
                        nc.tensor.matmul(o, vh[:, 0, :], probT[:, h % 2, 0:S], start=True, stop=False)
                        m = nc.tensor.matmul(o[:, P:S], vh[:, 1, :], probT[:, h % 2, S:S + P], start=False, stop=True)
                        m.then_inc(product_done.sem, product_done.next(key if h in (3, 5) else (L, "o", h)))
                    if (what, h) == ("v", 0):
                        pe.wait_ge(mixer_out.sem, mixer_out.at((L, "b")))
                        transposes((L, "bt", 0), STATE_BANK[0], [y_b[:, b, k * P:(k + 1) * P] for k in range(2) for b in range(NB)], r_ready)
                        transposes((L, "bt", 1), STATE_BANK[1], [y_b[:, b, 2 * P:3 * P] for b in range(NB)], r_ready)
                for key in ((L, "at"), (L, "bt", 0), (L, "bt", 1)):
                    pe.wait_ge(r_ready.sem, r_ready.at(key))
                for j in range(2):
                    pe.wait_ge(out_read.sem, out_read.at((L, "co", j)))
                for n in range(2):
                    token_major([(L, "wo", n, b) for b in range(NB)], [2 * n, 2 * n + 1],
                                [rows_of(A["w_out_2"][l], kh * 512, 4, n * 512, 512) for kh in range(2)], rT, reader=dve_read)
                hidden_from_rows((L, "mlp"), 4)

                def up(e):
                    for u in range(2):
                        feature_major((L, "up", e, u), (2 * e + u) % 4,
                                      rows_of(A["mlp_w1_2"][l], 0, KT, (2 * e + u) * 256, 256), hT,
                                      hidden=(L, "mlp") if e + u == 0 else None)

                def down(e):
                    for u in range(2):
                        pe.wait_ge(r_ready.sem, r_ready.at((L, "up", e, u)))
                    for n in range(2):
                        token_major([(L, "dn", n, b) for b in range(NB)], [4 + 2 * n, 5 + 2 * n],
                                    [rows_of(A["mlp_w2_2"][l], e * 512, 4, n * 512, 512)],
                                    lambda k, b: rT(4 * (e % 2) + k, b), reader=dve_read, opened=e == 0, closed=e == 7)
                    down_done[L, e] = unit_done[len(units) - 1]
                for e in range(9):
                    if e < 8:
                        up(e)
                    if e > 0:
                        down(e - 1)

        N_UNITS = len(units)

        @block.sync
        def _(sp):
            def load_unit(u):
                source, kts, n = units[u]
                sp.dma_start(w_raw[:, u % RAW_SLOTS, 0:kts * n].rearrange("p (k n) -> p k n", k=kts), source)\
                    .then_inc(w_loaded[u % RAW_SLOTS], 16)

            sp.dma_start(const[:, 0:P], A["const"][:, 0:P]).then_inc(ident_loaded, 16)
            load_unit(0)
            sp.dma_start(mem_in, A["mem"][0].rearrange("(b p) d -> p b d", p=P)).then_inc(mem_loaded, 16)
            xv = A["x"][0].rearrange("(c b a) d -> a b c d", a=4, b=4)
            for a in range(4):
                for b in range(4):
                    p0 = (a % 2) * 64 + b * 16
                    sp.dma_start(x_in[p0:p0 + 16, a // 2, :], xv[a, b]).then_inc(x_loaded, 16)
            load_unit(1)
            load_unit(2)
            sp.dma_start(const_once, A["const"][:, n_kept:]).then_inc(consts_loaded, 16)
            sp.dma_start(const[:, P:], A["const"][:, P:n_kept]).then_inc(consts_loaded, 16)
            at = 0
            for nm in ("norm_mix_g_2", "norm_mlp_g_2", "ssd_conv_w_2", "ssd_conv_b_2", "mla_q_norm_g_2", "mla_kv_norm_g_2",
                       "ssd_norm_g_2", "gmlp_b_s_2"):
                a = A[nm]
                flat = a.rearrange("l n -> (l n)") if len(a.shape) == 2 else a.rearrange("l k n -> (l k n)")
                n = flat.shape[0] // P
                sp.dma_start(rows_b[at:at + n, :], flat.rearrange("(k p) -> k p", p=P)).then_inc(rows_b_loaded, 16)
                at += n
            at = 0
            for nm in ("q_norm_g", "k_norm_g", "gmlp_v_norm_g_2", "ssd_dt_bias_2", "ssd_a_log_2", "ssd_d_2"):
                flat = A[nm].rearrange("l n -> (l n)")
                n = flat.shape[0]
                sp.dma_start(row[:, at:at + n], flat.partition_broadcast(P)).then_inc(rows_b_loaded, 16)
                at += n
            for u in range(RAW_SLOTS, N_UNITS):
                sp.wait_ge(w_split.sem, w_split.at(u - RAW_SLOTS))
                load_unit(u)
                for l, key in enumerate((("c0", "wo", 1, 1), ("d0", "wst"))):
                    if u == product_done.unit[key] + RAW_SLOTS + 1:
                        sp.wait_ge(product_done.sem, product_done.at(key))
                        sp.dma_start(ws_raw, A["gmlp_w_s_2"][l].rearrange("h t s -> t h s")).then_inc(ws_loaded, 16)
            sp.wait_ge(product_done.sem, product_done.at(("d1", "co", 1)))
            sp.dma_start(gf, A["final_norm_g_2"].partition_broadcast(P)).then_inc(gf_loaded, 16)
            for b in range(NB):
                sp.wait_ge(row_out.sem, row_out.at(b))
                sp.dma_start(out[0, b * P:(b + 1) * P, :], z[:, b, :]).then_inc(stored, 16)
            sp.wait_ge(stored, 16 * NB)

        @block.gpsimd
        def _(pool):
            at = 0
            for a in (A["ln_in_g"], A["ln_in_b"], A["ln_g"], A["ln_b"]):
                flat = a if len(a.shape) == 1 else a.rearrange("l n -> (l n)")
                n = flat.shape[0] // P
                pool.dma_start(rows_a[at:at + n, :], flat.rearrange("(k p) -> k p", p=P)).then_inc(rows_a_loaded, 16)
                at += n
            for u, (_, kts, n) in enumerate(units):
                pool.wait_ge(w_rounded.sem, w_rounded.at(u))
                s, m = u % SPLIT_SLOTS, kts * n
                nc.gpsimd.tensor_tensor(w_lo[:, s, 0:m], w_raw[:, u % RAW_SLOTS, 0:m], w_hi[:, s, 0:m].bitcast(F32),
                                               ALU.subtract).then_inc(w_split.sem, w_split.next(u))

        @block.scalar
        def _(act):
            def round_unit(u):
                _, kts, n = units[u]
                act.wait_ge(w_loaded[u % RAW_SLOTS], 16 * (u // RAW_SLOTS + 1))
                if u >= SPLIT_SLOTS:
                    act.wait_ge(product_done.sem, product_done.at(unit_done[u - SPLIT_SLOTS]))
                nc.scalar.activation(w_hi[:, u % SPLIT_SLOTS, 0:kts * n], w_raw[:, u % RAW_SLOTS, 0:kts * n], ACT.Copy).then_inc(w_rounded.sem, w_rounded.next(u))

            def round_weights(key, ahead=SPLIT_SLOTS):
                for u in range(w_rounded.made, min(N_UNITS, product_done.unit[key] + 1 + ahead)):
                    round_unit(u)

            def evac(key, dst, src, func=ACT.Copy, scale=1.0, bias=0.0):
                round_weights(key)
                act.wait_ge(product_done.sem, product_done.at(key))
                args = {} if func == ACT.Copy else {"bias": bias}
                nc.scalar.activation(dst, src, func, scale=scale, **args).then_inc(act_read.sem, act_read.next(key))

            def flat2(a):
                return a.rearrange("p a b -> p (a b)")

            def attend(L, steps):
                for what, i in steps:
                    if what == "s":
                        round_weights((L, "s", i))
                        act.wait_ge(product_done.sem, product_done.at((L, "s", i)))
                        if i >= 3:
                            act.wait_ge(product_done.sem, product_done.at((L, "t", i - 3)))
                        act.wait_ge(row_max.sem, row_max.at((L, i)))
                        o = bank[i % 2]
                        for b in range(NB):
                            ins = nc.scalar.activation(prob[:, i % 3, b * S:(b + 1) * S], o[:, b * S:(b + 1) * S], ACT.Exp,
                                                       bias=S_(16 + 4 * (i % 3) + b, 1), accum_out=S_(32 + 4 * (i % 3) + b, 1))
                            if b == 0:
                                ins.then_inc(exp_half.sem, exp_half.next((L, "s", i)))
                            else:
                                ins.then_inc(act_read.sem, act_read.next((L, "s", i)))
                    elif what == "t":
                        if i >= 2:
                            act.wait_ge(product_done.sem, product_done.at(out_key(L, i - 2)))
                        evac((L, "t", i), probT[:, i % 2, :], bank[2 + i % 2][:, :])

            def out_key(L, i):
                base, what = L
                if what == "m":
                    return (base, "mo") if i == 3 else (L, "o", i)
                return (base, "ao", i // 4) if i % 4 == 3 else (L, "o", i)

            def gates(L, dst):
                evac((L, "qm"), flat2(dst), bank[0][:, :], scale=0.125)
                for u in range(5):
                    evac((L, "gate", u), flat2(gate[:, 2 * u:2 * u + 2, :]), bank[GATE_BANK[u]][:, :], ACT.Silu)

            def gates_and_memory(L, dst):
                evac((L, "qm"), flat2(dst), bank[0][:, :], scale=0.125)
                for u in range(4):
                    evac((L, "gate", u), flat2(gate[:, 2 * u:2 * u + 2, :]), bank[GATE_BANK[u]][:, :])
                    attend((L, "m"), MEMORY_STEPS[u])
                act.wait_ge(act_read.sem, act_read.at((L, "gate", 3)))
                nc.scalar.activation(flat2(gate[:, 0:8, :]), flat2(gate[:, 0:8, :]), ACT.Silu).then_inc(gate_ready.sem, gate_ready.next(L))
                evac((L, "gate", 4), flat2(gate[:, 8:10, :]), bank[GATE_BANK[4]][:, :], ACT.Silu)
                attend((L, "m"), MEMORY_STEPS[4])

            def hidden_hi(L, nxt):
                for j in range(4):
                    act.wait_ge(dve_read.sem, dve_read.at((L, "zt", j)))
                    nc.scalar.activation(flat2(h_hi[:, 2 * j:2 * j + 2, :]), split_t[:, j % 2, :], ACT.Copy)\
                        .then_inc(h_rounded.sem, h_rounded.next((nxt, j)))

            round_unit(0)
            for j in range(4):
                act.wait_ge(product_done.sem, product_done.at(("mem", "t", j)))
                nc.scalar.activation(flat2(r_hi[:, 2 * j:2 * j + 2, :]), bank[4 + j][:, :], ACT.Copy).then_inc(split_hi.sem, split_hi.next(("mem", j)))
            round_unit(1)
            evac(("cols", "a"), col_a[:], bank[0][:, 0:N_COL_A])
            act.wait_ge(x_loaded, 256)
            for b, n in BY_SCALAR:
                act.wait_ge(row_stats.sem, row_stats.at(("in", b)))
                nc.scalar.activation(z[:, b, n * 512:(n + 1) * 512], x_in[:, b, n * 512:(n + 1) * 512], ACT.Identity,
                                     scale=S_(8 + b, 1), bias=S_(10 + b, 1)).then_inc(rows_normal.sem, rows_normal.next(("in", b, n)))
            hidden_hi("in", "a0")
            act.wait_ge(ident_loaded, 16)
            act.wait_ge(consts_loaded, 32)
            nc.scalar.activation(flat2(dft_hi[:, :, :]), const_once[:, 0:1024], ACT.Copy)
            nc.scalar.activation(ident_r[:], ident, ACT.Copy)
            nc.scalar.activation(res_hi[:], const_once[:, 1024:1024 + P], ACT.Copy).then_inc(tables_rounded.sem, tables_rounded.next(0))
            evac(("mem", "k"), flat2(mkT[:, :, :]), bank[4][:, :])
            evac(("mem", "v"), flat2(mv[:, :, :]), bank[5][:, :])

            for li, (kind, j) in enumerate(LAYERS):
                L = f"{kind}{j}"
                if kind == "a":
                    gates_and_memory(L, qmT)
                    for g in range(4):
                        evac((L, "f1", g, 0), spectra[:, 0, g, :], bank[2 * (g % 3)][:, :])
                elif kind == "b":
                    for c in range(3):
                        for b in range(NB):
                            round_weights((L, "p", c, b))
                            act.wait_ge(product_done.sem, product_done.at((L, "p", c, b)))
                            nc.scalar.activation(qkv[:, b, c * 512:(c + 1) * 512], bank[2 * c + b][:, :], ACT.Copy).then_inc(act_read.sem, act_read.next((L, "p", c, b)))
                    gates(L, b_qmT)
                    for t in range(4):
                        evac((L, "qt", t), flat2(bqT[:, 2 * t:2 * t + 2, :]), bank[6 + t % 2][:, :], scale=0.125)
                    for t in range(2):
                        evac((L, "kt", t), flat2(bkT[:, 2 * t:2 * t + 2, :]), bank[6 + t % 2][:, :])
                    attend((L, "m"), attention_order(MEM_HEADS))
                    attend((L, "h"), attention_order(HEADS))
                else:
                    gates_and_memory(L, c_qmT)
                    chunks = [(s, g) for g in range(3) for s in range(2)] + [(2, g) for g in range(3)]

                    def dilated_heads(half, steps):
                        for what, i in steps:
                            if what == "s":
                                round_weights((L, half, "s", i))
                                act.wait_ge(product_done.sem, product_done.at((L, half, "s", i)))
                                if i >= 3:
                                    act.wait_ge(product_done.sem, product_done.at((L, half, "t", i - 3)))
                                act.wait_ge(dve_read.sem, dve_read.at((L, half, "s", i)))
                                nc.scalar.activation(prob[:, i % 3, :], masked[:, i % 2, :], ACT.Exp, scale=-1.0,
                                                            bias=S_(16 + 4 * (i % 3), 1), accum_out=S_(32 + 4 * (i % 3), 1)).then_inc(exp_done.sem, exp_done.next((L, half, i)))
                            elif what == "t":
                                if i >= 2:
                                    act.wait_ge(product_done.sem, product_done.at((L, half, "o", i - 2) if (i - 2) % 8 != 7 else (L, half, "ao", (i - 2) // 8)))
                                evac((L, half, "t", i), probT[:, i % 2, :], bank[2 + i % 2][:, :])

                    order = list(attention_order(16))
                    for half in range(2):
                        for n, (s, g) in enumerate(chunks):
                            if n == 8:
                                dilated_heads(half, order[:HEADS_BEFORE])
                            if s == 2:
                                for b in range(NB):
                                    evac((L, half, "p", s, g, b), cv[:, b, g, :], bank[CHUNK_BANKS[n][b]][:, :])
                            if 1 <= n <= 6:
                                s, g = chunks[n - 1]
                                for t in range(2):
                                    evac((L, half, "xt", s, g, t), flat2((cqT if s == 0 else ckT)[:, g, 2 * t:2 * t + 2, :]),
                                         bank[4 + t][:, :], scale=0.125 if s == 0 else 1.0)
                        dilated_heads(half, order[HEADS_BEFORE:])
                round_weights((L, "wo", 1, 0), SPLIT_SLOTS - 1)
                for b, n in BY_SCALAR:
                    act.wait_ge(row_stats.sem, row_stats.at((L, b)))
                    nc.scalar.activation(z[:, b, n * 512:(n + 1) * 512], bank[2 * n + b][:, :], ACT.Identity,
                                         scale=S_(8 + b, 1), bias=S_(10 + b, 1)).then_inc(rows_normal.sem, rows_normal.next((L, b, n)))
                hidden_hi(L, LAYER_NAMES[li + 1])
                round_weights((L, "wo", 1, 1))

            def row_squares(squares, a, total, key):
                if square_sum.made:
                    act.wait_ge(square_sum.sem, square_sum.made)
                nc.scalar.activation(squares, a, ACT.Square, accum_out=total).then_inc(square_sum.sem, square_sum.next(key))

            def half_squares(L, key, b, n):
                cols = slice(n * 512, (n + 1) * 512)
                row_squares(z[:, b, cols], x[:, b, cols], S_(2 * b + n, 1), (L, key, b, n))

            def normal_rows(L):
                for b, n in BY_SCALAR:
                    act.wait_ge(row_stats.sem, row_stats.at((L, b)))
                    nc.scalar.activation(z[:, b, n * 512:(n + 1) * 512], x[:, b, n * 512:(n + 1) * 512], ACT.Identity,
                                         scale=S_(8 + b, 1)).then_inc(rows_normal.sem, rows_normal.next((L, b, n)))
                hidden_hi(L, L)

            evac(("cols", "b"), col_b[:], bank[4][:, 0:N_COL_B])
            act.wait_ge(rows_b_loaded, 16 * ROW_B_DMAS)
            nc.scalar.activation(row[:, 652:664], row[:, 652:664], ACT.Exp).then_inc(a_exp.sem, a_exp.next(0))
            for l in range(2):
                L = f"d{l}"
                if l == 0:
                    for b in range(NB):
                        for n in range(2):
                            evac(("x", b, n), x[:, b, n * 512:(n + 1) * 512], bank[2 * b + n][:, :])
                            act.wait_ge(act_read.sem, act_read.at(("x", b, n)))
                            half_squares(L, "mix", b, n)
                else:
                    round_weights(("d0", "dn", 1, 0), SPLIT_SLOTS - 1)
                    for n in range(2):
                        for b in range(NB):
                            act.wait_ge(dve_read.sem, dve_read.at(("d0", "dn", n, b)))
                            half_squares(L, "mix", b, n)
                normal_rows((L, "mix"))
                round_weights(("x", 1, 1) if l == 0 else ("d0", "dn", 1, 1))
                for b in range(NB):
                    evac((L, "cq", b), cqt[:, b, :], bank[b][:, 0:DTQ])
                for b in range(NB):
                    evac((L, "ck", b), ckt[:, b, :], bank[2 + b][:, 0:KVR])
                for nm, a, c0, n, s0 in (("cq", cqt, SSD_H, Q_RANK, 0), ("ck", ckt, 0, KV_RANK, 2)):
                    for b in range(NB):
                        act.wait_ge(act_read.sem, act_read.at((L, nm, b)))
                        row_squares(split_t[:, 1, 0:n], a[:, b, c0:c0 + n], S_(44 + s0 + b, 1), (L, nm, b))
                for u, n in enumerate((2, 2, 1)):
                    evac((L, "xbc", u), xbcT[:, 2 * u:2 * u + n, 3:3 + S], bank[4 + u][:, 0:n * S].rearrange("p (t s) -> p t s", t=n))
                act.wait_ge(steps_in.sem, steps_in.at((L, "e")))
                nc.scalar.activation(S_(88, 12), S_(76, 12), ACT.Exp).then_inc(exp_small.sem, exp_small.next((L, "e")))

                gains = [col("cq", l)[:, k:k + 1] for k in range(3)] + [col("ckv", l)[:, k:k + 1] for k in range(2)]
                for t in range(3):
                    act.wait_ge(product_done.sem, product_done.at((L, "lt", t)))
                    for m in range(2 if t < 2 else 1):
                        ins = nc.scalar.activation(r_hi[:, 5 + 2 * t + m, :], bank[LATENT_BANK[t]][:, m * S:(m + 1) * S], ACT.Identity,
                                                   scale=gains[2 * t + m])
                    ins.then_inc(split_hi.sem, split_hi.next((L, "lt", t)))
                for b in range(NB):
                    evac((L, "uv", b), uv[:, b, :], bank[2 + b][:, :], ACT.Gelu_apprx_tanh)
                for b in range(NB):
                    act.wait_ge(act_read.sem, act_read.at((L, "uv", b)))
                    row_squares(split_t[:, 1, 0:256], uv[:, b, 256:512], S_(48 + b, 1), (L, "uv", b))
                for n in range(2):
                    for b in range(NB):
                        evac((L, "qb", n, b), qtok[:, b, n * 288:(n + 1) * 288], bank[QB_BANK[2 * n + b]][:, 0:288])
                act.wait_ge(conv_done.sem, conv_done.at(L))
                nc.scalar.activation(xbcT[:, :, 3:3 + S], conv, ACT.Silu).then_inc(xbc_ready.sem, xbc_ready.next(L))
                round_weights((L, "xs", 0))
                act.wait_ge(product_done.sem, product_done.at((L, "xs", 0)))
                nc.scalar.activation(b_tok, bank[XS_BANK[0]][:, SSD_W:512], ACT.Copy)
                nc.scalar.activation(xs[:, 0, :], bank[XS_BANK[0]][:, 0:SSD_W], ACT.Copy).then_inc(act_read.sem, act_read.next((L, "xs", 0)))
                evac((L, "xs", 1), xs[:, 1, :], bank[XS_BANK[1]][:, 0:SSD_W])
                act.wait_ge(steps_in.sem, steps_in.at((L, "end")))
                nc.scalar.activation(S_(136, 12), S_(124, 12), ACT.Exp).then_inc(exp_small.sem, exp_small.next((L, "end")))
                for c in range(NB):
                    for g in range(2):
                        round_weights((L, "rc", c, g))
                        act.wait_ge(dve_read.sem, dve_read.at((L, "rc", c, g)))
                        d3 = decay[:, c * SSD_H + 3 * g:c * SSD_H + 3 * g + 3, :]
                        nc.scalar.activation(d3, d3, ACT.Exp).then_inc(exp_seg.sem, exp_seg.next((L, c, g)))
                for b in range(NB):
                    evac((L, "z", b), zg[:, b, :], bank[Z_BANK[b]][:, 0:SSD_W], ACT.Silu)
                evac((L, "st"), st_sb, bank[1][:, 0:192])
                for n in range(2):
                    for b in range(NB):
                        evac((L, "kv", n, b), kvtok[:, b, n * 384:(n + 1) * 384], bank[KV_BANK[2 * n + b]][:, 0:384])
                for t in range(3):
                    evac((L, "qt", t), flat2(mqT[0:M_QK, 2 * t:2 * t + 2, :]), bank[QT_BANK[t]][0:M_QK, :], scale=float(M_QK) ** -0.5)
                for t in range(3):
                    evac((L, "kt", t), flat2(mkvT[0:M_QK, 2 * t:2 * t + 2, :]), bank[KT_BANK[t]][0:M_QK, :])
                act.wait_ge(product_done.sem, product_done.at((L, "at")))
                nc.scalar.activation(flat2(r_hi[:, 0:2, :]), bank[GATING_BANK][:, :], ACT.Copy).then_inc(split_hi.sem, split_hi.next((L, "at")))
                act.wait_ge(z_gated.sem, z_gated.at(L))
                for g in range(4):
                    row_squares(split_t[:, 1, 0:192], flat2(y_b)[:, 192 * g:192 * g + 192], S_(496 + g, 1), (L, "y", g))
                for what, h in attention_order(M_H):
                    if what == "s":
                        round_weights((L, "s", h))
                        act.wait_ge(product_done.sem, product_done.at((L, "s", h)))
                        if h >= 3:
                            act.wait_ge(product_done.sem, product_done.at((L, "t", h - 3)))
                        for b, (c0, c1) in enumerate(((0, P), (P, P + S))):
                            if b == 0:
                                act.wait_ge(row_max.sem, row_max.at((L, h)))
                            else:
                                act.wait_ge(dve_read.sem, dve_read.at((L, "s", h)))
                            nc.scalar.activation(prob[:, h % 3, c0:c1], masked[:, h % 2, c0:c1], ACT.Exp, scale=-1.0,
                                                        bias=S_(16 + 4 * (h % 3) + b, 1), accum_out=S_(32 + 4 * (h % 3) + b, 1)).then_inc(exp_done.sem, exp_done.next((L, h, b)))
                    elif what == "t":
                        if h >= 2:
                            act.wait_ge(product_done.sem, product_done.at((L, "co", 0) if h - 2 == 3 else (L, "o", h - 2)))
                        evac((L, "t", h), probT[:, h % 2, 0:384], bank[2 + h % 2][:, 0:384])
                    elif h == 0:
                        act.wait_ge(product_done.sem, product_done.at((L, "bt", 0)))
                        for m in range(2):
                            ins = nc.scalar.activation(r_hi[:, 2 + m, :], bank[STATE_BANK[0]][:, m * S:(m + 1) * S], ACT.Identity, scale=col("ssd", l)[:, m:m + 1])
                        ins.then_inc(split_hi.sem, split_hi.next((L, "bt", 0)))
                        act.wait_ge(product_done.sem, product_done.at((L, "bt", 1)))
                        nc.scalar.activation(r_hi[:, 4, :], bank[STATE_BANK[1]][:, 0:S], ACT.Identity, scale=col("ssd", l)[:, 2:3]).then_inc(split_hi.sem, split_hi.next((L, "bt", 1)))
                    elif h == 3:
                        act.wait_ge(product_done.sem, product_done.at((L, "co", 0)))
                        nc.scalar.activation(flat2(r_hi[:, 5:7, :]), bank[HEAD_BANK[0]][:, :], ACT.Copy).then_inc(split_hi.sem, split_hi.next((L, "co", 0)))
                    elif h == 5:
                        act.wait_ge(product_done.sem, product_done.at((L, "co", 1)))
                        nc.scalar.activation(r_hi[:, 7, :], bank[HEAD_BANK[1]][:, 0:S], ACT.Copy).then_inc(split_hi.sem, split_hi.next((L, "co", 1)))
                round_weights((L, "wo", 1, 0), SPLIT_SLOTS - 1)
                for n in range(2):
                    for b in range(NB):
                        act.wait_ge(dve_read.sem, dve_read.at((L, "wo", n, b)))
                        half_squares(L, "mlp", b, n)
                normal_rows((L, "mlp"))
                round_weights((L, "wo", 1, 1))
                for e in range(8):
                    for u in range(2):
                        t = (2 * e + u) % 4
                        round_weights((L, "up", e, u))
                        act.wait_ge(product_done.sem, product_done.at((L, "up", e, u)))
                        if 2 * e + u >= 2:
                            act.wait_ge(r_ready.sem, r_ready.at((L, "up", (2 * e + u - 2) // 2, u)))
                        relu = masked[:, u, :]
                        nc.scalar.activation(relu, bank[t][:, :], ACT.Relu).then_inc(act_read.sem, act_read.next((L, "up", e, u)))
                        act.wait_ge(act_read.sem, act_read.at((L, "up", e, u)))
                        if e >= 2:
                            act.wait_ge(product_done.sem, product_done.at(down_done[L, e - 2]))
                        t0 = 4 * (e % 2) + 2 * u
                        nc.scalar.activation(flat2(r_hi[:, t0:t0 + 2, :]), relu, ACT.Square).then_inc(square_hi.sem, square_hi.next((L, "up", e, u)))
            round_weights(("d1", "dn", 1, 1))
            for n in range(2):
                for b in range(NB):
                    act.wait_ge(dve_read.sem, dve_read.at(("d1", "dn", n, b)))
                    half_squares("end", "end", b, n)

        @block.vector
        def _(dve):
            v = nc.vector

            def link(ins):
                ins.then_inc(vector_step.sem, vector_step.next(vector_step.made))
                dve.wait_ge(vector_step.sem, vector_step.made)

            def tt(o, a, b, op):
                link(v.tensor_tensor(o, a, b, op))

            def ts(o, a, s1, s2, op0, op1=ALU.bypass):
                link(v.tensor_scalar(o, a, s1, None, op0) if s2 is None else v.tensor_scalar(o, a, s1, s2, op0, op1))

            def stt(o, a, s, b, op0, op1):
                link(v.scalar_tensor_tensor(o, a, s, b, op0, op1))

            MUL, ADD, SUB = ALU.mult, ALU.add, ALU.subtract

            def rsqrt(y, a, t):
                ts(y.bitcast(I32), a.bitcast(I32), 1, None, ALU.logical_shift_right)
                ts(y.bitcast(I32), y.bitcast(I32), -1.0, float(0x5F3759DF), MUL, ADD)
                for n in range(3):
                    tt(t, y, y, MUL)
                    stt(t, a, -0.5, t, MUL, MUL)
                    stt(y, t, 1.5, y, ADD, MUL)

            def flat2(a):
                return a.rearrange("p a b -> p (a b)")

            def split(hi, lo, value):
                link(v.tensor_copy(hi, value))
                return v.tensor_tensor(lo, value, hi.bitcast(F32), SUB)

            def split_hidden(L, nxt, b0, gain, shift, natural=False):
                for j in range(5):
                    if j < 4:
                        dve.wait_ge(product_done.sem, product_done.at((L, "zt", j)))
                        if j >= 2:
                            dve.wait_ge(h_ready.sem, h_ready.at((nxt, j - 2)))
                        t = split_t[:, j % 2, :]
                        for m in range(2):
                            k = 2 * j + m
                            src, dst = bank[b0 + j][:, m * S:(m + 1) * S], t[:, m * S:(m + 1) * S]
                            if natural:
                                src = src.rearrange("p (a b c) -> p a b c", a=4, b=4)
                                dst = dst.rearrange("p (c b a) -> p a b c", a=4, b=4)
                            if shift is None:
                                ins = v.tensor_scalar(dst, src, gain[:, k:k + 1], None, MUL)
                            else:
                                ins = v.tensor_scalar(dst, src, gain[:, k:k + 1], shift[:, k:k + 1], MUL, ADD)
                        ins.then_inc(dve_read.sem, dve_read.next((L, "zt", j)))
                    if j > 0:
                        pair = slice(2 * j - 2, 2 * j)
                        dve.wait_ge(dve_read.sem, dve_read.at((L, "zt", j - 1)))
                        dve.wait_ge(h_rounded.sem, h_rounded.at((nxt, j - 1)))
                        v.tensor_tensor(flat2(h_lo[:, pair, :]), split_t[:, (j - 1) % 2, :], flat2(h_hi[:, pair, :]).bitcast(F32), SUB)\
                            .then_inc(h_ready.sem, h_ready.next((nxt, j - 1)))
                dve.wait_ge(h_ready.sem, h_ready.made)

            def rsqrt_col(y, a, t):
                ts(y.bitcast(I32), a.bitcast(I32), -0.5, float(0x5F3759DF - 2 ** 31), MUL, ADD)
                for three in (3.0, 12.0, 768.0):
                    stt(t, y, a, y, MUL, MUL)
                    if three < 768.0:
                        stt(y, t, three, y, SUB, MUL)
                return v.scalar_tensor_tensor(y, t, three, y, SUB, MUL)

            def row_norm(L, b):
                mean, var = S_(152 + 2 * b, 1), S_(153 + 2 * b, 1)
                link(v.bn_aggr(S_(152 + 2 * b, 2), S_(128 + 12 * b, 12)))
                ts(S_(4 + b, 1), var, 2.0 ** 26, 1e-5 * 2.0 ** 26, MUL, ADD)
                link(rsqrt_col(S_(8 + b, 1), S_(4 + b, 1), S_(6 + b, 1)))
                v.scalar_tensor_tensor(S_(10 + b, 1), mean, -1.0, S_(8 + b, 1), MUL, MUL).then_inc(row_stats.sem, row_stats.next((L, b)))

            def normal_half(L, src):
                v.tensor_scalar(z[:, 1, 0:512], src, S_(154, 1), S_(9, 1), SUB, MUL).then_inc(rows_normal_v.sem, rows_normal_v.next(L))

            def softmax_max(L, i, src, key):
                dve.wait_ge(product_done.sem, product_done.at(key))
                v.tensor_reduce(S_(16 + 4 * (i % 3), 2), src.rearrange("p (b k) -> p b k", b=NB), AX.X, ALU.max, negate=True).then_inc(row_max.sem, row_max.next((L, i)))

            def gated(L, j, key, src, parts=range(3)):
                t, pair = split_t[:, 0, :], slice(2 * j, 2 * j + 2)
                for part in parts:
                    if part == 0:
                        dve.wait_ge(product_done.sem, product_done.at(key))
                        v.tensor_tensor(t, src, flat2(gate[:, pair, :]), MUL).then_inc(out_read.sem, out_read.next(key))
                    elif part == 1:
                        dve.wait_ge(out_read.sem, out_read.at(key))
                        v.tensor_copy(flat2(r_hi[:, pair, :]), t).then_inc(gated_hi.sem, gated_hi.next((L, j)))
                    else:
                        dve.wait_ge(gated_hi.sem, gated_hi.at((L, j)))
                        v.tensor_tensor(flat2(r_lo[:, pair, :]), t, flat2(r_hi[:, pair, :]).bitcast(F32), SUB).then_inc(r_ready.sem, r_ready.next((L, j)))
                        dve.wait_ge(r_ready.sem, r_ready.made)

            def parts_after(i, n, last):
                if i == last:
                    return range(3)
                return [part for part in range(3) if i >= n - 1 + part and (i - part) % n == n - 1]

            def normalise(i, parts):
                n = len(parts)
                link(v.reciprocal(S_(52 + 2 * (i % 3), n), S_(32 + 4 * (i % 3), n)))
                return S_(52 + 2 * (i % 3), n)

            def attend(L, n, outs):
                for what, i in attention_order(n, "tsv"):
                    if what == "s":
                        softmax_max(L, i, bank[i % 2][:, :], (L, "s", i))
                    elif what == "t":
                        dve.wait_ge(act_read.sem, act_read.at((L, "s", i)))
                        r = normalise(i, range(NB))
                        for b in range(NB):
                            p_ = prob[:, i % 3, b * S:(b + 1) * S]
                            ins = v.tensor_scalar(p_, p_, r[:, b:b + 1], None, MUL)
                            if b == 1:
                                ins.then_inc(probs_normal.sem, probs_normal.next((L, i)))
                    else:
                        outs(i)

            for j in range(4):
                dve.wait_ge(split_hi.sem, split_hi.at(("mem", j)))
                v.tensor_tensor(flat2(r_lo[:, 2 * j:2 * j + 2, :]), bank[4 + j][:, :], flat2(r_hi[:, 2 * j:2 * j + 2, :]).bitcast(F32), SUB)\
                    .then_inc(r_ready.sem, r_ready.next(("mem", "t", j)))
            dve.wait_ge(x_loaded, 256)
            for b in range(NB):
                for n in range(2):
                    link(v.bn_stats(S_(128 + 12 * b + 6 * n, 6), x_in[:, b, n * 512:(n + 1) * 512]))
                row_norm("in", b)
            normal_half("in", x_in[:, 1, 0:512])
            dve.wait_ge(act_read.sem, act_read.at(("cols", "a")))
            split_hidden("in", "a0", 0, *ln_cols(0))
            dve.wait_ge(consts_loaded, 32)
            dve.wait_ge(tables_rounded.sem, tables_rounded.at(0))
            v.tensor_tensor(flat2(dft_lo[:, :, :]), const_once[:, 0:1024], flat2(dft_hi[:, :, :]).bitcast(F32), SUB)
            v.tensor_tensor(res_lo[:], const_once[:, 1024:1024 + P], res_hi[:].bitcast(F32), SUB).then_inc(tables_split.sem, tables_split.next("lo"))

            for li, (kind, j) in enumerate(LAYERS):
                L = f"{kind}{j}"

                def mem_out(i):
                    if i == 3:
                        if kind != "b":
                            dve.wait_ge(gate_ready.sem, gate_ready.at(L))
                        dve.wait_ge(act_read.sem, act_read.at((L, "gate", 4)))
                        gated(L, 4, (L, "mo"), bank[7][:, :])
                if kind == "a":
                    attend((L, "m"), MEM_HEADS, mem_out)
                    for g in range(4):
                        dve.wait_ge(product_done.sem, product_done.at((L, "f1", g, 1)))
                        v.tensor_copy(spectra[:, 1, g, :], bank[2 * (g % 3) + 1][:, :]).then_inc(dve_read.sem, dve_read.next((L, "f1", g, 1)))
                        dve.wait_ge(dve_read.sem, dve_read.made)
                    for t in range(4):
                        gated(L, t, (L, "f2", t), bank[2 * (t % 2)][:, :])
                elif kind == "b":
                    dve.wait_ge(rows_b_loaded, 16 * ROW_B_DMAS)
                    for n, g in enumerate((q_gain, k_gain)):
                        cos_t = K("axial_cos").rearrange("p (b d) -> p b d", b=NB)
                        sin_t = K("axial_sin").rearrange("p (b d) -> p b d", b=NB)
                        gb = g.unsqueeze(1).to_broadcast([P, NB, DH])
                        tt(gcos[:, n, :, :], cos_t, gb, MUL)
                        g4 = g.rearrange("p (h r e) -> p h r e", h=2, r=2)
                        for b in range(NB):
                            s4 = sin_t[:, b, :].rearrange("p (h r e) -> p h r e", h=2, r=2)
                            o4 = gsin[:, n, b, :].rearrange("p (h r e) -> p h r e", h=2, r=2)
                            for r in range(2):
                                tt(o4[:, :, r, :], s4[:, :, r, :], g4[:, :, 1 - r, :], MUL)
                    ssq = S_(160, 40)
                    for b in range(NB):
                        for c in range(3):
                            dve.wait_ge(act_read.sem, act_read.at((L, "p", c, b)))
                        tt(b_sq, qkv[:, b, 0:1280], qkv[:, b, 0:1280], MUL)
                        link(v.tensor_reduce(ssq[:, 20 * b:20 * b + 20], b_sq.rearrange("p (h d) -> p h d", d=DH), AX.X, ALU.add))
                    ts(ssq, ssq, 1.0 / DH, 1e-6, MUL, ADD)
                    rs = S_(200, 40)
                    rsqrt(rs, ssq, S_(240, 40))
                    for n, (c0, nh) in enumerate(((0, HEADS), (D, KV_HEADS))):
                        for b in range(NB):
                            src = qkv[:, b, c0:c0 + nh * DH]
                            rot = b_rot[:, 0:nh * DH]
                            s5 = src.rearrange("p (h f r e) -> p h f r e", f=2, r=2, e=16)
                            r5 = rot.rearrange("p (h f r e) -> p h f r e", f=2, r=2, e=16)
                            t5 = gsin[:, n, b, :].rearrange("p (f r e) -> p f r e", f=2, r=2)
                            for r in range(2):
                                for f in range(2):
                                    tt(r5[:, :, f, r, :], s5[:, :, f, 1 - r, :], t5[:, f, r, :].unsqueeze(1).to_broadcast([P, nh, 16]), MUL)
                            s3 = src.rearrange("p (h d) -> p h d", d=DH)
                            tt(s3, s3, gcos[:, n, b, :].unsqueeze(1).to_broadcast([P, nh, DH]), MUL)
                            tt(src, src, rot, ADD)
                            rb = rs[:, 20 * b + (0 if n == 0 else HEADS):20 * b + (HEADS if n == 0 else 20)]
                            if n == 0:
                                v.tensor_tensor(s3, s3, rb.unsqueeze(2).to_broadcast([P, nh, DH]), MUL).then_inc(roped.sem, roped.next((L, "q", b)))
                                dve.wait_ge(roped.sem, roped.made)
                            else:
                                for r in range(2):
                                    ins = v.tensor_tensor(k_dup[:, b, :, r, :], s3, rb.unsqueeze(2).to_broadcast([P, nh, DH]), MUL)
                                    if r == 1:
                                        ins.then_inc(roped.sem, roped.next((L, "k", b)))
                                        dve.wait_ge(roped.sem, roped.made)
                                    else:
                                        link(ins)
                    attend((L, "m"), MEM_HEADS, mem_out)

                    def head_out(i):
                        parts = parts_after(i, 4, HEADS - 1)
                        j = (i + 1) // 4 - 1
                        if parts:
                            gated(L, j, (L, "ao", j), bank[4 + j % 3][:, :], parts)
                    attend((L, "h"), HEADS, head_out)
                else:
                    attend((L, "m"), MEM_HEADS, mem_out)
                    cos_t = K("line_cos").rearrange("p (b d) -> p b d", b=NB)
                    sin_t = K("line_sin").rearrange("p (b d) -> p b d", b=NB)
                    mask = K("dilated_mask").rearrange("p (b k) -> p b k", b=NB)
                    for half in range(2):
                        chunks = [(s, g) for g in range(3) for s in range(2)]
                        for n, (s, g) in enumerate(chunks):
                            for b in range(NB):
                                dve.wait_ge(product_done.sem, product_done.at((L, half, "p", s, g, b)))
                                if (half, n) > (0, 0):
                                    ph, pn = (half, n - 1) if n else (0, 5)
                                    dve.wait_ge(product_done.sem, product_done.at((L, ph, "xt", *chunks[pn], 1)))
                                src = bank[CHUNK_BANKS[n][b]][:, :]
                                s4 = src.rearrange("p (h r e) -> p h r e", r=2, e=32)
                                s3 = src.rearrange("p (h d) -> p h d", d=DH)
                                dst = c_rot[:, b, :]
                                d4 = dst.rearrange("p (h r e) -> p h r e", r=2, e=32)
                                c3 = c_tmp.rearrange("p (h e) -> p h e", e=32)
                                tt(dst.rearrange("p (h d) -> p h d", d=DH), s3, cos_t[:, b, :].unsqueeze(1).to_broadcast([P, 8, DH]), MUL)
                                for r in range(2):
                                    sr = sin_t[:, b, r * 32:(r + 1) * 32].unsqueeze(1).to_broadcast([P, 8, 32])
                                    ins = v.tensor_tensor(c3, s4[:, :, 1 - r, :], sr, MUL)
                                    if r:
                                        ins.then_inc(dve_read.sem, dve_read.next((L, half, "p", s, g, b)))
                                        dve.wait_ge(dve_read.sem, dve_read.made)
                                    else:
                                        link(ins)
                                    ins = v.tensor_tensor(d4[:, :, r, :], d4[:, :, r, :], c3, ADD)
                                    if r:
                                        ins.then_inc(roped.sem, roped.next((L, half, s, g, b)))
                                        dve.wait_ge(roped.sem, roped.made)
                                    else:
                                        link(ins)
                        for what, i in attention_order(16, "tsv"):
                            if what == "s":
                                dve.wait_ge(product_done.sem, product_done.at((L, half, "s", i)))
                                if i >= 2:
                                    dve.wait_ge(exp_done.sem, exp_done.at((L, half, i - 2)))
                                v.tensor_tensor_reduce(out=masked[:, i % 2, :], in0=bank[i % 2][:, :], in1=mask[:, i % 2, :], scale=-1.0,
                                                          scalar=BIG, op0=ADD, op1=ALU.min, accum_out=S_(16 + 4 * (i % 3), 1)).then_inc(dve_read.sem, dve_read.next((L, half, "s", i)))
                            elif what == "t":
                                dve.wait_ge(exp_done.sem, exp_done.at((L, half, i)))
                                r = normalise(i, range(1))
                                p_ = prob[:, i % 3, :]
                                v.tensor_scalar(p_, p_, r, None, MUL).then_inc(probs_normal.sem, probs_normal.next((L, half, i)))
                            else:
                                parts = parts_after(i, 8, 15)
                                j = (i + 1) // 8 - 1
                                if parts:
                                    gated(L, 2 * half + j, (L, half, "ao", j), bank[6 + j][:, :], parts)
                for n in range(2):
                    for b in range(NB):
                        dve.wait_ge(product_done.sem, product_done.at((L, "wo", n, b)))
                        link(v.bn_stats(S_(128 + 12 * b + 6 * n, 6), bank[2 * n + b][:, :]))
                        if n == 1:
                            row_norm(L, b)
                normal_half(L, bank[1][:, :])
                split_hidden(L, LAYER_NAMES[li + 1], 4, *ln_cols(li + 1), natural=li == 3)

            def add_rows(key, n, b, o):
                dve.wait_ge(product_done.sem, product_done.at(key))
                xx = x[:, b, n * 512:(n + 1) * 512]
                v.tensor_tensor(xx, xx, o[:, :], ADD).then_inc(dve_read.sem, dve_read.next(key))

            def rms(L, key, b):
                a = S_(4 + b, 1)
                dve.wait_ge(square_sum.sem, square_sum.at((L, key, b, 0)))
                ts(a, S_(2 * b, 1), 1e-6 * D, None, ADD)
                dve.wait_ge(square_sum.sem, square_sum.at((L, key, b, 1)))
                ts(a, a, S_(2 * b + 1, 1), 2.0 ** 26 / D, ADD, MUL)
                rsqrt_col(S_(8 + b, 1), a, S_(6 + b, 1)).then_inc(row_stats.sem, row_stats.next(((L, key), b)))

            def rms_rows(L, key, gain):
                dve.wait_ge(row_stats.sem, row_stats.at(((L, key), 1)))
                v.tensor_scalar(z[:, 1, 0:512], x[:, 1, 0:512], S_(9, 1), None, MUL).then_inc(rows_normal_v.sem, rows_normal_v.next((L, key)))
                split_hidden((L, key), (L, key), 4, gain, None)

            dve.wait_ge(act_read.sem, act_read.at(("cols", "b")))
            dve.wait_ge(a_exp.sem, a_exp.at(0))
            ts(row[:, 652:664], row[:, 652:664], -1.0, None, MUL)
            for l in range(2):
                L = f"d{l}"
                if l == 0:
                    for b in range(NB):
                        rms(L, "mix", b)
                rms_rows(L, "mix", col("mix", l))
                link(v.memset(xbcT[:, :, 0:3], 0.0))
                for nm in ("cq", "ck"):
                    for b in range(NB):
                        dve.wait_ge(square_sum.sem, square_sum.at((L, nm, b)))
                ts(S_(104, 2), S_(44, 2), 1.0 / Q_RANK, 1e-6, MUL, ADD)
                ts(S_(106, 2), S_(46, 2), 1.0 / KV_RANK, 1e-6, MUL, ADD)
                rsqrt(S_(108, 4), S_(104, 4), S_(112, 4))
                for i, (nm, a, c0, n) in enumerate((("cq", cqt, SSD_H, Q_RANK), ("ck", ckt, 0, KV_RANK))):
                    for b in range(NB):
                        v.tensor_scalar(a[:, b, c0:c0 + n], a[:, b, c0:c0 + n], S_(108 + 2 * i + b, 1), None, MUL).then_inc(latent_normal.sem, latent_normal.next((L, nm, b)))
                        dve.wait_ge(latent_normal.sem, latent_normal.made)
                val, low = S_(256, 12), S_(76, 12)
                tt(val.rearrange("p (b h) -> p b h", b=NB), cqt[:, :, 0:SSD_H], dt_bias[:, l, :].unsqueeze(1).to_broadcast([P, NB, SSD_H]), ADD)
                v.scalar_tensor_tensor(low, val, -1.0, val, MUL, ALU.min).then_inc(steps_in.sem, steps_in.next((L, "e")))
                dve.wait_ge(steps_in.sem, steps_in.made)
                kr, kt_, ku = S_(320, 64), S_(384, 64), ckt[:, :, KV_RANK:KVR]
                cos_m = K("mla_cos").rearrange("p (b d) -> p b d", b=NB)
                sin_m = K("mla_sin").rearrange("p (b d) -> p b d", b=NB)
                kr3, kt3 = kr.rearrange("p (b d) -> p b d", b=NB), kt_.rearrange("p (b d) -> p b d", b=NB)
                tt(kr3, ku, cos_m, MUL)
                for r in range(2):
                    tt(kt3[:, :, 16 * r:16 * r + 16], ku[:, :, 16 - 16 * r:32 - 16 * r], sin_m[:, :, 16 * r:16 * r + 16], MUL)
                tt(kr, kr, kt_, ADD)
                cw, cb = col("conv_w", l), col("conv_b", l)

                def convolve(tiles):
                    for t in tiles:
                        dve.wait_ge(act_read.sem, act_read.at((L, "xbc", t // 2)))
                        ts(conv[:, t, :], xbcT[:, t, 3:3 + S], cw[:, 15 + t:16 + t], cb[:, t:t + 1], MUL, ADD)
                        for k in range(3):
                            ins = v.scalar_tensor_tensor(conv[:, t, :], xbcT[:, t, k:k + S], cw[:, 5 * k + t:5 * k + t + 1], conv[:, t, :], MUL, ADD)
                            if (t, k) == (4, 2):
                                ins.then_inc(conv_done.sem, conv_done.next(L))
                            else:
                                link(ins)
                convolve(range(3))
                gains = [col("cq", l)[:, k:k + 1] for k in range(3)] + [col("ckv", l)[:, k:k + 1] for k in range(2)]
                for t in range(3):
                    dve.wait_ge(split_hi.sem, split_hi.at((L, "lt", t)))
                    for m in range(2 if t < 2 else 1):
                        k = 5 + 2 * t + m
                        ins = v.scalar_tensor_tensor(r_lo[:, k, :], bank[LATENT_BANK[t]][:, m * S:(m + 1) * S], gains[2 * t + m],
                                                     r_hi[:, k, :].bitcast(F32), MUL, SUB)
                    ins.then_inc(r_ready.sem, r_ready.next((L, "lt", t)))
                convolve(range(3, 5))
                dve.wait_ge(exp_small.sem, exp_small.at((L, "e")))
                e, w1, w2, q = S_(88, 12), S_(276, 12), S_(288, 12), S_(300, 12)
                ts(w1, e, 2.0, None, ADD)
                link(v.reciprocal(w1, w1))
                tt(w1, w1, e, MUL)
                tt(w2, w1, w1, MUL)
                ts(q, w2, 1.0 / 17, None, MUL)
                for n in (15, 13, 11, 9, 7, 5, 3):
                    stt(q, q, 1.0 / n, w2, ADD, MUL)
                stt(q, q, 1.0, w1, ADD, MUL)
                dt = S_(452, 12)
                ts(val, val, 0.0, None, ALU.max)
                stt(dt, q, 2.0, val, MUL, ADD)
                v.tensor_tensor(S_(64, 12).rearrange("p (b h) -> p b h", b=NB), dt.rearrange("p (b h) -> p b h", b=NB), a_neg[:, l, :].unsqueeze(1).to_broadcast([P, NB, SSD_H]), MUL).then_inc(steps_ready.sem, steps_ready.next((L, "dtA")))
                dve.wait_ge(product_done.sem, product_done.at((L, "wst")))
                v.tensor_tensor(wsT, bank[4][:, :].rearrange("p (h t) -> p h t", h=4), K("upto").unsqueeze(1).to_broadcast([P, 4, P]), MUL).then_inc(dve_read.sem, dve_read.next((L, "wst")))
                for b in range(NB):
                    dve.wait_ge(square_sum.sem, square_sum.at((L, "uv", b)))
                ts(S_(268, 2), S_(48, 2), 1.0 / 256, 1e-6, MUL, ADD)
                rsqrt(S_(270, 2), S_(268, 2), S_(272, 2))
                for b in range(NB):
                    vv = uv[:, b, 256:512]
                    ins = v.scalar_tensor_tensor(vv, vv, S_(270 + b, 1), gv[:, l, :], MUL, MUL)
                ins.then_inc(gmlp_ready.sem, gmlp_ready.next((L, "v")))
                dve.wait_ge(product_done.sem, product_done.at((L, "cum")))
                cum = S_(464, 24)
                v.tensor_copy(cum, bank[1][:, 0:24]).then_inc(dve_read.sem, dve_read.next((L, "cum")))
                dve.wait_ge(dve_read.sem, dve_read.made)
                v.tensor_copy(S_(130, 6), cum[:, 6:12])
                v.tensor_tensor(S_(124, 6), cum[:, 12:18], cum[:, 0:6], SUB).then_inc(steps_in.sem, steps_in.next((L, "end")))
                for c in range(NB):
                    for g in range(2):
                        dve.wait_ge(product_done.sem, product_done.at((L, "rc", c, g)))
                        for h in range(3):
                            i = c * SSD_H + 3 * g + h
                            ins = v.scalar_tensor_tensor(decay[:, i, :], bank[RC_BANK[2 * c + g]][:, h * P:(h + 1) * P], cum[:, i:i + 1],
                                                         K("future_st"), SUB, ADD)
                        ins.then_inc(dve_read.sem, dve_read.next((L, "rc", c, g)))
                dve.wait_ge(product_done.sem, product_done.at((L, "gm")))
                og = bank[1][:, :].rearrange("p (h c d) -> p h c d", h=4, c=NB)
                for k in range(4):
                    uu = uv[:, :, k * DH:(k + 1) * DH]
                    ins = v.scalar_tensor_tensor(uu, og[:, k, :, :], col("bs", l)[:, k:k + 1], uu, ADD, MUL)
                ins.then_inc(gating_read.sem, gating_read.next((L, "gm")))
                dve.wait_ge(exp_small.sem, exp_small.at((L, "end")))
                tt(S_(490, 6), S_(136, 6), dt[:, 0:6], MUL)
                dve.wait_ge(act_read.sem, act_read.at((L, "xs", 0)))
                v.tensor_tensor(x_dec.rearrange("p (h d) -> p h d", h=SSD_H), xs[:, 0, :].rearrange("p (h d) -> p h d", h=SSD_H), S_(490, 6).unsqueeze(2).to_broadcast([P, SSD_H, DH]), MUL).then_inc(state_in.sem, state_in.next(L))
                for c in range(NB):
                    dve.wait_ge(act_read.sem, act_read.at((L, "xs", c)))
                    tt(y_b[:, c, :].rearrange("p (h d) -> p h d", h=SSD_H), xs[:, c, :].rearrange("p (h d) -> p h d", h=SSD_H),
                       d_skip[:, l, :].unsqueeze(2).to_broadcast([P, SSD_H, DH]), MUL)
                for n in range(2):
                    for b in range(NB):
                        dve.wait_ge(act_read.sem, act_read.at((L, "qb", n, b)))
                rot = split_t[:, 0, 0:384].rearrange("p (b h d) -> p b h d", b=NB, h=M_H)
                for b in range(NB):
                    qr = qtok[:, b, :].rearrange("p (h d) -> p h d", h=M_H)[:, :, DH:M_QK]
                    for r in range(2):
                        tt(rot[:, b, :, 16 * r:16 * r + 16], qr[:, :, 16 - 16 * r:32 - 16 * r],
                           sin_m[:, b, 16 * r:16 * r + 16].unsqueeze(1).to_broadcast([P, M_H, 16]), MUL)
                    tt(qr, qr, cos_m[:, b, :].unsqueeze(1).to_broadcast([P, M_H, M_ROPE]), MUL)
                    ins = v.tensor_tensor(qr, qr, rot[:, b, :, :], ADD)
                    if b == 1:
                        ins.then_inc(roped.sem, roped.next((L, "q")))
                dve.wait_ge(product_done.sem, product_done.at((L, "cb", 1)))
                for c in range(NB):
                    for g in range(2):
                        dve.wait_ge(exp_seg.sem, exp_seg.at((L, c, g)))
                        for h in range(3):
                            i = c * SSD_H + 3 * g + h
                            ins = v.scalar_tensor_tensor(decay[:, i, :], decay[:, i, :], dt[:, i:i + 1],
                                                         bank[CB_BANK][:, g * S + c * P:g * S + (c + 1) * P], MUL, MUL)
                        ins.then_inc(decay_ready.sem, decay_ready.next((L, c, g)))
                for n in range(2):
                    for b in range(NB):
                        dve.wait_ge(act_read.sem, act_read.at((L, "kv", n, b)))
                for b in range(NB):
                    kk = ktok[:, b, :].rearrange("p (h d) -> p h d", h=M_H)
                    v.tensor_copy(kk[:, :, 0:DH], kvtok[:, b, :].rearrange("p (h d) -> p h d", h=M_H)[:, :, 0:DH])
                    ins = v.tensor_copy(kk[:, :, DH:M_QK], kr3[:, b, :].unsqueeze(1).to_broadcast([P, M_H, M_ROPE]))
                    if b == 1:
                        ins.then_inc(roped.sem, roped.next((L, "k")))

                yf = flat2(y_b)
                t3 = split_t[:, 0, 0:SSD_W]
                for c in range(NB):
                    dve.wait_ge(product_done.sem, product_done.at((L, "yd", c)))
                    v.tensor_tensor(y_b[:, c, :], y_b[:, c, :], bank[STATE_BANK[c]][:, 0:SSD_W], ADD).then_inc(state_read.sem, state_read.next((L, "yd", c)))
                dve.wait_ge(state_read.sem, state_read.made)
                dve.wait_ge(product_done.sem, product_done.at((L, "yo", 1)))
                for g in range(2):
                    v.tensor_tensor(t3[:, 192 * g:192 * g + 192].rearrange("p (h d) -> p h d", h=3),
                                    bank[1][:, 192 * g:192 * g + 192].rearrange("p (h d) -> p h d", h=3),
                                    S_(142 + 3 * g, 3).unsqueeze(2).to_broadcast([P, 3, DH]), MUL).then_inc(state_read.sem, state_read.next((L, "yo", g)))
                dve.wait_ge(state_read.sem, state_read.made)
                tt(y_b[:, 1, :], y_b[:, 1, :], t3, ADD)
                for b in range(NB):
                    dve.wait_ge(act_read.sem, act_read.at((L, "z", b)))
                v.tensor_tensor(yf, yf, flat2(zg), MUL).then_inc(z_gated.sem, z_gated.next(L))

                def split_lo(key, dst, src, hi, flow, gain=None):
                    dve.wait_ge(split_hi.sem, split_hi.at(key))
                    if gain is None:
                        v.tensor_tensor(dst, src, hi.bitcast(F32), SUB).then_inc(flow.sem, flow.next(key))
                    else:
                        for m, g in enumerate(gain):
                            ins = v.scalar_tensor_tensor(dst[:, m * S:(m + 1) * S], src[:, m * S:(m + 1) * S], g,
                                                         hi[:, m * S:(m + 1) * S].bitcast(F32), MUL, SUB)
                        ins.then_inc(flow.sem, flow.next(key))

                split_lo((L, "at"), flat2(r_lo[:, 0:2, :]), bank[GATING_BANK][:, :], flat2(r_hi[:, 0:2, :]), r_ready)
                for what, h in attention_order(M_H, "tsv"):
                    if what == "s":
                        dve.wait_ge(product_done.sem, product_done.at((L, "s", h)))
                        o = bank[4 + h % 2]
                        for b, (c0, c1) in enumerate(((0, P), (P, P + S))):
                            if h >= 2:
                                dve.wait_ge(exp_done.sem, exp_done.at((L, h - 2, b)))
                            if h >= 3:
                                dve.wait_ge(exp_done.sem, exp_done.at((L, h - 3, b)))
                            ins = v.tensor_tensor_reduce(out=masked[:, h % 2, c0:c1], in0=o[:, c0:c1], in1=K("causal")[:, c0:c1] if b == 0 else K("causal")[:, P:P + S],
                                                      scale=-1.0, scalar=BIG, op0=ADD, op1=ALU.min, accum_out=S_(16 + 4 * (h % 3) + b, 1))
                            if b == 1:
                                ins.then_inc(dve_read.sem, dve_read.next((L, "s", h)))
                            else:
                                ins.then_inc(row_max.sem, row_max.next((L, h)))
                    elif what == "t":
                        for b in range(NB):
                            dve.wait_ge(exp_done.sem, exp_done.at((L, h, b)))
                        r = normalise(h, range(NB))
                        for b, (c0, c1) in enumerate(((0, P), (P, P + S))):
                            p_ = prob[:, h % 3, c0:c1]
                            ins = v.tensor_scalar(p_, p_, r[:, b:b + 1], None, MUL)
                        ins.then_inc(probs_normal.sem, probs_normal.next((L, h)))
                    elif h == 3:
                        split_lo((L, "co", 0), flat2(r_lo[:, 5:7, :]), bank[HEAD_BANK[0]][:, :], flat2(r_hi[:, 5:7, :]), out_read)
                    elif h == 5:
                        split_lo((L, "co", 1), r_lo[:, 7, :], bank[HEAD_BANK[1]][:, 0:S], r_hi[:, 7, :], out_read)
                    if (what, h) == ("s", 1):
                        dve.wait_ge(square_sum.sem, square_sum.at((L, "y", 3)))
                        ts(S_(496, 4), S_(496, 4), 1.0 / 192, 1e-6, MUL, ADD)
                        rsqrt(S_(500, 4), S_(496, 4), S_(504, 4))
                        y4 = yf.rearrange("p (g n) -> p g n", g=4)
                        v.tensor_tensor(y4, y4, S_(500, 4).unsqueeze(2).to_broadcast([P, 4, 192]), MUL).then_inc(mixer_out.sem, mixer_out.next((L, "b")))
                    elif (what, h) == ("v", 0):
                        gains = [col("ssd", l)[:, k:k + 1] for k in range(3)]
                        split_lo((L, "bt", 0), flat2(r_lo[:, 2:4, :]), bank[STATE_BANK[0]][:, :], flat2(r_hi[:, 2:4, :]), r_ready, gains[0:2])
                        split_lo((L, "bt", 1), r_lo[:, 4, :], bank[STATE_BANK[1]][:, 0:S], r_hi[:, 4, :], r_ready, gains[2:3])
                for n in range(2):
                    for b in range(NB):
                        add_rows((L, "wo", n, b), n, b, bank[2 * n + b])
                        if n == 1:
                            rms(L, "mlp", b)
                rms_rows(L, "mlp", col("mlp", l))
                for e in range(8):
                    for u in range(2):
                        dve.wait_ge(square_hi.sem, square_hi.at((L, "up", e, u)))
                        relu, f = masked[:, u, :], split_t[:, u, :]
                        tt(f, relu, relu, MUL)
                        t0 = 4 * (e % 2) + 2 * u
                        v.tensor_tensor(flat2(r_lo[:, t0:t0 + 2, :]), f, flat2(r_hi[:, t0:t0 + 2, :]).bitcast(F32), SUB).then_inc(r_ready.sem, r_ready.next((L, "up", e, u)))
                        dve.wait_ge(r_ready.sem, r_ready.made)
                for n in range(2):
                    for b in range(NB):
                        add_rows((L, "dn", n, b), n, b, bank[4 + 2 * n + b])
                        if n == 1 and l == 0:
                            rms("d1", "mix", b)
                        elif n == 1:
                            rms("end", "end", b)
                            if b == 0:
                                dve.wait_ge(gf_loaded, 16)
                            dve.wait_ge(row_stats.sem, row_stats.made)
                            v.scalar_tensor_tensor(z[:, b, :], x[:, b, :], S_(8 + b, 1), gf, MUL, MUL).then_inc(row_out.sem, row_out.next(b))

        for steps in every:
            assert steps.made == len(steps.order)


_INS = ["x", "mem", "ln_in_g", "ln_in_b", "w_mem_kv", "w_in_a", "w_in_b", "q_norm_g", "k_norm_g", "w_in_c", "w_out", "ln_g",
        "ln_b", "norm_mix_g_2", "w_in_2", "gmlp_v_norm_g_2", "gmlp_w_s_2", "gmlp_b_s_2", "ssd_conv_w_2", "ssd_conv_b_2",
        "ssd_dt_bias_2", "ssd_a_log_2", "ssd_d_2", "ssd_norm_g_2", "mla_q_norm_g_2", "mla_w_qb_2", "mla_kv_norm_g_2",
        "mla_w_kvb_2", "w_out_2", "norm_mlp_g_2", "mlp_w1_2", "mlp_w2_2", "final_norm_g_2"]


def kernel(**inputs):
    import concourse.bacc as bacc
    from concourse.bass_utils import run_bass_kernel_spmd

    nc = bacc.Bacc("TRN2", target_bir_lowering=False, num_devices=1)
    arrays, aps = {}, {}
    for name in _INS + ["const"]:
        a = constants()[0] if name == "const" else np.ascontiguousarray(inputs[name])
        arrays[f"in_{name}"] = a
        aps[name] = nc.dram_tensor(f"in_{name}", a.shape, mybir.dt.from_np(a.dtype), kind="ExternalInput").ap()
    out = nc.dram_tensor("out", (1, S, D), F32, kind="ExternalOutput").ap()
    build(nc, aps, out)
    return run_bass_kernel_spmd(nc, [arrays], core_ids=[0]).results[0]["out"]
```

```python
from contextlib import ExitStack

import numpy as np

import concourse.bass as bass
from concourse import mybir

F32 = mybir.dt.float32
F32R = mybir.dt.float32r
I32 = mybir.dt.int32
ACT = mybir.ActivationFunctionType
ALU = mybir.AluOpType
AX = mybir.AxisListType

P = 128
S = 256
NB = S // P
D = 1024
KT = D // P
DH = 64
N_MEM = 256
MASKED = -1e30
BIG = 3.0e38

MEM_HEADS = 4
MEM_W = MEM_HEADS * DH
INNER = D + MEM_W
YT = INNER // P
TAIL = INNER + MEM_W
HEADS = D // DH
PROBS = 4
HEADS_AHEAD = PROBS - 1
KV_HEADS = HEADS // 4
ALPHA = 8.0 ** 0.25
GW = D // 4
DIL_W = 3 * D

UV = 512
SSD_H = 6
SSD_W = SSD_H * DH
XBC = SSD_W + 256
Q_RANK = 384
KV_RANK = 256
M_ROPE = 32
M_QK = 96
M_H = 6
D_FF = 4096
C_UV, C_Z, C_XBC = 0, UV, UV + SSD_W
C_DT = C_XBC + XBC
C_CKV = C_DT + SSD_H + Q_RANK
DTQ = SSD_H + Q_RANK
KVR = KV_RANK + M_ROPE

RAW_SLOTS = 3
SPLIT_SLOTS = 3
UNIT = 2048


def token_order():
    p = np.arange(S)
    return 16 * (p % 16) + 4 * (p // 16 % 4) + p // 64


CONST_AT = {}


def constants():
    t = token_order()
    parts = []

    def put(name, a):
        a = np.asarray(a, np.float64)
        if a.ndim == 2 and a.shape[0] == S:
            a = a.reshape(NB, P, -1).transpose(1, 0, 2).reshape(P, -1)
        CONST_AT[name] = (sum(x.shape[1] for x in parts), a.shape[1])
        parts.append(a)

    put("ident", np.eye(P))
    put("ones", np.ones((P, P)))
    i = np.arange(P)
    upto = (i[:, None] <= i[None, :]).astype(np.float64)
    put("upto", upto)
    put("future_st", (1 - upto) * MASKED)
    causal = (1 - upto.T) * MASKED
    put("causal", np.concatenate([causal, np.zeros((P, P)), causal], 1))
    a = 2 * np.pi * np.outer(t, t) / S
    put("dft_tok", np.concatenate([np.cos(a), -np.sin(a)], 1) / 16)

    def rope(pos, dim, base=10000.0):
        f = base ** (-(np.arange(0, dim, 2) / dim))
        a = (np.asarray(pos, np.float32)[:, None] * f.astype(np.float32)[None, :]).astype(np.float64)
        c, s = np.cos(a), np.sin(a)
        return np.concatenate([c, c], 1), np.concatenate([-s, s], 1)

    rc, rs = rope(t // 64, DH // 2)
    cc, cs = rope(t % 64, DH // 2)
    put("axial_cos", np.concatenate([rc, cc], 1))
    put("axial_sin", np.concatenate([rs, cs], 1))
    c, s = rope(t, DH)
    put("line_cos", c)
    put("line_sin", s)
    c, s = rope(np.arange(S), M_ROPE)
    put("mla_cos", c)
    put("mla_sin", s)
    mask = np.zeros((S, 512))
    for b in range(NB):
        q = t[b * P:(b + 1) * P, None]
        own = t[None, b * P:(b + 1) * P]
        mask[b * P:(b + 1) * P, 0:S] = np.abs(t[None, :] - q) > 64
        mask[b * P:(b + 1) * P, S:S + P] = (own - q) % 4 != 0
        mask[b * P:(b + 1) * P, S + P:] = (own - q) % 16 != 0
    put("dilated_mask", mask * MASKED)
    n_kept = sum(x.shape[1] for x in parts)
    j = np.arange(GW)
    a = 2 * np.pi * np.outer(j, j) / GW
    put("dft_ch", np.concatenate([np.cos(a), np.sin(a)], 1) / 16)
    return np.ascontiguousarray(np.concatenate(parts, 1).astype(np.float32)), n_kept


def build(nc, A, out):
    _, n_kept = constants()
    with ExitStack() as ctx:
        def sb(name, shape, dt=F32):
            return ctx.enter_context(nc.sbuf_tensor(name, shape, dt))

        w_raw = sb("w_raw", [P, RAW_SLOTS, UNIT])
        w_hi = sb("w_hi", [P, SPLIT_SLOTS, UNIT], F32R)
        w_lo = sb("w_lo", [P, SPLIT_SLOTS, UNIT], F32R)
        h_hi = sb("h_hi", [P, KT, S], F32R)
        h_lo = sb("h_lo", [P, KT, S], F32R)
        r_hi = sb("r_hi", [P, YT, S], F32R)
        r_lo = sb("r_lo", [P, YT, S], F32R)
        const = sb("const", [P, n_kept])
        dft_hi = sb("dft_hi", [P, 2, 512], F32R)
        dft_lo = sb("dft_lo", [P, 2, 512], F32R)
        ident_r = sb("ident_r", [P, P], F32R)
        gate = sb("gate", [P, YT, S])
        mem_kv = sb("mem_kv", [P, 2, 512])
        mkT = mem_kv[:, 0, :].rearrange("p (a m) -> p a m", a=2)
        mv = mem_kv[:, 1, :].rearrange("p (b n) -> p b n", b=NB)
        N_COL_A, N_COL_B = 80, 106
        col_a = sb("col_a", [P, N_COL_A])
        col_b = sb("col_b", [P, N_COL_B])
        row = sb("row", [P, 2 * DH + 2 * 256 + 36])
        masked = sb("masked", [P, 2, 512])
        prob = sb("prob", [P, PROBS, 512])
        probT = sb("probT", [P, 2, 512])
        split_t = sb("split_t", [P, 2, 512])
        stat = sb("stat", [P, 512])
        ARENA = 9676
        arena = sb("arena", [P, ARENA])

        bank = [ctx.enter_context(nc.psum_tensor(f"bank{i}", [P, 512], F32)) for i in range(8)]

        def K(name):
            at, n = CONST_AT[name]
            return const[:, at:at + n]

        ident = K("ident")

        class Steps:

            def __init__(self, name):
                self.sem = ctx.enter_context(nc.semaphore(name))
                self.order, self.made, self.unit = {}, 0, {}
                every.append(self)

            def at(self, key):
                return self.order.setdefault(key, len(self.order) + 1)

            def after(self, key):
                return self.sem, self.at(key)

            def next(self, key):
                self.made += 1
                assert self.at(key) == self.made, (key, self.at(key), self.made)
                self.unit[key] = len(units) - 1
                return 1

        every = []
        product_done = Steps("product_done")
        act_read = Steps("act_read")
        dve_read = Steps("dve_read")
        tiles_read = Steps("tiles_read")
        state_read = Steps("state_read")
        gating_read = Steps("gating_read")
        out_read = Steps("out_read")
        w_rounded = Steps("w_rounded")
        w_split = Steps("w_split")
        tables_rounded = Steps("tables_rounded")
        tables_split = Steps("tables_split")
        a_exp = Steps("a_exp")
        row_stats = Steps("row_stats")
        row_scales = Steps("row_scales")
        tiles_gained = Steps("tiles_gained")
        xbc_scaled = Steps("xbc_scaled")
        rows_normal = Steps("rows_normal")
        rows_normal_v = Steps("rows_normal_v")
        h_rounded = Steps("h_rounded")
        h_ready = Steps("h_ready")
        r_ready = Steps("r_ready")
        gate_ready = Steps("gate_ready")
        gated_hi = Steps("gated_hi")
        row_max = Steps("row_max")
        scores_read = Steps("scores_read")
        exp_half = Steps("exp_half")
        exp_done = Steps("exp_done")
        probs_normal = Steps("probs_normal")
        roped = Steps("roped")
        square_sum = Steps("square_sum")
        square_hi = Steps("square_hi")
        latent_normal = Steps("latent_normal")
        xbc_ready = Steps("xbc_ready")
        conv_done = Steps("conv_done")
        gmlp_ready = Steps("gmlp_ready")
        steps_in = Steps("steps_in")
        exp_small = Steps("exp_small")
        steps_ready = Steps("steps_ready")
        exp_seg = Steps("exp_seg")
        decay_ready = Steps("decay_ready")
        split_hi = Steps("split_hi")
        z_gated = Steps("z_gated")
        state_in = Steps("state_in")
        mixer_out = Steps("mixer_out")
        row_out = Steps("row_out")
        vector_step = Steps("vector_step")
        w_loaded = [ctx.enter_context(nc.semaphore(f"w_loaded{i}")) for i in range(RAW_SLOTS)]
        ident_loaded = ctx.enter_context(nc.semaphore("ident_loaded"))
        consts_loaded = ctx.enter_context(nc.semaphore("consts_loaded"))
        x_loaded = ctx.enter_context(nc.semaphore("x_loaded"))
        mem_loaded = ctx.enter_context(nc.semaphore("mem_loaded"))
        rows_a_loaded = ctx.enter_context(nc.semaphore("rows_a_loaded"))
        rows_b_loaded = ctx.enter_context(nc.semaphore("rows_b_loaded"))
        ws_loaded = ctx.enter_context(nc.semaphore("ws_loaded"))
        gf_loaded = ctx.enter_context(nc.semaphore("gf_loaded"))
        stored = ctx.enter_context(nc.semaphore("stored"))

        units = []
        unit_done = {}
        down_done = {}
        left = {}

        def view(at, *shape):
            n = int(np.prod(shape))
            assert at + n <= ARENA, (at, shape)
            v = arena[:, at:at + n]
            if len(shape) == 1:
                return v
            names = "abcd"[:len(shape)]
            return v.rearrange(f"p ({' '.join(names)}) -> p {' '.join(names)}", **{k: s for k, s in zip(names, shape)})

        z = view(2048, NB, D)
        x_in = view(0, NB, D)
        mem_in = view(4096, NB, D)
        const_once = view(6144, 1024)
        rows_a = arena[0:N_COL_A, 7300:7300 + P]
        rows_b = arena[0:N_COL_B, 7428:7428 + P]
        qmT = view(8000, 2, S)
        spectra = view(0, NB, 4, 512)
        qkv = view(0, NB, 1536)
        b_sq = view(3072, 1280)
        k_dup = view(4352, NB, KV_HEADS, 2, DH)
        b_rot = b_sq[:, 0:1024]
        gcos = view(5376, 2, NB, DH)
        gsin = view(5632, 2, NB, DH)
        bkT = view(5888, KV_HEADS, S)
        b_qmT = view(6912, 2, S)
        bqT = view(7424, 8, S)
        cqT = view(0, 3, 4, S)
        ckT = view(3072, 3, 4, S)
        cv = view(6144, NB, 3, 512)
        c_rot = prob[:, 0:2, :]
        c_tmp = split_t[:, 1, 0:256]
        c_qmT = view(0, 2, S)
        x = view(0, NB, D)
        qtok = view(2048, NB, 576)
        zg = view(3200, NB, SSD_W)
        xbcT = view(4096, 5, S + 3)
        mqT = view(4096, M_H, S)
        xs = view(5632, NB, SSD_W)
        kvtok = view(6400, NB, 768)
        ktok = view(7936, NB, 576)
        cqt = view(7936, NB, DTQ)
        ckt = view(7936 + NB * DTQ, NB, KVR)
        mem_space = mem_kv[:, :, :].rearrange("p a b -> p (a b)")
        y_b = mem_space[:, 0:NB * SSD_W].rearrange("p (b n) -> p b n", b=NB)
        st_sb = mem_space[:, NB * SSD_W:NB * SSD_W + 192]
        tables_at = CONST_AT["dft_tok"][0]
        decay = const[:, tables_at:tables_at + NB * SSD_H * P].rearrange("p (i t) -> p i t", t=P)
        ws_raw = K("dilated_mask")[:, 0:512].rearrange("p (h s) -> p h s", h=4)
        wsT = K("dilated_mask")[:, 512:1024].rearrange("p (h t) -> p h t", h=4)
        b_tok = view(3968, P)
        x_dec = view(9292, SSD_W)
        assert CONST_AT["mla_cos"][0] == tables_at + NB * SSD_H * P
        uv = gate[:, 0:4, :].rearrange("p a b -> p (a b)").rearrange("p (b n) -> p b n", b=NB)
        mkvT = gate[:, 4:10, :]
        conv = prob[:, :, :].rearrange("p a b -> p (a b)")[:, 0:1280].rearrange("p (t s) -> p t s", t=5)
        gf = gate[:, 0:4, :].rearrange("p a b -> p (a b)")

        def S_(at, n):
            return stat[:, at:at + n]

        q_gain, k_gain = row[:, 0:DH], row[:, DH:2 * DH]
        gv = row[:, 2 * DH:2 * DH + 512].rearrange("p (l n) -> p l n", l=2)
        dt_bias = row[:, 640:652].rearrange("p (l h) -> p l h", l=2)
        a_neg = row[:, 652:664].rearrange("p (l h) -> p l h", l=2)
        d_skip = row[:, 664:676].rearrange("p (l h) -> p l h", l=2)

        def ln_cols(i):
            if i == 0:
                return col_a[:, 0:8], col_a[:, 8:16]
            return col_a[:, 16 + 8 * (i - 1):24 + 8 * (i - 1)], col_a[:, 48 + 8 * (i - 1):56 + 8 * (i - 1)]

        col_at, n_b = {}, 0
        for nm, n in (("mix", 8), ("mlp", 8), ("conv_w", 20), ("conv_b", 5), ("cq", 3), ("ckv", 2), ("ssd", 3), ("bs", 4)):
            col_at[nm] = (n_b, n)
            n_b += 2 * n
        assert n_b == N_COL_B

        def col(nm, l):
            at, n = col_at[nm]
            return col_b[:, at + l * n:at + (l + 1) * n]

        ROW_A_DMAS, ROW_B_DMAS = 4, 8 + 6

        LATENT_BANK, QB_BANK, RC_BANK, XS_BANK, Z_BANK = (7, 0, 1), (5, 6, 7, 0), (2, 3, 4, 5), (0, 6), (0, 6)
        KV_BANK, QT_BANK, KT_BANK, STATE_BANK, CB_BANK = (2, 3, 4, 5), (7, 2, 3), (4, 5, 7), (0, 6), 7
        CQ_BANK, CK_BANK, XBC_BANK, RMS_BANK = (4, 5), (6, 7), (0, 1, 2), 3
        GATING_BANK, HEAD_BANK = 1, (7, 1)
        block = ctx.enter_context(nc.Block())

        def rows_of(w, k0, kts, c0, n):
            return w[k0:k0 + kts * P, c0:c0 + n].rearrange("(k p) n -> p k n", p=P), kts, n

        LAYERS = [("a", 0), ("b", 0), ("c", 0), ("a", 1)]
        LAYER_NAMES = [f"{k}{j}" for k, j in LAYERS] + [("d0", "mix")]
        BY_SCALAR = [(0, 0), (0, 1), (1, 1)]

        CHUNK_BANKS = [[2 * (n % 2), 2 * (n % 2) + 1] for n in range(8)] + [[6, 7]]
        HEADS_BEFORE, HEADS_AFTER = 2, 5

        LONG, SHORT, NORMAL_LAG = (HEADS_AHEAD, HEADS_AHEAD + 1), (2, 3), 2

        def attention_order(n, lags=LONG, steps="stv"):
            lag = dict(zip("stv", (0, *lags)))
            for i in range(n + lags[-1]):
                for what in steps:
                    if 0 <= i - lag[what] < n:
                        yield what, i - lag[what]

        memory_order, cuts = list(attention_order(MEM_HEADS, SHORT)), (0, 1, 4, 7, 9, 11, 12)
        MEMORY_STEPS = [memory_order[c0:c1] for c0, c1 in zip(cuts[:-1], cuts[1:])]
        GATE_BANK = (4, 5, 6, 4, 5)
        B_QK_BANK = (2, 3, 6, 7, 4, 5)
        B_OUT_BANK = (7, 4, 5, 6, 4)

        def b_out_key(L, group):
            return (L, "ao", group - 1) if group else (L, "mo")

        @block.tensor
        def _(pe):
            def unit(source):
                u = len(units)
                units.append(source)
                pe.wait_ge(w_split.sem, w_split.at(u))
                slot, (_, kts, n) = u % SPLIT_SLOTS, source
                return u, [w[:, slot, 0:kts * n].rearrange("p (k n) -> p k n", k=kts) for w in (w_hi, w_lo)]

            def mm3(o, lhs, rhs, start, stop):
                nc.tensor.matmul(o, lhs[0], rhs[0], start=start, stop=False)
                nc.tensor.matmul(o, lhs[0], rhs[1], start=False, stop=False)
                return nc.tensor.matmul(o, lhs[1], rhs[0], start=False, stop=stop)

            def hT(k, b=None):
                cols = slice(0, S) if b is None else slice(b * P, (b + 1) * P)
                return h_hi[:, k, cols], h_lo[:, k, cols]

            def rT(k, b=None):
                cols = slice(0, S) if b is None else slice(b * P, (b + 1) * P)
                return r_hi[:, k, cols], r_lo[:, k, cols]

            def feature_major(key, b, source, act, reader=act_read, hidden=None):
                if b in left:
                    pe.wait_ge(*left[b])
                left[b] = reader.after(key)
                o = bank[b]
                u, w = unit(source)
                _, kts, n = source
                tiles = n // P
                step = kts if hidden is None else 2
                for k0 in range(0, kts, step):
                    if hidden is not None:
                        pe.wait_ge(h_ready.sem, h_ready.at((hidden, k0 // 2)))
                    for m in range(tiles):
                        for k in range(k0, k0 + step):
                            i = mm3(o[:, m * S:(m + 1) * S], [a[:, k, m * P:(m + 1) * P] for a in w], act(k),
                                    k + m == 0, k == kts - 1 and m == tiles - 1)
                i.then_inc(product_done.sem, product_done.next(key))
                unit_done[u] = key

            def token_major(keys, banks, sources, act, reader=act_read, hidden=None, opened=True, closed=True):
                for b in range(NB):
                    if opened and banks[b] in left:
                        pe.wait_ge(*left[banks[b]])
                    left[banks[b]] = reader.after(keys[b])
                o = [bank[banks[b]] for b in range(NB)]
                k0 = 0
                for s, source in enumerate(sources):
                    u, w = unit(source)
                    _, kts, n = source
                    step = kts if hidden is None else 2
                    for k2, b in [(k2, b) for k2 in range(0, kts, step) for b in range(NB)]:
                        last_unit = s == len(sources) - 1
                        for k in range(k2, k2 + step):
                            if hidden is not None and b == 0 and k % 2 == 0:
                                pe.wait_ge(h_ready.sem, h_ready.at((hidden, (k0 + k) // 2)))
                            i = mm3(o[b][:, 0:n], act(k0 + k, b), [a[:, k, :] for a in w],
                                    opened and s == 0 and k == 0, closed and last_unit and k == kts - 1)
                        if k2 + step < kts:
                            continue
                        if last_unit and closed:
                            i.then_inc(product_done.sem, product_done.next(keys[b]))
                        elif b == NB - 1:
                            i.then_inc(product_done.sem, product_done.next(("unit", u)))
                    unit_done[u] = keys[NB - 1] if last_unit and closed else ("unit", u)
                    k0 += kts

            def transposes(key, b, ins, reader, width=P):
                if b in left:
                    pe.wait_ge(*left[b])
                left[b] = reader.after(key)
                o = bank[b]
                for n, a in enumerate(ins):
                    i = nc.tensor.transpose(o[0:a.shape[1], n * width:n * width + P], a, ident)
                i.then_inc(product_done.sem, product_done.next(key))

            def hidden_from_rows(L, b0):
                for b in range(NB):
                    for j in range(4):
                        if b == 0:
                            pe.wait_ge(rows_normal.sem, rows_normal.at((L, 0, j // 2)))
                            if b0 + j in left:
                                pe.wait_ge(*left[b0 + j])
                            left[b0 + j] = tiles_read.after((L, "zt", j))
                        elif j < 2:
                            pe.wait_ge(rows_normal_v.sem, rows_normal_v.at(L))
                        else:
                            pe.wait_ge(rows_normal.sem, rows_normal.at((L, 1, 1)))
                        for m in range(2):
                            k = 2 * j + m
                            i = nc.tensor.transpose(bank[b0 + j][:, m * S + b * P:m * S + (b + 1) * P], z[:, b, k * P:(k + 1) * P], ident)
                        if b == NB - 1:
                            i.then_inc(product_done.sem, product_done.next((L, "zt", j)))

            def stream_tiles(L, added, n):
                for j in (2 * n, 2 * n + 1):
                    if 4 + j in left:
                        pe.wait_ge(*left[4 + j])
                    left[4 + j] = tiles_read.after((L, "zt", j))
                    for b in range(NB):
                        pe.wait_ge(dve_read.sem, dve_read.at((*added, n, b)))
                        for m in range(2):
                            k = 2 * j + m
                            i = nc.tensor.transpose(bank[4 + j][:, m * S + b * P:m * S + (b + 1) * P], x[:, b, k * P:(k + 1) * P], ident)
                    i.then_inc(product_done.sem, product_done.next((L, "zt", j)))

            def attend(L, heads, steps, sb0, tb0, q_of, k_of, v_of, o_of):
                for what, i in steps:
                    h = heads[i]
                    if what == "s":
                        n_b = sb0 + i % 2
                        if n_b in left:
                            pe.wait_ge(*left[n_b])
                        left[n_b] = scores_read.after((L, "s", h))
                        o = bank[n_b]
                        for b in range(NB):
                            m = nc.tensor.matmul(o[:, b * S:(b + 1) * S], q_of(h)[:, b * P:(b + 1) * P], k_of(h),
                                                 start=True, stop=True)
                        m.then_inc(product_done.sem, product_done.next((L, "s", h)))
                    elif what == "t":
                        pe.wait_ge(probs_normal.sem, probs_normal.at((L, h)))
                        pr = prob[:, i % PROBS, :]
                        transposes((L, "t", h), tb0 + i % 2,
                                   [pr[:, b * S + k * P:b * S + (k + 1) * P] for k in range(2) for b in range(NB)],
                                   act_read)
                    else:
                        pe.wait_ge(act_read.sem, act_read.at((L, "t", h)))
                        key, b, o, first, last = o_of(i, h)
                        if first:
                            if b in left:
                                pe.wait_ge(*left[b])
                            left[b] = out_read.after(key)
                        for k in range(2):
                            m = nc.tensor.matmul(o, v_of(h, k), probT[:, i % 2, k * S:(k + 1) * S],
                                                 start=k == 0, stop=k == 1)
                        m.then_inc(product_done.sem, product_done.next(key if last else (L, "o", h)))

            def memory_heads(L, qT_, steps):
                def o_of(i, h):
                    b = 7
                    return (L, "mo"), b, bank[b][64 * (h % 2):64 * (h % 2) + 64, (h // 2) * S:(h // 2 + 1) * S], i == 0, i == 3
                pe.wait_ge(act_read.sem, act_read.at((L, "qm")))
                attend((L, "m"), range(MEM_HEADS), steps, 0, 2,
                       lambda h: qT_[64 * (h % 2):64 * (h % 2) + 64, h // 2, :],
                       lambda h: mkT[64 * (h % 2):64 * (h % 2) + 64, h // 2, :],
                       lambda h, k: mv[:, k, h * DH:(h + 1) * DH], o_of)

            def gates(L, w, tail, hidden=None, qT_=None):
                feature_major((L, "qm"), 0, rows_of(w, 0, KT, tail + INNER, MEM_W), hT, hidden=hidden)
                for u in range(5):
                    feature_major((L, "gate", u), GATE_BANK[u], rows_of(w, 0, KT, tail + u * 256, 256), hT)
                    if qT_ is not None:
                        memory_heads(L, qT_, MEMORY_STEPS[u])

            def out_product(L, i):
                for n in range(2):
                    for b in range(NB):
                        if 2 * n + b in left:
                            pe.wait_ge(*left[2 * n + b])
                        if n == 0 and b == 1:
                            left[2 * n + b] = rows_normal_v.after(L)
                        else:
                            left[2 * n + b] = rows_normal.after((L, b, n))
                        for j in range(4):
                            for part, h_part in enumerate(hT(4 * n + j, b)):
                                nc.tensor.matmul(bank[2 * n + b][:, j * P:(j + 1) * P], h_part, ident_r[:], start=j + part == 0, stop=False)
                    for k0, kts in ((8, 2), (0, 4), (4, 4)):
                        u, w = unit(rows_of(A["w_out"][i], k0 * P, kts, n * 512, 512))
                        for b in range(NB):
                            for k in range(kts):
                                if n == 0 and b == 0 and k % 2 == 0:
                                    pe.wait_ge(r_ready.sem, r_ready.at((L, (k0 + k) // 2)))
                                m = mm3(bank[2 * n + b][:, :], rT(k0 + k, b), [a[:, k, :] for a in w], False, k0 + k == 7)
                            if k0 == 4:
                                m.then_inc(product_done.sem, product_done.next((L, "wo", n, b)))
                            elif b == NB - 1:
                                m.then_inc(product_done.sem, product_done.next(("unit", u)))
                        unit_done[u] = (L, "wo", n, NB - 1) if k0 == 4 else ("unit", u)

            pe.wait_ge(ident_loaded, 16)
            pe.wait_ge(mem_loaded, 16)
            for j in range(4):
                transposes(("mem", "t", j), 4 + j,
                           [mem_in[:, b, k * P:(k + 1) * P] for k in (2 * j, 2 * j + 1) for b in range(NB)], r_ready)
            pe.wait_ge(rows_a_loaded, 16 * ROW_A_DMAS)
            left[0] = act_read.after(("cols", "a"))
            nc.tensor.transpose(bank[0][:, 0:N_COL_A], rows_a, ident[0:N_COL_A, 0:N_COL_A])\
                .then_inc(product_done.sem, product_done.next(("cols", "a")))
            for j in range(4):
                pe.wait_ge(r_ready.sem, r_ready.at(("mem", "t", j)))
            feature_major(("mem", "k"), 4, rows_of(A["w_mem_kv"], 0, KT, 0, MEM_W), rT)
            hidden_from_rows("in", 0)
            u, w = unit(rows_of(A["w_mem_kv"], 0, KT, MEM_W, MEM_W))
            if 5 in left:
                pe.wait_ge(*left[5])
            left[5] = act_read.after(("mem", "v"))
            o = bank[5]
            for b in range(NB):
                for k in range(KT):
                    i = mm3(o[:, b * MEM_W:(b + 1) * MEM_W], rT(k, b), [a[:, k, :] for a in w], k == 0, k == KT - 1)
            i.then_inc(product_done.sem, product_done.next(("mem", "v")))
            unit_done[u] = ("mem", "v")

            for li, (kind, j) in enumerate(LAYERS):
                L = f"{kind}{j}"
                if li == 1:
                    pe.wait_ge(rows_b_loaded, 16 * ROW_B_DMAS)
                    if 3 in left:
                        pe.wait_ge(*left[3])
                    left[3] = act_read.after(("cols", "b"))
                    nc.tensor.transpose(bank[3][:, 0:N_COL_B], rows_b, ident[0:N_COL_B, 0:N_COL_B])\
                        .then_inc(product_done.sem, product_done.next(("cols", "b")))
                if kind == "a":
                    w = A["w_in_a"][j]
                    gates(L, w, 0, hidden=L, qT_=qmT)
                    if j == 0:
                        pe.wait_ge(consts_loaded, 32)
                        pe.wait_ge(tables_split.sem, tables_split.at("lo"))
                    for g in range(4):
                        for b in range(NB):
                            n_b = 2 * (g % 3) + b
                            if n_b in left:
                                pe.wait_ge(*left[n_b])
                            left[n_b] = (act_read if b == 0 else dve_read).after((L, "f1", g, b))
                            o = bank[n_b]
                            for k in range(2):
                                i = mm3(o[:, :], hT(2 * g + k, b), (dft_hi[:, k, :], dft_lo[:, k, :]), k == 0, k == 1)
                            i.then_inc(product_done.sem, product_done.next((L, "f1", g, b)))
                        if g == 0:
                            memory_heads(L, qmT, MEMORY_STEPS[5])
                    dt = K("dft_tok").rearrange("p (b c) -> p b c", b=NB)
                    for t in range(4):
                        pe.wait_ge(act_read.sem, act_read.at((L, "f1", t, 0)))
                        pe.wait_ge(dve_read.sem, dve_read.at((L, "f1", t, 1)))
                        n_b = 2 * (t % 2)
                        if n_b in left:
                            pe.wait_ge(*left[n_b])
                        left[n_b] = out_read.after((L, "f2", t))
                        o = bank[n_b]
                        for c in range(2):
                            for part in range(2):
                                for b in range(NB):
                                    i = nc.tensor.matmul(
                                        o[:, c * S:(c + 1) * S], spectra[:, b, t, part * GW + c * P:part * GW + (c + 1) * P],
                                        dt[:, b, part * S:(part + 1) * S], start=part + b == 0, stop=part + b == 2)
                        i.then_inc(product_done.sem, product_done.next((L, "f2", t)))
                elif kind == "b":
                    w = A["w_in_b"][0]
                    for c in range(3):
                        token_major([(L, "p", c, b) for b in range(NB)], [2 * c, 2 * c + 1],
                                    [rows_of(w, kh * 512, 4, c * 512, 512) for kh in range(2)], hT, hidden=L if c == 0 else None)
                    gates(L, w, 1536)
                    def b_half(a, h, tile):
                        return a[64 * (h % 2):64 * (h % 2) + 64, tile, :]

                    def q_of(i):
                        return b_half(b_qmT, i, i // 2) if i < MEM_HEADS else b_half(bqT, i, (i - MEM_HEADS) // 2)

                    def k_of(i):
                        return b_half(mkT, i, i // 2) if i < MEM_HEADS else b_half(bkT, i, (i - MEM_HEADS) // 4)

                    def v_of(i, k):
                        if i < MEM_HEADS:
                            return mv[:, k, i * DH:(i + 1) * DH]
                        at = D + KV_HEADS * DH + (i - MEM_HEADS) // 4 * DH
                        return qkv[:, k, at:at + DH]

                    def o_of(i, h):
                        b = B_OUT_BANK[i // 4]
                        return b_out_key(L, i // 4), b, bank[b][64 * (h % 2):64 * (h % 2) + 64, (i % 4 // 2) * S:(i % 4 // 2 + 1) * S], i % 4 == 0, i % 4 == 3

                    def all_heads(steps):
                        attend((L, "h"), range(MEM_HEADS + HEADS), steps, 0, 2, q_of, k_of, v_of, o_of)
                    order = list(attention_order(MEM_HEADS + HEADS))
                    pe.wait_ge(act_read.sem, act_read.at((L, "qm")))
                    all_heads(order[:2])
                    for t in range(4):
                        for b in range(NB):
                            pe.wait_ge(roped.sem, roped.at((L, "q", b)))
                        transposes((L, "qt", t), B_QK_BANK[t],
                                   [qkv[:, b, m * P:(m + 1) * P] for m in (2 * t, 2 * t + 1) for b in range(NB)], act_read)
                    for t in range(2):
                        for b in range(NB):
                            pe.wait_ge(roped.sem, roped.at((L, "k", b)))
                        transposes((L, "kt", t), B_QK_BANK[4 + t],
                                   [k_dup[:, b, m, :, :].rearrange("p a d -> p (a d)") for m in (2 * t, 2 * t + 1) for b in range(NB)],
                                   act_read)
                    all_heads(order[2:4])
                    for t in range(4):
                        pe.wait_ge(act_read.sem, act_read.at((L, "qt", t)))
                    for t in range(2):
                        pe.wait_ge(act_read.sem, act_read.at((L, "kt", t)))
                    all_heads(order[4:])
                else:
                    w = A["w_in_c"][0]
                    gates(L, w, 3 * DIL_W, hidden=L, qT_=c_qmT)
                    chunks = [(s, g) for g in range(3) for s in range(2)] + [(2, g) for g in range(3)]

                    def chunk(half, n):
                        s, g = chunks[n]
                        token_major([(L, half, "p", s, g, b) for b in range(NB)], CHUNK_BANKS[n],
                                    [rows_of(w, kh * 512, 4, s * DIL_W + g * D + half * 512, 512) for kh in range(2)],
                                    hT, reader=dve_read if s < 2 else act_read)

                    def turn(half, n):
                        s, g = chunks[n]
                        for t in range(2):
                            for b in range(NB):
                                pe.wait_ge(roped.sem, roped.at((L, half, s, g, b)))
                            transposes((L, half, "xt", s, g, t), 4 + t,
                                       [c_rot[:, b, m * P:(m + 1) * P] for m in (2 * t, 2 * t + 1) for b in range(NB)],
                                       act_read)

                    def dilated_heads(half, steps):
                        for what, i in steps:
                            h, b = i // 2, i % 2
                            at, pr = 64 * (h % 2), h // 2
                            qs = slice(b * P, (b + 1) * P)
                            if what == "s":
                                n_b = i % 2
                                if n_b in left:
                                    pe.wait_ge(*left[n_b])
                                left[n_b] = dve_read.after((L, half, "s", i))
                                o = bank[n_b]
                                for g, (c0, c1, ks) in enumerate(((0, S, slice(0, S)), (S, S + P, qs), (S + P, 512, qs))):
                                    m = nc.tensor.matmul(o[:, c0:c1], cqT[at:at + 64, g, pr, qs], ckT[at:at + 64, g, pr, ks],
                                                         start=True, stop=True)
                                m.then_inc(product_done.sem, product_done.next((L, half, "s", i)))
                            elif what == "t":
                                pe.wait_ge(probs_normal.sem, probs_normal.at((L, half, i)))
                                transposes((L, half, "t", i), 2 + i % 2, [prob[:, i % PROBS, k * P:(k + 1) * P] for k in range(4)], act_read)
                            else:
                                if i == 0:
                                    for g in range(3):
                                        for kb in range(NB):
                                            pe.wait_ge(act_read.sem, act_read.at((L, half, "p", 2, g, kb)))
                                pe.wait_ge(act_read.sem, act_read.at((L, half, "t", i)))
                                ob = 6 + (i // 8) % 2
                                key = (L, half, "ao", i // 8)
                                if i % 8 == 0:
                                    if ob in left:
                                        pe.wait_ge(*left[ob])
                                    left[ob] = out_read.after(key)
                                o = bank[ob][at:at + 64, (pr % 2) * S + b * P:(pr % 2) * S + (b + 1) * P]
                                for k, (g, kb) in enumerate(((0, 0), (0, 1), (1, b), (2, b))):
                                    m = nc.tensor.matmul(o, cv[:, kb, g, h * DH:(h + 1) * DH], probT[:, i % 2, k * P:(k + 1) * P],
                                                         start=k == 0, stop=k == 3)
                                m.then_inc(product_done.sem, product_done.next(key if i % 8 == 7 else (L, half, "o", i)))

                    order = list(attention_order(16))
                    chunk(0, 0)
                    memory_heads(L, c_qmT, MEMORY_STEPS[5])
                    for half in range(2):
                        for n in range(1, 8):
                            chunk(half, n)
                            if n <= 6:
                                turn(half, n - 1)
                        for g in range(3):
                            for s in range(2):
                                for t in range(2):
                                    pe.wait_ge(act_read.sem, act_read.at((L, half, "xt", s, g, t)))
                        dilated_heads(half, order[:HEADS_BEFORE])
                        chunk(half, 8)
                        dilated_heads(half, order[HEADS_BEFORE:-HEADS_AFTER])
                        if half == 0:
                            chunk(1, 0)
                        dilated_heads(half, order[-HEADS_AFTER:])
                out_product(L, li)
                hidden_from_rows(L, 4)

            for j in range(4):
                pe.wait_ge(tiles_read.sem, tiles_read.at((L, "zt", j)))
                n = j // 2
                for b in range(NB):
                    n_b = 2 * b + n
                    if j % 2 == 0:
                        if n_b in left:
                            pe.wait_ge(*left[n_b])
                        left[n_b] = act_read.after(("x", b, n))
                    for m in range(2):
                        k = 2 * (j % 2) + m
                        i = nc.tensor.transpose(bank[n_b][:, k * P:(k + 1) * P], split_t[:, j % 2, m * S + b * P:m * S + (b + 1) * P], ident)
                    if j % 2 == 1:
                        i.then_inc(product_done.sem, product_done.next(("x", b, n)))
                    elif b == NB - 1:
                        i.then_inc(product_done.sem, product_done.next(("xt", j)))

            for l in range(2):
                L = f"d{l}"
                w = A["w_in_2"][l]
                if l == 1:
                    for n in range(2):
                        stream_tiles((L, "mix"), ("d0", "dn"), n)

                def proj(nm, banks, c0, n, hidden=None):
                    token_major([(L, nm, b) for b in range(NB)], banks, [rows_of(w, kh * 512, 4, c0, n) for kh in range(2)], hT, hidden=hidden)
                proj("cq", CQ_BANK, C_DT, DTQ, hidden=(L, "mix"))
                proj("ck", CK_BANK, C_CKV, KVR)
                for u, n in enumerate((256, 256, 128)):
                    feature_major((L, "xbc", u), XBC_BANK[u], rows_of(w, 0, KT, C_XBC + u * 256, n), hT, reader=xbc_scaled)
                    if u == 0:
                        for b in range(NB):
                            pe.wait_ge(row_scales.sem, row_scales.at(((L, "mix"), b)))
                        if RMS_BANK in left:
                            pe.wait_ge(*left[RMS_BANK])
                        left[RMS_BANK] = act_read.after((L, "rms"))
                        for b in range(NB):
                            i = nc.tensor.matmul(bank[RMS_BANK][:, b * P:(b + 1) * P], S_(8 + b, 1).to_broadcast([P, P]), ident, start=True, stop=True)
                        i.then_inc(product_done.sem, product_done.next((L, "rms")))
                tiles = [(cqt, SSD_H + k * P, "cq") for k in range(3)] + [(ckt, k * P, "ck") for k in range(2)]
                for t in range(3):
                    for nm in ("cq", "ck"):
                        for b in range(NB):
                            pe.wait_ge(latent_normal.sem, latent_normal.at((L, nm, b)))
                    transposes((L, "lt", t), LATENT_BANK[t],
                               [a[:, b, at:at + P] for a, at, _ in tiles[2 * t:2 * t + 2] for b in range(NB)], r_ready)
                proj("uv", [2, 3], C_UV, UV)
                pe.wait_ge(ws_loaded, 16 * (l + 1))
                transposes((L, "wst"), 4, [ws_raw[:, h, :] for h in range(4)], dve_read)
                u, wq = unit(rows_of(A["mla_w_qb_2"][l], 0, 3, 0, 576))
                for n in range(2):
                    for b in range(NB):
                        n_b = QB_BANK[2 * n + b]
                        if n_b in left:
                            pe.wait_ge(*left[n_b])
                        left[n_b] = act_read.after((L, "qb", n, b))
                        o = bank[n_b]
                        for k in range(3):
                            if n + b == 0 and k % 2 == 0:
                                pe.wait_ge(r_ready.sem, r_ready.at((L, "lt", k // 2)))
                            i = mm3(o[:, 0:288], rT(5 + k, b), [a[:, k, n * 288:(n + 1) * 288] for a in wq], k == 0, k == 2)
                        i.then_inc(product_done.sem, product_done.next((L, "qb", n, b)))
                unit_done[u] = (L, "qb", 1, 1)
                pe.wait_ge(steps_ready.sem, steps_ready.at((L, "dtA")))
                dtA = S_(64, 12)
                if 1 in left:
                    pe.wait_ge(*left[1])
                left[1] = dve_read.after((L, "cum"))
                o = bank[1]
                nc.tensor.matmul(o[:, 0:12], K("upto"), dtA, start=True, stop=True)
                nc.tensor.matmul(o[:, 12:24], K("ones"), dtA, start=True, stop=True).then_inc(product_done.sem, product_done.next((L, "cum")))
                for c in range(NB):
                    for g in range(2):
                        n_b = RC_BANK[2 * c + g]
                        if n_b in left:
                            pe.wait_ge(*left[n_b])
                        left[n_b] = dve_read.after((L, "rc", c, g))
                        o = bank[n_b]
                        for h in range(3):
                            at = 64 + c * SSD_H + 3 * g + h
                            i = nc.tensor.matmul(o[:, h * P:(h + 1) * P], stat[:, at:at + 1].to_broadcast([P, P]), K("upto"),
                                                 start=True, stop=True)
                        i.then_inc(product_done.sem, product_done.next((L, "rc", c, g)))
                pe.wait_ge(gmlp_ready.sem, gmlp_ready.at((L, "v")))
                pe.wait_ge(dve_read.sem, dve_read.at((L, "wst")))
                if 1 in left:
                    pe.wait_ge(*left[1])
                left[1] = gating_read.after((L, "gm"))
                v_half = uv[:, :, 256:512].rearrange("p c (h d) -> p h c d", h=4)
                ov = bank[1][:, :].rearrange("p (h c d) -> p h c d", h=4, c=NB)
                for h in range(4):
                    i = nc.tensor.matmul(ov[:, h, :, :], wsT[:, h, :], v_half[:, h, :, :], start=True, stop=True)
                i.then_inc(product_done.sem, product_done.next((L, "gm")))
                pe.wait_ge(xbc_ready.sem, xbc_ready.at(L))
                for c in range(NB):
                    transposes((L, "xs", c), XS_BANK[c], [xbcT[:, t, 3 + c * P:3 + (c + 1) * P] for t in range(4 if c == 0 else 3)], act_read)
                if CB_BANK in left:
                    pe.wait_ge(*left[CB_BANK])
                for g in range(2):
                    if g == 1:
                        pe.wait_ge(product_done.sem, product_done.at((L, "cb", 0)))
                    for c in range(NB):
                        i = nc.tensor.matmul(bank[CB_BANK][:, g * S + c * P:g * S + (c + 1) * P],
                                             xbcT[64 * g:64 * g + 64, 3, 3 + c * P:3 + (c + 1) * P],
                                             xbcT[64 * g:64 * g + 64, 4, 3 + c * P:3 + (c + 1) * P], start=True, stop=True)
                    i.then_inc(product_done.sem, product_done.next((L, "cb", g)))
                proj("z", Z_BANK, C_Z, SSD_W)
                pe.wait_ge(state_in.sem, state_in.at(L))
                if 1 in left:
                    pe.wait_ge(*left[1])
                left[1] = act_read.after((L, "st"))
                o = bank[1]
                for g in range(2):
                    i = nc.tensor.matmul(o[64 * g:64 * g + 64, 0:192], b_tok[:, 64 * g:64 * g + 64], x_dec[:, 192 * g:192 * g + 192],
                                         start=True, stop=True)
                i.then_inc(product_done.sem, product_done.next((L, "st")))
                u, wkv = unit(rows_of(A["mla_w_kvb_2"][l], 0, 2, 0, 768))
                pe.wait_ge(r_ready.sem, r_ready.at((L, "lt", 2)))
                for n in range(2):
                    for b in range(NB):
                        n_b = KV_BANK[2 * n + b]
                        if n_b in left:
                            pe.wait_ge(*left[n_b])
                        left[n_b] = act_read.after((L, "kv", n, b))
                        o = bank[n_b]
                        for k in range(2):
                            i = mm3(o[:, 0:384], rT(8 + k, b), [a[:, k, n * 384:(n + 1) * 384] for a in wkv], k == 0, k == 1)
                        i.then_inc(product_done.sem, product_done.next((L, "kv", n, b)))
                unit_done[u] = (L, "kv", 1, 1)
                for c in range(NB):
                    for g in range(2):
                        pe.wait_ge(decay_ready.sem, decay_ready.at((L, c, g)))
                    n_b = STATE_BANK[c]
                    if n_b in left:
                        pe.wait_ge(*left[n_b])
                    left[n_b] = state_read.after((L, "yd", c))
                    for h in range(SSD_H):
                        i = nc.tensor.matmul(bank[n_b][:, h * DH:(h + 1) * DH], decay[:, c * SSD_H + h, :], xs[:, c, h * DH:(h + 1) * DH],
                                             start=True, stop=True)
                    i.then_inc(product_done.sem, product_done.next((L, "yd", c)))
                pe.wait_ge(act_read.sem, act_read.at((L, "st")))
                for g in range(2):
                    left[1] = state_read.after((L, "yo", g))
                    if g == 1:
                        pe.wait_ge(product_done.sem, product_done.at((L, "yo", 0)))
                    i = nc.tensor.matmul(bank[1][:, 192 * g:192 * g + 192], xbcT[64 * g:64 * g + 64, 4, 3 + P:3 + S],
                                         st_sb[64 * g:64 * g + 64, :], start=True, stop=True)
                    i.then_inc(product_done.sem, product_done.next((L, "yo", g)))

                pe.wait_ge(roped.sem, roped.at((L, "q")))
                left[CB_BANK] = decay_ready.after((L, NB - 1, 1))
                for t in range(3):
                    transposes((L, "qt", t), QT_BANK[t], [qtok[:, b, h * M_QK:(h + 1) * M_QK] for h in (2 * t, 2 * t + 1) for b in range(NB)], act_read)
                pe.wait_ge(roped.sem, roped.at((L, "k")))
                for t in range(3):
                    transposes((L, "kt", t), KT_BANK[t], [ktok[:, b, h * M_QK:(h + 1) * M_QK] for h in (2 * t, 2 * t + 1) for b in range(NB)], act_read)
                pe.wait_ge(gating_read.sem, gating_read.at((L, "gm")))
                transposes((L, "at"), GATING_BANK, [uv[:, b, k * P:(k + 1) * P] for k in range(2) for b in range(NB)], r_ready)

                for t in range(3):
                    pe.wait_ge(act_read.sem, act_read.at((L, "qt", t)))
                    pe.wait_ge(act_read.sem, act_read.at((L, "kt", t)))
                for what, h in attention_order(M_H):
                    if what == "s":
                        n_b = 4 + h % 2
                        if n_b in left:
                            pe.wait_ge(*left[n_b])
                        left[n_b] = dve_read.after((L, "s", h))
                        o = bank[n_b]
                        for b in range(NB):
                            n = (b + 1) * P
                            m = nc.tensor.matmul(o[:, b * P:b * P + n], mqT[0:M_QK, h, b * P:(b + 1) * P], mkvT[0:M_QK, h, 0:n],
                                                 start=True, stop=True)
                        m.then_inc(product_done.sem, product_done.next((L, "s", h)))
                    elif what == "t":
                        pe.wait_ge(probs_normal.sem, probs_normal.at((L, h)))
                        transposes((L, "t", h), 2 + h % 2, [prob[:, h % PROBS, k * P:(k + 1) * P] for k in range(3)], act_read)
                    else:
                        pe.wait_ge(act_read.sem, act_read.at((L, "t", h)))
                        ob, key = HEAD_BANK[h // 4], (L, "co", h // 4)
                        if h % 4 == 0:
                            if ob in left:
                                pe.wait_ge(*left[ob])
                            left[ob] = out_read.after(key)
                        o = bank[ob][64 * (h % 2):64 * (h % 2) + 64, (h % 4 // 2) * S:(h % 4 // 2 + 1) * S]
                        vh = kvtok[:, :, h * P + DH:(h + 1) * P]
                        nc.tensor.matmul(o, vh[:, 0, :], probT[:, h % 2, 0:S], start=True, stop=False)
                        m = nc.tensor.matmul(o[:, P:S], vh[:, 1, :], probT[:, h % 2, S:S + P], start=False, stop=True)
                        m.then_inc(product_done.sem, product_done.next(key if h in (3, 5) else (L, "o", h)))
                    if (what, h) == ("v", 0):
                        pe.wait_ge(mixer_out.sem, mixer_out.at((L, "b")))
                        transposes((L, "bt", 0), STATE_BANK[0], [y_b[:, b, k * P:(k + 1) * P] for k in range(2) for b in range(NB)], r_ready)
                        transposes((L, "bt", 1), STATE_BANK[1], [y_b[:, b, 2 * P:3 * P] for b in range(NB)], r_ready)
                for key in ((L, "at"), (L, "bt", 0), (L, "bt", 1)):
                    pe.wait_ge(r_ready.sem, r_ready.at(key))
                for j in range(2):
                    pe.wait_ge(out_read.sem, out_read.at((L, "co", j)))
                for n in range(2):
                    for kh in range(2):
                        token_major([(L, "wo", n, b) for b in range(NB)], [2 * n, 2 * n + 1],
                                    [rows_of(A["w_out_2"][l], kh * 512, 4, n * 512, 512)],
                                    lambda k, b: rT(4 * kh + k, b), reader=dve_read, opened=kh == 0, closed=kh == 1)
                        if (n, kh) == (1, 0):
                            stream_tiles((L, "mlp"), (L, "wo"), 0)
                stream_tiles((L, "mlp"), (L, "wo"), 1)

                def up(e):
                    for u in range(2):
                        feature_major((L, "up", e, u), (2 * e + u) % 4,
                                      rows_of(A["mlp_w1_2"][l], 0, KT, (2 * e + u) * 256, 256), hT,
                                      hidden=(L, "mlp") if e + u == 0 else None)

                def down(e):
                    for u in range(2):
                        pe.wait_ge(r_ready.sem, r_ready.at((L, "up", e, u)))
                    for n in range(2):
                        token_major([(L, "dn", n, b) for b in range(NB)], [4 + 2 * n, 5 + 2 * n],
                                    [rows_of(A["mlp_w2_2"][l], e * 512, 4, n * 512, 512)],
                                    lambda k, b: rT(4 * (e % 2) + k, b), reader=dve_read, opened=e == 0, closed=e == 7)
                    down_done[L, e] = unit_done[len(units) - 1]
                for e in range(9):
                    if e < 8:
                        up(e)
                    if e > 0:
                        down(e - 1)

        N_UNITS = len(units)

        @block.sync
        def _(sp):
            def load_unit(u):
                source, kts, n = units[u]
                sp.dma_start(w_raw[:, u % RAW_SLOTS, 0:kts * n].rearrange("p (k n) -> p k n", k=kts), source)\
                    .then_inc(w_loaded[u % RAW_SLOTS], 16)

            sp.dma_start(const[:, 0:P], A["const"][:, 0:P]).then_inc(ident_loaded, 16)
            load_unit(0)
            sp.dma_start(mem_in, A["mem"][0].rearrange("(b p) d -> p b d", p=P)).then_inc(mem_loaded, 16)
            xv = A["x"][0].rearrange("(c b a) d -> a b c d", a=4, b=4)
            for a in range(4):
                for b in range(4):
                    p0 = (a % 2) * 64 + b * 16
                    sp.dma_start(x_in[p0:p0 + 16, a // 2, :], xv[a, b]).then_inc(x_loaded, 16)
            load_unit(1)
            load_unit(2)
            sp.dma_start(const_once, A["const"][:, n_kept:]).then_inc(consts_loaded, 16)
            sp.dma_start(const[:, P:], A["const"][:, P:n_kept]).then_inc(consts_loaded, 16)
            at = 0
            for nm in ("norm_mix_g_2", "norm_mlp_g_2", "ssd_conv_w_2", "ssd_conv_b_2", "mla_q_norm_g_2", "mla_kv_norm_g_2",
                       "ssd_norm_g_2", "gmlp_b_s_2"):
                a = A[nm]
                flat = a.rearrange("l n -> (l n)") if len(a.shape) == 2 else a.rearrange("l k n -> (l k n)")
                n = flat.shape[0] // P
                sp.dma_start(rows_b[at:at + n, :], flat.rearrange("(k p) -> k p", p=P)).then_inc(rows_b_loaded, 16)
                at += n
            at = 0
            for nm in ("q_norm_g", "k_norm_g", "gmlp_v_norm_g_2", "ssd_dt_bias_2", "ssd_a_log_2", "ssd_d_2"):
                flat = A[nm].rearrange("l n -> (l n)")
                n = flat.shape[0]
                sp.dma_start(row[:, at:at + n], flat.partition_broadcast(P)).then_inc(rows_b_loaded, 16)
                at += n
            for u in range(RAW_SLOTS, N_UNITS):
                sp.wait_ge(w_split.sem, w_split.at(u - RAW_SLOTS))
                load_unit(u)
                for l, key in enumerate((("c0", "wo", 1, 1), ("d0", "wst"))):
                    if u == product_done.unit[key] + RAW_SLOTS + 1:
                        sp.wait_ge(product_done.sem, product_done.at(key))
                        sp.dma_start(ws_raw, A["gmlp_w_s_2"][l].rearrange("h t s -> t h s")).then_inc(ws_loaded, 16)
            sp.wait_ge(product_done.sem, product_done.at(("d1", "co", 1)))
            sp.dma_start(gf, A["final_norm_g_2"].partition_broadcast(P)).then_inc(gf_loaded, 16)
            for b in range(NB):
                sp.wait_ge(row_out.sem, row_out.at(b))
                sp.dma_start(out[0, b * P:(b + 1) * P, :], z[:, b, :]).then_inc(stored, 16)
            sp.wait_ge(stored, 16 * NB)

        @block.gpsimd
        def _(pool):
            at = 0
            for a in (A["ln_in_g"], A["ln_in_b"], A["ln_g"], A["ln_b"]):
                flat = a if len(a.shape) == 1 else a.rearrange("l n -> (l n)")
                n = flat.shape[0] // P
                pool.dma_start(rows_a[at:at + n, :], flat.rearrange("(k p) -> k p", p=P)).then_inc(rows_a_loaded, 16)
                at += n
            for u, (_, kts, n) in enumerate(units):
                pool.wait_ge(w_rounded.sem, w_rounded.at(u))
                s, m = u % SPLIT_SLOTS, kts * n
                nc.gpsimd.tensor_tensor(w_lo[:, s, 0:m], w_raw[:, u % RAW_SLOTS, 0:m], w_hi[:, s, 0:m].bitcast(F32),
                                               ALU.subtract).then_inc(w_split.sem, w_split.next(u))

        @block.scalar
        def _(act):
            def round_unit(u):
                _, kts, n = units[u]
                act.wait_ge(w_loaded[u % RAW_SLOTS], 16 * (u // RAW_SLOTS + 1))
                if u >= SPLIT_SLOTS:
                    act.wait_ge(product_done.sem, product_done.at(unit_done[u - SPLIT_SLOTS]))
                nc.scalar.activation(w_hi[:, u % SPLIT_SLOTS, 0:kts * n], w_raw[:, u % RAW_SLOTS, 0:kts * n], ACT.Copy).then_inc(w_rounded.sem, w_rounded.next(u))

            def round_weights(key, ahead=SPLIT_SLOTS):
                for u in range(w_rounded.made, min(N_UNITS, product_done.unit[key] + 1 + ahead)):
                    round_unit(u)

            def evac(key, dst, src, func=ACT.Copy, scale=1.0, bias=0.0):
                round_weights(key)
                act.wait_ge(product_done.sem, product_done.at(key))
                args = {} if func == ACT.Copy else {"bias": bias}
                nc.scalar.activation(dst, src, func, scale=scale, **args).then_inc(act_read.sem, act_read.next(key))

            def flat2(a):
                return a.rearrange("p a b -> p (a b)")

            def attend(L, steps):
                for what, i in steps:
                    if what == "s":
                        round_weights((L, "s", i))
                        act.wait_ge(product_done.sem, product_done.at((L, "s", i)))
                        if i >= PROBS:
                            act.wait_ge(product_done.sem, product_done.at((L, "t", i - PROBS)))
                        act.wait_ge(row_max.sem, row_max.at((L, i)))
                        o = bank[i % 2]
                        for b in range(NB):
                            ins = nc.scalar.activation(prob[:, i % PROBS, b * S:(b + 1) * S], o[:, b * S:(b + 1) * S], ACT.Exp,
                                                       bias=S_(16 + 4 * (i % PROBS) + b, 1), accum_out=S_(32 + 4 * (i % PROBS) + b, 1))
                            if b == 0:
                                ins.then_inc(exp_half.sem, exp_half.next((L, "s", i)))
                            else:
                                ins.then_inc(scores_read.sem, scores_read.next((L, "s", i)))
                    elif what == "t":
                        if i >= 2:
                            act.wait_ge(product_done.sem, product_done.at(out_key(L, i - 2)))
                        evac((L, "t", i), probT[:, i % 2, :], bank[2 + i % 2][:, :])

            def out_key(L, i):
                base, what = L
                if what == "m":
                    return (base, "mo") if i == 3 else (L, "o", i)
                return b_out_key(base, i // 4) if i % 4 == 3 else (L, "o", i)

            def gates(L, dst):
                evac((L, "qm"), flat2(dst), bank[0][:, :], scale=0.125)
                for u in range(5):
                    evac((L, "gate", u), flat2(gate[:, 2 * u:2 * u + 2, :]), bank[GATE_BANK[u]][:, :], ACT.Silu)

            def gates_and_memory(L, dst):
                evac((L, "qm"), flat2(dst), bank[0][:, :], scale=0.125)
                for u in range(4):
                    evac((L, "gate", u), flat2(gate[:, 2 * u:2 * u + 2, :]), bank[GATE_BANK[u]][:, :])
                    attend((L, "m"), MEMORY_STEPS[u])
                act.wait_ge(act_read.sem, act_read.at((L, "gate", 3)))
                nc.scalar.activation(flat2(gate[:, 0:8, :]), flat2(gate[:, 0:8, :]), ACT.Silu).then_inc(gate_ready.sem, gate_ready.next(L))
                evac((L, "gate", 4), flat2(gate[:, 8:10, :]), bank[GATE_BANK[4]][:, :], ACT.Silu)
                attend((L, "m"), MEMORY_STEPS[4])

            def hidden_hi(L, nxt, tiles, tiles_there):
                for j in range(4):
                    act.wait_ge(tiles_there.sem, tiles_there.at((L, "zt", j)))
                    nc.scalar.activation(flat2(h_hi[:, 2 * j:2 * j + 2, :]), tiles[:, j % 2, :], ACT.Copy)\
                        .then_inc(h_rounded.sem, h_rounded.next((nxt, j)))

            round_unit(0)
            for j in range(4):
                act.wait_ge(product_done.sem, product_done.at(("mem", "t", j)))
                nc.scalar.activation(flat2(r_hi[:, 2 * j:2 * j + 2, :]), bank[4 + j][:, :], ACT.Copy).then_inc(split_hi.sem, split_hi.next(("mem", j)))
            round_unit(1)
            evac(("cols", "a"), col_a[:], bank[0][:, 0:N_COL_A])
            act.wait_ge(x_loaded, 256)
            for b, n in BY_SCALAR:
                act.wait_ge(row_stats.sem, row_stats.at(("in", b)))
                nc.scalar.activation(z[:, b, n * 512:(n + 1) * 512], x_in[:, b, n * 512:(n + 1) * 512], ACT.Identity,
                                     scale=S_(8 + b, 1), bias=S_(10 + b, 1)).then_inc(rows_normal.sem, rows_normal.next(("in", b, n)))
            hidden_hi("in", "a0", split_t, tiles_read)
            act.wait_ge(ident_loaded, 16)
            act.wait_ge(consts_loaded, 32)
            nc.scalar.activation(flat2(dft_hi[:, :, :]), const_once, ACT.Copy)
            nc.scalar.activation(ident_r[:], ident, ACT.Copy).then_inc(tables_rounded.sem, tables_rounded.next(0))
            evac(("mem", "k"), flat2(mkT[:, :, :]), bank[4][:, :])
            evac(("mem", "v"), flat2(mv[:, :, :]), bank[5][:, :])

            for li, (kind, j) in enumerate(LAYERS):
                L = f"{kind}{j}"
                if li == 1:
                    evac(("cols", "b"), col_b[:], bank[3][:, 0:N_COL_B])
                if kind == "a":
                    gates_and_memory(L, qmT)
                    for g in range(4):
                        evac((L, "f1", g, 0), spectra[:, 0, g, :], bank[2 * (g % 3)][:, :])
                elif kind == "b":
                    for c in range(3):
                        for b in range(NB):
                            round_weights((L, "p", c, b))
                            act.wait_ge(product_done.sem, product_done.at((L, "p", c, b)))
                            nc.scalar.activation(qkv[:, b, c * 512:(c + 1) * 512], bank[2 * c + b][:, :], ACT.Copy).then_inc(act_read.sem, act_read.next((L, "p", c, b)))
                    gates(L, b_qmT)
                    for t in range(4):
                        evac((L, "qt", t), flat2(bqT[:, 2 * t:2 * t + 2, :]), bank[B_QK_BANK[t]][:, :], scale=0.125)
                    for t in range(2):
                        evac((L, "kt", t), flat2(bkT[:, 2 * t:2 * t + 2, :]), bank[B_QK_BANK[4 + t]][:, :])
                    attend((L, "h"), attention_order(MEM_HEADS + HEADS, LONG, "tsv"))
                else:
                    gates_and_memory(L, c_qmT)
                    chunks = [(s, g) for g in range(3) for s in range(2)] + [(2, g) for g in range(3)]

                    def dilated_heads(half, steps):
                        for what, i in steps:
                            if what == "s":
                                round_weights((L, half, "s", i))
                                act.wait_ge(product_done.sem, product_done.at((L, half, "s", i)))
                                if i >= PROBS:
                                    act.wait_ge(product_done.sem, product_done.at((L, half, "t", i - PROBS)))
                                act.wait_ge(dve_read.sem, dve_read.at((L, half, "s", i)))
                                nc.scalar.activation(prob[:, i % PROBS, :], masked[:, i % 2, :], ACT.Exp, scale=-1.0,
                                                            bias=S_(16 + 4 * (i % PROBS), 1), accum_out=S_(32 + 4 * (i % PROBS), 1)).then_inc(exp_done.sem, exp_done.next((L, half, i)))
                            elif what == "t":
                                if i >= 2:
                                    act.wait_ge(product_done.sem, product_done.at((L, half, "o", i - 2) if (i - 2) % 8 != 7 else (L, half, "ao", (i - 2) // 8)))
                                evac((L, half, "t", i), probT[:, i % 2, :], bank[2 + i % 2][:, :])

                    order = list(attention_order(16, LONG, "tsv"))
                    for half in range(2):
                        for n, (s, g) in enumerate(chunks):
                            if n == 8:
                                dilated_heads(half, order[:HEADS_BEFORE])
                            if s == 2:
                                for b in range(NB):
                                    evac((L, half, "p", s, g, b), cv[:, b, g, :], bank[CHUNK_BANKS[n][b]][:, :])
                            if 1 <= n <= 6:
                                s, g = chunks[n - 1]
                                for t in range(2):
                                    evac((L, half, "xt", s, g, t), flat2((cqT if s == 0 else ckT)[:, g, 2 * t:2 * t + 2, :]),
                                         bank[4 + t][:, :], scale=0.125 if s == 0 else 1.0)
                        dilated_heads(half, order[HEADS_BEFORE:])
                round_weights((L, "wo", 1, 0), SPLIT_SLOTS - 1)
                for b, n in BY_SCALAR:
                    act.wait_ge(row_stats.sem, row_stats.at((L, b)))
                    nc.scalar.activation(z[:, b, n * 512:(n + 1) * 512], bank[2 * n + b][:, :], ACT.Identity,
                                         scale=S_(8 + b, 1), bias=S_(10 + b, 1)).then_inc(rows_normal.sem, rows_normal.next((L, b, n)))
                if li < len(LAYERS) - 1:
                    hidden_hi(L, LAYER_NAMES[li + 1], split_t, tiles_read)
                else:
                    hidden_hi(L, LAYER_NAMES[li + 1], masked, tiles_gained)
                round_weights((L, "wo", 1, 1))

            def row_squares(squares, a, total, key):
                if square_sum.made:
                    act.wait_ge(square_sum.sem, square_sum.made)
                nc.scalar.activation(squares, a, ACT.Square, accum_out=total).then_inc(square_sum.sem, square_sum.next(key))

            def half_squares(L, key, b, n):
                cols = slice(n * 512, (n + 1) * 512)
                row_squares(z[:, b, cols], x[:, b, cols], S_(2 * b + n, 1), (L, key, b, n))

            for l in range(2):
                L = f"d{l}"
                if l == 0:
                    for n in range(2):
                        for b in range(NB):
                            evac(("x", b, n), x[:, b, n * 512:(n + 1) * 512], bank[2 * b + n][:, :])
                            act.wait_ge(act_read.sem, act_read.at(("x", b, n)))
                            half_squares(L, "mix", b, n)
                    act.wait_ge(rows_b_loaded, 16 * ROW_B_DMAS)
                    nc.scalar.activation(row[:, 652:664], row[:, 652:664], ACT.Exp).then_inc(a_exp.sem, a_exp.next(0))
                else:
                    round_weights(("d0", "dn", 1, 0), SPLIT_SLOTS - 1)
                    hidden_hi((L, "mix"), (L, "mix"), split_t, tiles_read)
                    round_weights(("d0", "dn", 1, 1))
                    for n in range(2):
                        for b in range(NB):
                            act.wait_ge(dve_read.sem, dve_read.at(("d0", "dn", n, b)))
                            half_squares(L, "mix", b, n)
                for b in range(NB):
                    act.wait_ge(row_scales.sem, row_scales.at(((L, "mix"), b)))
                    evac((L, "cq", b), cqt[:, b, :], bank[CQ_BANK[b]][:, 0:DTQ], ACT.Identity, scale=S_(8 + b, 1))
                for b in range(NB):
                    evac((L, "ck", b), ckt[:, b, :], bank[CK_BANK[b]][:, 0:KVR], ACT.Identity, scale=S_(8 + b, 1))
                evac((L, "rms"), masked[:, 0, 0:S], bank[RMS_BANK][:, 0:S])
                for nm, a, c0, n, s0 in (("cq", cqt, SSD_H, Q_RANK, 0), ("ck", ckt, 0, KV_RANK, 2)):
                    for b in range(NB):
                        act.wait_ge(act_read.sem, act_read.at((L, nm, b)))
                        row_squares(split_t[:, 1, 0:n], a[:, b, c0:c0 + n], S_(44 + s0 + b, 1), (L, nm, b))
                act.wait_ge(steps_in.sem, steps_in.at((L, "e")))
                nc.scalar.activation(S_(88, 12), S_(76, 12), ACT.Exp).then_inc(exp_small.sem, exp_small.next((L, "e")))

                gains = [col("cq", l)[:, k:k + 1] for k in range(3)] + [col("ckv", l)[:, k:k + 1] for k in range(2)]
                for t in range(3):
                    act.wait_ge(product_done.sem, product_done.at((L, "lt", t)))
                    for m in range(2 if t < 2 else 1):
                        ins = nc.scalar.activation(r_hi[:, 5 + 2 * t + m, :], bank[LATENT_BANK[t]][:, m * S:(m + 1) * S], ACT.Identity,
                                                   scale=gains[2 * t + m])
                    ins.then_inc(split_hi.sem, split_hi.next((L, "lt", t)))
                for b in range(NB):
                    evac((L, "uv", b), uv[:, b, :], bank[2 + b][:, :], ACT.Gelu_apprx_tanh, scale=S_(8 + b, 1))
                for b in range(NB):
                    act.wait_ge(act_read.sem, act_read.at((L, "uv", b)))
                    row_squares(split_t[:, 1, 0:256], uv[:, b, 256:512], S_(48 + b, 1), (L, "uv", b))
                for n in range(2):
                    for b in range(NB):
                        evac((L, "qb", n, b), qtok[:, b, n * 288:(n + 1) * 288], bank[QB_BANK[2 * n + b]][:, 0:288])
                act.wait_ge(conv_done.sem, conv_done.at(L))
                nc.scalar.activation(xbcT[:, :, 3:3 + S], conv, ACT.Silu).then_inc(xbc_ready.sem, xbc_ready.next(L))
                round_weights((L, "xs", 0))
                act.wait_ge(product_done.sem, product_done.at((L, "xs", 0)))
                nc.scalar.activation(b_tok, bank[XS_BANK[0]][:, SSD_W:512], ACT.Copy)
                nc.scalar.activation(xs[:, 0, :], bank[XS_BANK[0]][:, 0:SSD_W], ACT.Copy).then_inc(act_read.sem, act_read.next((L, "xs", 0)))
                evac((L, "xs", 1), xs[:, 1, :], bank[XS_BANK[1]][:, 0:SSD_W])
                act.wait_ge(steps_in.sem, steps_in.at((L, "end")))
                nc.scalar.activation(S_(136, 12), S_(124, 12), ACT.Exp).then_inc(exp_small.sem, exp_small.next((L, "end")))
                for c in range(NB):
                    for g in range(2):
                        round_weights((L, "rc", c, g))
                        act.wait_ge(dve_read.sem, dve_read.at((L, "rc", c, g)))
                        d3 = decay[:, c * SSD_H + 3 * g:c * SSD_H + 3 * g + 3, :]
                        nc.scalar.activation(d3, d3, ACT.Exp).then_inc(exp_seg.sem, exp_seg.next((L, c, g)))
                for b in range(NB):
                    evac((L, "z", b), zg[:, b, :], bank[Z_BANK[b]][:, 0:SSD_W], ACT.Silu, scale=S_(8 + b, 1))
                evac((L, "st"), st_sb, bank[1][:, 0:192])
                for n in range(2):
                    for b in range(NB):
                        evac((L, "kv", n, b), kvtok[:, b, n * 384:(n + 1) * 384], bank[KV_BANK[2 * n + b]][:, 0:384])
                for t in range(3):
                    evac((L, "qt", t), flat2(mqT[0:M_QK, 2 * t:2 * t + 2, :]), bank[QT_BANK[t]][0:M_QK, :], scale=float(M_QK) ** -0.5)
                for t in range(3):
                    evac((L, "kt", t), flat2(mkvT[0:M_QK, 2 * t:2 * t + 2, :]), bank[KT_BANK[t]][0:M_QK, :])
                act.wait_ge(product_done.sem, product_done.at((L, "at")))
                nc.scalar.activation(flat2(r_hi[:, 0:2, :]), bank[GATING_BANK][:, :], ACT.Copy).then_inc(split_hi.sem, split_hi.next((L, "at")))
                act.wait_ge(z_gated.sem, z_gated.at(L))
                for g in range(4):
                    row_squares(split_t[:, 1, 0:192], flat2(y_b)[:, 192 * g:192 * g + 192], S_(496 + g, 1), (L, "y", g))
                for what, h in attention_order(M_H, LONG, "tsv"):
                    if what == "s":
                        round_weights((L, "s", h))
                        act.wait_ge(product_done.sem, product_done.at((L, "s", h)))
                        if h >= PROBS:
                            act.wait_ge(product_done.sem, product_done.at((L, "t", h - PROBS)))
                        for b, (c0, c1) in enumerate(((0, P), (P, P + S))):
                            if b == 0:
                                act.wait_ge(row_max.sem, row_max.at((L, h)))
                            else:
                                act.wait_ge(dve_read.sem, dve_read.at((L, "s", h)))
                            nc.scalar.activation(prob[:, h % PROBS, c0:c1], masked[:, h % 2, c0:c1], ACT.Exp, scale=-1.0,
                                                        bias=S_(16 + 4 * (h % PROBS) + b, 1), accum_out=S_(32 + 4 * (h % PROBS) + b, 1)).then_inc(exp_done.sem, exp_done.next((L, h, b)))
                    elif what == "t":
                        if h >= 2:
                            act.wait_ge(product_done.sem, product_done.at((L, "co", 0) if h - 2 == 3 else (L, "o", h - 2)))
                        evac((L, "t", h), probT[:, h % 2, 0:384], bank[2 + h % 2][:, 0:384])
                    elif h == 0:
                        act.wait_ge(product_done.sem, product_done.at((L, "bt", 0)))
                        for m in range(2):
                            ins = nc.scalar.activation(r_hi[:, 2 + m, :], bank[STATE_BANK[0]][:, m * S:(m + 1) * S], ACT.Identity, scale=col("ssd", l)[:, m:m + 1])
                        ins.then_inc(split_hi.sem, split_hi.next((L, "bt", 0)))
                        act.wait_ge(product_done.sem, product_done.at((L, "bt", 1)))
                        nc.scalar.activation(r_hi[:, 4, :], bank[STATE_BANK[1]][:, 0:S], ACT.Identity, scale=col("ssd", l)[:, 2:3]).then_inc(split_hi.sem, split_hi.next((L, "bt", 1)))
                    elif h == 3:
                        act.wait_ge(product_done.sem, product_done.at((L, "co", 0)))
                        nc.scalar.activation(flat2(r_hi[:, 5:7, :]), bank[HEAD_BANK[0]][:, :], ACT.Copy).then_inc(split_hi.sem, split_hi.next((L, "co", 0)))
                    elif h == 5:
                        act.wait_ge(product_done.sem, product_done.at((L, "co", 1)))
                        nc.scalar.activation(r_hi[:, 7, :], bank[HEAD_BANK[1]][:, 0:S], ACT.Copy).then_inc(split_hi.sem, split_hi.next((L, "co", 1)))
                round_weights((L, "wo", 1, 0), SPLIT_SLOTS - 1)
                hidden_hi((L, "mlp"), (L, "mlp"), split_t, tiles_read)
                round_weights((L, "wo", 1, 1))
                for n in range(2):
                    for b in range(NB):
                        act.wait_ge(dve_read.sem, dve_read.at((L, "wo", n, b)))
                        half_squares(L, "mlp", b, n)
                for e in range(8):
                    for u in range(2):
                        t = (2 * e + u) % 4
                        round_weights((L, "up", e, u))
                        act.wait_ge(product_done.sem, product_done.at((L, "up", e, u)))
                        if 2 * e + u >= 2:
                            act.wait_ge(r_ready.sem, r_ready.at((L, "up", (2 * e + u - 2) // 2, u)))
                        relu = masked[:, u, :]
                        nc.scalar.activation(relu, bank[t][:, :], ACT.Relu).then_inc(act_read.sem, act_read.next((L, "up", e, u)))
                        act.wait_ge(act_read.sem, act_read.at((L, "up", e, u)))
                        if e >= 2:
                            act.wait_ge(product_done.sem, product_done.at(down_done[L, e - 2]))
                        t0 = 4 * (e % 2) + 2 * u
                        nc.scalar.activation(flat2(r_hi[:, t0:t0 + 2, :]), relu, ACT.Square).then_inc(square_hi.sem, square_hi.next((L, "up", e, u)))
            round_weights(("d1", "dn", 1, 1))
            for n in range(2):
                for b in range(NB):
                    act.wait_ge(dve_read.sem, dve_read.at(("d1", "dn", n, b)))
                    half_squares("end", "end", b, n)

        @block.vector
        def _(dve):
            v = nc.vector

            def link(ins):
                ins.then_inc(vector_step.sem, vector_step.next(vector_step.made))
                dve.wait_ge(vector_step.sem, vector_step.made)

            def tt(o, a, b, op):
                link(v.tensor_tensor(o, a, b, op))

            def ts(o, a, s1, s2, op0, op1=ALU.bypass):
                link(v.tensor_scalar(o, a, s1, None, op0) if s2 is None else v.tensor_scalar(o, a, s1, s2, op0, op1))

            def stt(o, a, s, b, op0, op1):
                link(v.scalar_tensor_tensor(o, a, s, b, op0, op1))

            MUL, ADD, SUB = ALU.mult, ALU.add, ALU.subtract

            def rsqrt(y, a, t):
                ts(y.bitcast(I32), a.bitcast(I32), 1, None, ALU.logical_shift_right)
                ts(y.bitcast(I32), y.bitcast(I32), -1.0, float(0x5F3759DF), MUL, ADD)
                for n in range(3):
                    tt(t, y, y, MUL)
                    stt(t, a, -0.5, t, MUL, MUL)
                    stt(y, t, 1.5, y, ADD, MUL)

            def flat2(a):
                return a.rearrange("p a b -> p (a b)")

            def split(hi, lo, value):
                link(v.tensor_copy(hi, value))
                return v.tensor_tensor(lo, value, hi.bitcast(F32), SUB)

            def split_hidden(L, nxt, b0, gain, shift, natural=False, js=range(4), next_gain=None):
                tiles = split_t if next_gain is None else masked
                for j in range(js[0], js[-1] + 2):
                    if j in js:
                        dve.wait_ge(product_done.sem, product_done.at((L, "zt", j)))
                        if j >= 2:
                            dve.wait_ge(h_ready.sem, h_ready.at((nxt, j - 2)))
                        if next_gain is not None and j >= 2:
                            dve.wait_ge(product_done.sem, product_done.at(("xt", 0) if j == 2 else ("x", 1, 0)))
                        t = split_t[:, j % 2, :]
                        for m in range(2):
                            k = 2 * j + m
                            src, dst = bank[b0 + j][:, m * S:(m + 1) * S], t[:, m * S:(m + 1) * S]
                            if natural:
                                src = src.rearrange("p (a b c) -> p a b c", a=4, b=4)
                                dst = dst.rearrange("p (c b a) -> p a b c", a=4, b=4)
                            if shift is None:
                                ins = v.tensor_scalar(dst, src, gain[:, k:k + 1], None, MUL)
                            else:
                                ins = v.tensor_scalar(dst, src, gain[:, k:k + 1], shift[:, k:k + 1], MUL, ADD)
                        ins.then_inc(tiles_read.sem, tiles_read.next((L, "zt", j)))
                        if next_gain is not None:
                            dve.wait_ge(tiles_read.sem, tiles_read.made)
                            for m in range(2):
                                half = slice(m * S, (m + 1) * S)
                                ins = v.tensor_scalar(masked[:, j % 2, half], t[:, half], next_gain[:, 2 * j + m:2 * j + m + 1], None, MUL)
                            ins.then_inc(tiles_gained.sem, tiles_gained.next((L, "zt", j)))
                    if j - 1 in js:
                        pair = slice(2 * j - 2, 2 * j)
                        there = tiles_read if next_gain is None else tiles_gained
                        dve.wait_ge(there.sem, there.at((L, "zt", j - 1)))
                        dve.wait_ge(h_rounded.sem, h_rounded.at((nxt, j - 1)))
                        v.tensor_tensor(flat2(h_lo[:, pair, :]), tiles[:, (j - 1) % 2, :], flat2(h_hi[:, pair, :]).bitcast(F32), SUB)\
                            .then_inc(h_ready.sem, h_ready.next((nxt, j - 1)))
                dve.wait_ge(h_ready.sem, h_ready.made)

            def rsqrt_col(y, a, t):
                ts(y.bitcast(I32), a.bitcast(I32), -0.5, float(0x5F3759DF - 2 ** 31), MUL, ADD)
                for three in (3.0, 12.0, 768.0):
                    stt(t, y, a, y, MUL, MUL)
                    if three < 768.0:
                        stt(y, t, three, y, SUB, MUL)
                return v.scalar_tensor_tensor(y, t, three, y, SUB, MUL)

            def row_norm(L, b, factor=1.0):
                mean, var = S_(152 + 2 * b, 1), S_(153 + 2 * b, 1)
                link(v.bn_aggr(S_(152 + 2 * b, 2), S_(128 + 12 * b, 12)))
                ts(S_(4 + b, 1), var, 2.0 ** 26, 1e-5 / factor ** 2 * 2.0 ** 26, MUL, ADD)
                link(rsqrt_col(S_(8 + b, 1), S_(4 + b, 1), S_(6 + b, 1)))
                v.scalar_tensor_tensor(S_(10 + b, 1), mean, -1.0, S_(8 + b, 1), MUL, MUL).then_inc(row_stats.sem, row_stats.next((L, b)))

            def normal_half(L, src):
                v.tensor_scalar(z[:, 1, 0:512], src, S_(154, 1), S_(9, 1), SUB, MUL).then_inc(rows_normal_v.sem, rows_normal_v.next(L))

            def softmax_max(L, i, src, key):
                dve.wait_ge(product_done.sem, product_done.at(key))
                v.tensor_reduce(S_(16 + 4 * (i % PROBS), 2), src.rearrange("p (b k) -> p b k", b=NB), AX.X, ALU.max, negate=True).then_inc(row_max.sem, row_max.next((L, i)))

            def gated(L, j, key, src, parts=range(3)):
                t, pair = split_t[:, 0, :], slice(2 * j, 2 * j + 2)
                for part in parts:
                    if part == 0:
                        dve.wait_ge(product_done.sem, product_done.at(key))
                        v.scalar_tensor_tensor(t, src, 1.0 / ALPHA, flat2(gate[:, pair, :]), MUL, MUL).then_inc(out_read.sem, out_read.next(key))
                    elif part == 1:
                        dve.wait_ge(out_read.sem, out_read.at(key))
                        v.tensor_copy(flat2(r_hi[:, pair, :]), t).then_inc(gated_hi.sem, gated_hi.next((L, j)))
                    else:
                        dve.wait_ge(gated_hi.sem, gated_hi.at((L, j)))
                        v.tensor_tensor(flat2(r_lo[:, pair, :]), t, flat2(r_hi[:, pair, :]).bitcast(F32), SUB).then_inc(r_ready.sem, r_ready.next((L, j)))
                        dve.wait_ge(r_ready.sem, r_ready.made)

            def parts_after(i, n, last):
                if i == last:
                    return range(3)
                return [part for part in range(3) if i >= n - 1 + part and (i - part) % n == n - 1]

            def normalise(i, parts):
                n = len(parts)
                link(v.reciprocal(S_(52 + 2 * (i % PROBS), n), S_(32 + 4 * (i % PROBS), n)))
                return S_(52 + 2 * (i % PROBS), n)

            def attend(L, n, lags, outs):
                for what, i in attention_order(n, (NORMAL_LAG, lags[1]), "tsv"):
                    if what == "s":
                        softmax_max(L, i, bank[i % 2][:, :], (L, "s", i))
                    elif what == "t":
                        dve.wait_ge(scores_read.sem, scores_read.at((L, "s", i)))
                        r = normalise(i, range(NB))
                        for b in range(NB):
                            p_ = prob[:, i % PROBS, b * S:(b + 1) * S]
                            ins = v.tensor_scalar(p_, p_, r[:, b:b + 1], None, MUL)
                            if b == 1:
                                ins.then_inc(probs_normal.sem, probs_normal.next((L, i)))
                    else:
                        outs(i)

            for j in range(4):
                dve.wait_ge(split_hi.sem, split_hi.at(("mem", j)))
                v.tensor_tensor(flat2(r_lo[:, 2 * j:2 * j + 2, :]), bank[4 + j][:, :], flat2(r_hi[:, 2 * j:2 * j + 2, :]).bitcast(F32), SUB)\
                    .then_inc(r_ready.sem, r_ready.next(("mem", "t", j)))
            dve.wait_ge(x_loaded, 256)
            for b in range(NB):
                for n in range(2):
                    link(v.bn_stats(S_(128 + 12 * b + 6 * n, 6), x_in[:, b, n * 512:(n + 1) * 512]))
                row_norm("in", b)
            normal_half("in", x_in[:, 1, 0:512])
            dve.wait_ge(act_read.sem, act_read.at(("cols", "a")))
            split_hidden("in", "a0", 0, *ln_cols(0))
            dve.wait_ge(consts_loaded, 32)
            dve.wait_ge(tables_rounded.sem, tables_rounded.at(0))
            v.tensor_tensor(flat2(dft_lo[:, :, :]), const_once, flat2(dft_hi[:, :, :]).bitcast(F32), SUB).then_inc(tables_split.sem, tables_split.next("lo"))

            for li, (kind, j) in enumerate(LAYERS):
                L = f"{kind}{j}"

                def mem_out(i):
                    if i == 3:
                        dve.wait_ge(gate_ready.sem, gate_ready.at(L))
                        dve.wait_ge(act_read.sem, act_read.at((L, "gate", 4)))
                        gated(L, 4, (L, "mo"), bank[7][:, :])
                if kind == "a":
                    attend((L, "m"), MEM_HEADS, SHORT, mem_out)
                    for g in range(4):
                        dve.wait_ge(product_done.sem, product_done.at((L, "f1", g, 1)))
                        v.tensor_copy(spectra[:, 1, g, :], bank[2 * (g % 3) + 1][:, :]).then_inc(dve_read.sem, dve_read.next((L, "f1", g, 1)))
                        dve.wait_ge(dve_read.sem, dve_read.made)
                    for t in range(4):
                        gated(L, t, (L, "f2", t), bank[2 * (t % 2)][:, :])
                elif kind == "b":
                    dve.wait_ge(rows_b_loaded, 16 * ROW_B_DMAS)
                    for n, g in enumerate((q_gain, k_gain)):
                        cos_t = K("axial_cos").rearrange("p (b d) -> p b d", b=NB)
                        sin_t = K("axial_sin").rearrange("p (b d) -> p b d", b=NB)
                        gb = g.unsqueeze(1).to_broadcast([P, NB, DH])
                        tt(gcos[:, n, :, :], cos_t, gb, MUL)
                        g4 = g.rearrange("p (h r e) -> p h r e", h=2, r=2)
                        for b in range(NB):
                            s4 = sin_t[:, b, :].rearrange("p (h r e) -> p h r e", h=2, r=2)
                            o4 = gsin[:, n, b, :].rearrange("p (h r e) -> p h r e", h=2, r=2)
                            for r in range(2):
                                tt(o4[:, :, r, :], s4[:, :, r, :], g4[:, :, 1 - r, :], MUL)
                    ssq = S_(160, 40)
                    for b in range(NB):
                        for c in range(3):
                            dve.wait_ge(act_read.sem, act_read.at((L, "p", c, b)))
                        tt(b_sq, qkv[:, b, 0:1280], qkv[:, b, 0:1280], MUL)
                        link(v.tensor_reduce(ssq[:, 20 * b:20 * b + 20], b_sq.rearrange("p (h d) -> p h d", d=DH), AX.X, ALU.add))
                    ts(ssq, ssq, 1.0 / DH, 1e-6, MUL, ADD)
                    rs = S_(200, 40)
                    rsqrt(rs, ssq, S_(240, 40))
                    for n, (c0, nh) in enumerate(((0, HEADS), (D, KV_HEADS))):
                        for b in range(NB):
                            src = qkv[:, b, c0:c0 + nh * DH]
                            rot = b_rot[:, 0:nh * DH]
                            s5 = src.rearrange("p (h f r e) -> p h f r e", f=2, r=2, e=16)
                            r5 = rot.rearrange("p (h f r e) -> p h f r e", f=2, r=2, e=16)
                            t5 = gsin[:, n, b, :].rearrange("p (f r e) -> p f r e", f=2, r=2)
                            for r in range(2):
                                for f in range(2):
                                    tt(r5[:, :, f, r, :], s5[:, :, f, 1 - r, :], t5[:, f, r, :].unsqueeze(1).to_broadcast([P, nh, 16]), MUL)
                            s3 = src.rearrange("p (h d) -> p h d", d=DH)
                            tt(s3, s3, gcos[:, n, b, :].unsqueeze(1).to_broadcast([P, nh, DH]), MUL)
                            tt(src, src, rot, ADD)
                            rb = rs[:, 20 * b + (0 if n == 0 else HEADS):20 * b + (HEADS if n == 0 else 20)]
                            if n == 0:
                                v.tensor_tensor(s3, s3, rb.unsqueeze(2).to_broadcast([P, nh, DH]), MUL).then_inc(roped.sem, roped.next((L, "q", b)))
                                dve.wait_ge(roped.sem, roped.made)
                            else:
                                for r in range(2):
                                    ins = v.tensor_tensor(k_dup[:, b, :, r, :], s3, rb.unsqueeze(2).to_broadcast([P, nh, DH]), MUL)
                                    if r == 1:
                                        ins.then_inc(roped.sem, roped.next((L, "k", b)))
                                        dve.wait_ge(roped.sem, roped.made)
                                    else:
                                        link(ins)

                    def head_out(i):
                        parts = parts_after(i, 4, MEM_HEADS + HEADS - 1)
                        group = (i + 1) // 4 - 1
                        if parts:
                            if i == 3:
                                dve.wait_ge(act_read.sem, act_read.at((L, "gate", 4)))
                            gated(L, group - 1 if group else 4, b_out_key(L, group), bank[B_OUT_BANK[group]][:, :], parts)
                    attend((L, "h"), MEM_HEADS + HEADS, LONG, head_out)
                else:
                    attend((L, "m"), MEM_HEADS, SHORT, mem_out)
                    cos_t = K("line_cos").rearrange("p (b d) -> p b d", b=NB)
                    sin_t = K("line_sin").rearrange("p (b d) -> p b d", b=NB)
                    mask = K("dilated_mask").rearrange("p (b k) -> p b k", b=NB)
                    for half in range(2):
                        chunks = [(s, g) for g in range(3) for s in range(2)]
                        for n, (s, g) in enumerate(chunks):
                            for b in range(NB):
                                dve.wait_ge(product_done.sem, product_done.at((L, half, "p", s, g, b)))
                                if (half, n) > (0, 0):
                                    ph, pn = (half, n - 1) if n else (0, 5)
                                    dve.wait_ge(product_done.sem, product_done.at((L, ph, "xt", *chunks[pn], 1)))
                                src = bank[CHUNK_BANKS[n][b]][:, :]
                                s4 = src.rearrange("p (h r e) -> p h r e", r=2, e=32)
                                s3 = src.rearrange("p (h d) -> p h d", d=DH)
                                dst = c_rot[:, b, :]
                                d4 = dst.rearrange("p (h r e) -> p h r e", r=2, e=32)
                                c3 = c_tmp.rearrange("p (h e) -> p h e", e=32)
                                tt(dst.rearrange("p (h d) -> p h d", d=DH), s3, cos_t[:, b, :].unsqueeze(1).to_broadcast([P, 8, DH]), MUL)
                                for r in range(2):
                                    sr = sin_t[:, b, r * 32:(r + 1) * 32].unsqueeze(1).to_broadcast([P, 8, 32])
                                    ins = v.tensor_tensor(c3, s4[:, :, 1 - r, :], sr, MUL)
                                    if r:
                                        ins.then_inc(dve_read.sem, dve_read.next((L, half, "p", s, g, b)))
                                        dve.wait_ge(dve_read.sem, dve_read.made)
                                    else:
                                        link(ins)
                                    ins = v.tensor_tensor(d4[:, :, r, :], d4[:, :, r, :], c3, ADD)
                                    if r:
                                        ins.then_inc(roped.sem, roped.next((L, half, s, g, b)))
                                        dve.wait_ge(roped.sem, roped.made)
                                    else:
                                        link(ins)
                        for what, i in attention_order(16, (NORMAL_LAG, LONG[1]), "tsv"):
                            if what == "s":
                                dve.wait_ge(product_done.sem, product_done.at((L, half, "s", i)))
                                if i >= 2:
                                    dve.wait_ge(exp_done.sem, exp_done.at((L, half, i - 2)))
                                v.tensor_tensor_reduce(out=masked[:, i % 2, :], in0=bank[i % 2][:, :], in1=mask[:, i % 2, :], scale=-1.0,
                                                          scalar=BIG, op0=ADD, op1=ALU.min, accum_out=S_(16 + 4 * (i % PROBS), 1)).then_inc(dve_read.sem, dve_read.next((L, half, "s", i)))
                            elif what == "t":
                                dve.wait_ge(exp_done.sem, exp_done.at((L, half, i)))
                                r = normalise(i, range(1))
                                p_ = prob[:, i % PROBS, :]
                                v.tensor_scalar(p_, p_, r, None, MUL).then_inc(probs_normal.sem, probs_normal.next((L, half, i)))
                            else:
                                parts = parts_after(i, 8, 15)
                                j = (i + 1) // 8 - 1
                                if parts:
                                    gated(L, 2 * half + j, (L, half, "ao", j), bank[6 + j][:, :], parts)
                for n in range(2):
                    for b in range(NB):
                        dve.wait_ge(product_done.sem, product_done.at((L, "wo", n, b)))
                        link(v.bn_stats(S_(128 + 12 * b + 6 * n, 6), bank[2 * n + b][:, :]))
                        if n == 1:
                            row_norm(L, b, factor=ALPHA)
                normal_half(L, bank[1][:, :])
                if li < len(LAYERS) - 1:
                    split_hidden(L, LAYER_NAMES[li + 1], 4, *ln_cols(li + 1))
                else:
                    dve.wait_ge(act_read.sem, act_read.at(("cols", "b")))
                    split_hidden(L, LAYER_NAMES[li + 1], 4, *ln_cols(li + 1), natural=True, next_gain=col("mix", 0))

            def add_rows(key, n, b, o, factor=None):
                dve.wait_ge(product_done.sem, product_done.at(key))
                xx = x[:, b, n * 512:(n + 1) * 512]
                ins = v.tensor_tensor(xx, xx, o[:, :], ADD) if factor is None else v.scalar_tensor_tensor(xx, o[:, :], factor, xx, MUL, ADD)
                ins.then_inc(dve_read.sem, dve_read.next(key))

            def rms(L, key, b):
                a = S_(4 + b, 1)
                dve.wait_ge(square_sum.sem, square_sum.at((L, key, b, 0)))
                ts(a, S_(2 * b, 1), 1e-6 * D, None, ADD)
                dve.wait_ge(square_sum.sem, square_sum.at((L, key, b, 1)))
                ts(a, a, S_(2 * b + 1, 1), 2.0 ** 26 / D, ADD, MUL)
                return rsqrt_col(S_(8 + b, 1), a, S_(6 + b, 1))

            for l in range(2):
                L = f"d{l}"
                if l == 1:
                    split_hidden((L, "mix"), (L, "mix"), 4, col("mix", l), None)
                for b in range(NB):
                    rms(L, "mix", b).then_inc(row_scales.sem, row_scales.next(((L, "mix"), b)))
                if l == 0:
                    dve.wait_ge(a_exp.sem, a_exp.at(0))
                    ts(row[:, 652:664], row[:, 652:664], -1.0, None, MUL)
                link(v.memset(xbcT[:, :, 0:3], 0.0))
                for nm in ("cq", "ck"):
                    for b in range(NB):
                        dve.wait_ge(square_sum.sem, square_sum.at((L, nm, b)))
                ts(S_(104, 2), S_(44, 2), 1.0 / Q_RANK, 1e-6, MUL, ADD)
                ts(S_(106, 2), S_(46, 2), 1.0 / KV_RANK, 1e-6, MUL, ADD)
                rsqrt(S_(108, 4), S_(104, 4), S_(112, 4))
                for i, (nm, a, c0, n) in enumerate((("cq", cqt, SSD_H, Q_RANK), ("ck", ckt, 0, KV_RANK))):
                    for b in range(NB):
                        v.tensor_scalar(a[:, b, c0:c0 + n], a[:, b, c0:c0 + n], S_(108 + 2 * i + b, 1), None, MUL).then_inc(latent_normal.sem, latent_normal.next((L, nm, b)))
                        dve.wait_ge(latent_normal.sem, latent_normal.made)
                val, low = S_(256, 12), S_(76, 12)
                tt(val.rearrange("p (b h) -> p b h", b=NB), cqt[:, :, 0:SSD_H], dt_bias[:, l, :].unsqueeze(1).to_broadcast([P, NB, SSD_H]), ADD)
                v.scalar_tensor_tensor(low, val, -1.0, val, MUL, ALU.min).then_inc(steps_in.sem, steps_in.next((L, "e")))
                dve.wait_ge(steps_in.sem, steps_in.made)
                kr, kt_, ku = S_(320, 64), S_(384, 64), ckt[:, :, KV_RANK:KVR]
                cos_m = K("mla_cos").rearrange("p (b d) -> p b d", b=NB)
                sin_m = K("mla_sin").rearrange("p (b d) -> p b d", b=NB)
                kr3, kt3 = kr.rearrange("p (b d) -> p b d", b=NB), kt_.rearrange("p (b d) -> p b d", b=NB)
                tt(kr3, ku, cos_m, MUL)
                for r in range(2):
                    tt(kt3[:, :, 16 * r:16 * r + 16], ku[:, :, 16 - 16 * r:32 - 16 * r], sin_m[:, :, 16 * r:16 * r + 16], MUL)
                tt(kr, kr, kt_, ADD)
                dve.wait_ge(act_read.sem, act_read.at((L, "rms")))
                for u, n in enumerate((2, 2, 1)):
                    dve.wait_ge(product_done.sem, product_done.at((L, "xbc", u)))
                    v.tensor_tensor(xbcT[:, 2 * u:2 * u + n, 3:3 + S], bank[XBC_BANK[u]][:, 0:n * S].rearrange("p (t s) -> p t s", t=n),
                                    masked[:, 0, 0:S].unsqueeze(1).to_broadcast([P, n, S]), MUL).then_inc(xbc_scaled.sem, xbc_scaled.next((L, "xbc", u)))
                cw, cb = col("conv_w", l), col("conv_b", l)

                def convolve(tiles):
                    for t in tiles:
                        dve.wait_ge(xbc_scaled.sem, xbc_scaled.at((L, "xbc", t // 2)))
                        ts(conv[:, t, :], xbcT[:, t, 3:3 + S], cw[:, 15 + t:16 + t], cb[:, t:t + 1], MUL, ADD)
                        for k in range(3):
                            ins = v.scalar_tensor_tensor(conv[:, t, :], xbcT[:, t, k:k + S], cw[:, 5 * k + t:5 * k + t + 1], conv[:, t, :], MUL, ADD)
                            if (t, k) == (4, 2):
                                ins.then_inc(conv_done.sem, conv_done.next(L))
                            else:
                                link(ins)
                convolve(range(3))
                gains = [col("cq", l)[:, k:k + 1] for k in range(3)] + [col("ckv", l)[:, k:k + 1] for k in range(2)]
                for t in range(3):
                    dve.wait_ge(split_hi.sem, split_hi.at((L, "lt", t)))
                    for m in range(2 if t < 2 else 1):
                        k = 5 + 2 * t + m
                        ins = v.scalar_tensor_tensor(r_lo[:, k, :], bank[LATENT_BANK[t]][:, m * S:(m + 1) * S], gains[2 * t + m],
                                                     r_hi[:, k, :].bitcast(F32), MUL, SUB)
                    ins.then_inc(r_ready.sem, r_ready.next((L, "lt", t)))
                convolve(range(3, 5))
                dve.wait_ge(exp_small.sem, exp_small.at((L, "e")))
                e, w1, w2, q = S_(88, 12), S_(276, 12), S_(288, 12), S_(300, 12)
                ts(w1, e, 2.0, None, ADD)
                link(v.reciprocal(w1, w1))
                tt(w1, w1, e, MUL)
                tt(w2, w1, w1, MUL)
                ts(q, w2, 1.0 / 17, None, MUL)
                for n in (15, 13, 11, 9, 7, 5, 3):
                    stt(q, q, 1.0 / n, w2, ADD, MUL)
                stt(q, q, 1.0, w1, ADD, MUL)
                dt = S_(452, 12)
                ts(val, val, 0.0, None, ALU.max)
                stt(dt, q, 2.0, val, MUL, ADD)
                v.tensor_tensor(S_(64, 12).rearrange("p (b h) -> p b h", b=NB), dt.rearrange("p (b h) -> p b h", b=NB), a_neg[:, l, :].unsqueeze(1).to_broadcast([P, NB, SSD_H]), MUL).then_inc(steps_ready.sem, steps_ready.next((L, "dtA")))
                dve.wait_ge(product_done.sem, product_done.at((L, "wst")))
                v.tensor_tensor(wsT, bank[4][:, :].rearrange("p (h t) -> p h t", h=4), K("upto").unsqueeze(1).to_broadcast([P, 4, P]), MUL).then_inc(dve_read.sem, dve_read.next((L, "wst")))
                for b in range(NB):
                    dve.wait_ge(square_sum.sem, square_sum.at((L, "uv", b)))
                ts(S_(268, 2), S_(48, 2), 1.0 / 256, 1e-6, MUL, ADD)
                rsqrt(S_(270, 2), S_(268, 2), S_(272, 2))
                for b in range(NB):
                    vv = uv[:, b, 256:512]
                    ins = v.scalar_tensor_tensor(vv, vv, S_(270 + b, 1), gv[:, l, :], MUL, MUL)
                ins.then_inc(gmlp_ready.sem, gmlp_ready.next((L, "v")))
                dve.wait_ge(product_done.sem, product_done.at((L, "cum")))
                cum = S_(464, 24)
                v.tensor_copy(cum, bank[1][:, 0:24]).then_inc(dve_read.sem, dve_read.next((L, "cum")))
                dve.wait_ge(dve_read.sem, dve_read.made)
                v.tensor_copy(S_(130, 6), cum[:, 6:12])
                v.tensor_tensor(S_(124, 6), cum[:, 12:18], cum[:, 0:6], SUB).then_inc(steps_in.sem, steps_in.next((L, "end")))
                for c in range(NB):
                    for g in range(2):
                        dve.wait_ge(product_done.sem, product_done.at((L, "rc", c, g)))
                        for h in range(3):
                            i = c * SSD_H + 3 * g + h
                            ins = v.scalar_tensor_tensor(decay[:, i, :], bank[RC_BANK[2 * c + g]][:, h * P:(h + 1) * P], cum[:, i:i + 1],
                                                         K("future_st"), SUB, ADD)
                        ins.then_inc(dve_read.sem, dve_read.next((L, "rc", c, g)))
                dve.wait_ge(product_done.sem, product_done.at((L, "gm")))
                og = bank[1][:, :].rearrange("p (h c d) -> p h c d", h=4, c=NB)
                for k in range(4):
                    uu = uv[:, :, k * DH:(k + 1) * DH]
                    ins = v.scalar_tensor_tensor(uu, og[:, k, :, :], col("bs", l)[:, k:k + 1], uu, ADD, MUL)
                ins.then_inc(gating_read.sem, gating_read.next((L, "gm")))
                dve.wait_ge(exp_small.sem, exp_small.at((L, "end")))
                tt(S_(490, 6), S_(136, 6), dt[:, 0:6], MUL)
                dve.wait_ge(act_read.sem, act_read.at((L, "xs", 0)))
                v.tensor_tensor(x_dec.rearrange("p (h d) -> p h d", h=SSD_H), xs[:, 0, :].rearrange("p (h d) -> p h d", h=SSD_H), S_(490, 6).unsqueeze(2).to_broadcast([P, SSD_H, DH]), MUL).then_inc(state_in.sem, state_in.next(L))
                for c in range(NB):
                    dve.wait_ge(act_read.sem, act_read.at((L, "xs", c)))
                    tt(y_b[:, c, :].rearrange("p (h d) -> p h d", h=SSD_H), xs[:, c, :].rearrange("p (h d) -> p h d", h=SSD_H),
                       d_skip[:, l, :].unsqueeze(2).to_broadcast([P, SSD_H, DH]), MUL)
                for n in range(2):
                    for b in range(NB):
                        dve.wait_ge(act_read.sem, act_read.at((L, "qb", n, b)))
                rot = split_t[:, 0, 0:384].rearrange("p (b h d) -> p b h d", b=NB, h=M_H)
                for b in range(NB):
                    qr = qtok[:, b, :].rearrange("p (h d) -> p h d", h=M_H)[:, :, DH:M_QK]
                    for r in range(2):
                        tt(rot[:, b, :, 16 * r:16 * r + 16], qr[:, :, 16 - 16 * r:32 - 16 * r],
                           sin_m[:, b, 16 * r:16 * r + 16].unsqueeze(1).to_broadcast([P, M_H, 16]), MUL)
                    tt(qr, qr, cos_m[:, b, :].unsqueeze(1).to_broadcast([P, M_H, M_ROPE]), MUL)
                    ins = v.tensor_tensor(qr, qr, rot[:, b, :, :], ADD)
                    if b == 1:
                        ins.then_inc(roped.sem, roped.next((L, "q")))
                dve.wait_ge(product_done.sem, product_done.at((L, "cb", 1)))
                for c in range(NB):
                    for g in range(2):
                        dve.wait_ge(exp_seg.sem, exp_seg.at((L, c, g)))
                        for h in range(3):
                            i = c * SSD_H + 3 * g + h
                            ins = v.scalar_tensor_tensor(decay[:, i, :], decay[:, i, :], dt[:, i:i + 1],
                                                         bank[CB_BANK][:, g * S + c * P:g * S + (c + 1) * P], MUL, MUL)
                        ins.then_inc(decay_ready.sem, decay_ready.next((L, c, g)))
                for n in range(2):
                    for b in range(NB):
                        dve.wait_ge(act_read.sem, act_read.at((L, "kv", n, b)))
                for b in range(NB):
                    kk = ktok[:, b, :].rearrange("p (h d) -> p h d", h=M_H)
                    v.tensor_copy(kk[:, :, 0:DH], kvtok[:, b, :].rearrange("p (h d) -> p h d", h=M_H)[:, :, 0:DH])
                    ins = v.tensor_copy(kk[:, :, DH:M_QK], kr3[:, b, :].unsqueeze(1).to_broadcast([P, M_H, M_ROPE]))
                    if b == 1:
                        ins.then_inc(roped.sem, roped.next((L, "k")))

                yf = flat2(y_b)
                t3 = split_t[:, 0, 0:SSD_W]
                for c in range(NB):
                    dve.wait_ge(product_done.sem, product_done.at((L, "yd", c)))
                    v.tensor_tensor(y_b[:, c, :], y_b[:, c, :], bank[STATE_BANK[c]][:, 0:SSD_W], ADD).then_inc(state_read.sem, state_read.next((L, "yd", c)))
                dve.wait_ge(state_read.sem, state_read.made)
                dve.wait_ge(product_done.sem, product_done.at((L, "yo", 1)))
                for g in range(2):
                    v.tensor_tensor(t3[:, 192 * g:192 * g + 192].rearrange("p (h d) -> p h d", h=3),
                                    bank[1][:, 192 * g:192 * g + 192].rearrange("p (h d) -> p h d", h=3),
                                    S_(142 + 3 * g, 3).unsqueeze(2).to_broadcast([P, 3, DH]), MUL).then_inc(state_read.sem, state_read.next((L, "yo", g)))
                dve.wait_ge(state_read.sem, state_read.made)
                tt(y_b[:, 1, :], y_b[:, 1, :], t3, ADD)
                for b in range(NB):
                    dve.wait_ge(act_read.sem, act_read.at((L, "z", b)))
                v.tensor_tensor(yf, yf, flat2(zg), MUL).then_inc(z_gated.sem, z_gated.next(L))

                def split_lo(key, dst, src, hi, flow, gain=None):
                    dve.wait_ge(split_hi.sem, split_hi.at(key))
                    if gain is None:
                        v.tensor_tensor(dst, src, hi.bitcast(F32), SUB).then_inc(flow.sem, flow.next(key))
                    else:
                        for m, g in enumerate(gain):
                            ins = v.scalar_tensor_tensor(dst[:, m * S:(m + 1) * S], src[:, m * S:(m + 1) * S], g,
                                                         hi[:, m * S:(m + 1) * S].bitcast(F32), MUL, SUB)
                        ins.then_inc(flow.sem, flow.next(key))

                split_lo((L, "at"), flat2(r_lo[:, 0:2, :]), bank[GATING_BANK][:, :], flat2(r_hi[:, 0:2, :]), r_ready)
                for what, h in attention_order(M_H, (NORMAL_LAG, LONG[1]), "tsv"):
                    if what == "s":
                        dve.wait_ge(product_done.sem, product_done.at((L, "s", h)))
                        o = bank[4 + h % 2]
                        for b, (c0, c1) in enumerate(((0, P), (P, P + S))):
                            if h >= 2:
                                dve.wait_ge(exp_done.sem, exp_done.at((L, h - 2, b)))
                            if h >= PROBS:
                                dve.wait_ge(exp_done.sem, exp_done.at((L, h - PROBS, b)))
                            ins = v.tensor_tensor_reduce(out=masked[:, h % 2, c0:c1], in0=o[:, c0:c1], in1=K("causal")[:, c0:c1] if b == 0 else K("causal")[:, P:P + S],
                                                      scale=-1.0, scalar=BIG, op0=ADD, op1=ALU.min, accum_out=S_(16 + 4 * (h % PROBS) + b, 1))
                            if b == 1:
                                ins.then_inc(dve_read.sem, dve_read.next((L, "s", h)))
                            else:
                                ins.then_inc(row_max.sem, row_max.next((L, h)))
                    elif what == "t":
                        for b in range(NB):
                            dve.wait_ge(exp_done.sem, exp_done.at((L, h, b)))
                        r = normalise(h, range(NB))
                        for b, (c0, c1) in enumerate(((0, P), (P, P + S))):
                            p_ = prob[:, h % PROBS, c0:c1]
                            ins = v.tensor_scalar(p_, p_, r[:, b:b + 1], None, MUL)
                        ins.then_inc(probs_normal.sem, probs_normal.next((L, h)))
                    elif h == 3:
                        split_lo((L, "co", 0), flat2(r_lo[:, 5:7, :]), bank[HEAD_BANK[0]][:, :], flat2(r_hi[:, 5:7, :]), out_read)
                    elif h == 5:
                        split_lo((L, "co", 1), r_lo[:, 7, :], bank[HEAD_BANK[1]][:, 0:S], r_hi[:, 7, :], out_read)
                    if (what, h) == ("s", 1):
                        dve.wait_ge(square_sum.sem, square_sum.at((L, "y", 3)))
                        ts(S_(496, 4), S_(496, 4), 1.0 / 192, 1e-6, MUL, ADD)
                        rsqrt(S_(500, 4), S_(496, 4), S_(504, 4))
                        y4 = yf.rearrange("p (g n) -> p g n", g=4)
                        v.tensor_tensor(y4, y4, S_(500, 4).unsqueeze(2).to_broadcast([P, 4, 192]), MUL).then_inc(mixer_out.sem, mixer_out.next((L, "b")))
                    elif (what, h) == ("v", 1):
                        gains = [col("ssd", l)[:, k:k + 1] for k in range(3)]
                        split_lo((L, "bt", 0), flat2(r_lo[:, 2:4, :]), bank[STATE_BANK[0]][:, :], flat2(r_hi[:, 2:4, :]), r_ready, gains[0:2])
                        split_lo((L, "bt", 1), r_lo[:, 4, :], bank[STATE_BANK[1]][:, 0:S], r_hi[:, 4, :], r_ready, gains[2:3])
                for n in range(2):
                    for b in range(NB):
                        add_rows((L, "wo", n, b), n, b, bank[2 * n + b])
                    split_hidden((L, "mlp"), (L, "mlp"), 4, col("mlp", l), None, js=range(2 * n, 2 * n + 2))
                for b in range(NB):
                    link(rms(L, "mlp", b))
                    tt(S_(10 + b, 1), S_(8 + b, 1), S_(8 + b, 1), MUL)
                for e in range(8):
                    for u in range(2):
                        dve.wait_ge(square_hi.sem, square_hi.at((L, "up", e, u)))
                        relu, f = masked[:, u, :], split_t[:, u, :]
                        tt(f, relu, relu, MUL)
                        t0 = 4 * (e % 2) + 2 * u
                        v.tensor_tensor(flat2(r_lo[:, t0:t0 + 2, :]), f, flat2(r_hi[:, t0:t0 + 2, :]).bitcast(F32), SUB).then_inc(r_ready.sem, r_ready.next((L, "up", e, u)))
                        dve.wait_ge(r_ready.sem, r_ready.made)
                for n in range(2):
                    for b in range(NB):
                        add_rows((L, "dn", n, b), n, b, bank[4 + 2 * n + b], factor=S_(10 + b, 1))
                        if n == 1 and l == 1:
                            link(rms("end", "end", b))
                            if b == 0:
                                dve.wait_ge(gf_loaded, 16)
                            v.scalar_tensor_tensor(z[:, b, :], x[:, b, :], S_(8 + b, 1), gf, MUL, MUL).then_inc(row_out.sem, row_out.next(b))

        for steps in every:
            assert steps.made == len(steps.order)


_INS = ["x", "mem", "ln_in_g", "ln_in_b", "w_mem_kv", "w_in_a", "w_in_b", "q_norm_g", "k_norm_g", "w_in_c", "w_out", "ln_g",
        "ln_b", "norm_mix_g_2", "w_in_2", "gmlp_v_norm_g_2", "gmlp_w_s_2", "gmlp_b_s_2", "ssd_conv_w_2", "ssd_conv_b_2",
        "ssd_dt_bias_2", "ssd_a_log_2", "ssd_d_2", "ssd_norm_g_2", "mla_q_norm_g_2", "mla_w_qb_2", "mla_kv_norm_g_2",
        "mla_w_kvb_2", "w_out_2", "norm_mlp_g_2", "mlp_w1_2", "mlp_w2_2", "final_norm_g_2"]


def kernel(**inputs):
    import concourse.bacc as bacc
    from concourse.bass_utils import run_bass_kernel_spmd

    nc = bacc.Bacc("TRN2", target_bir_lowering=False, num_devices=1)
    arrays, aps = {}, {}
    for name in _INS + ["const"]:
        a = constants()[0] if name == "const" else np.ascontiguousarray(inputs[name])
        arrays[f"in_{name}"] = a
        aps[name] = nc.dram_tensor(f"in_{name}", a.shape, mybir.dt.from_np(a.dtype), kind="ExternalInput").ap()
    out = nc.dram_tensor("out", (1, S, D), F32, kind="ExternalOutput").ap()
    build(nc, aps, out)
    return run_bass_kernel_spmd(nc, [arrays], core_ids=[0]).results[0]["out"]
```
